# Optimizing a Trainium2 kernel written in Bass

```python
import math
import jax, jax.numpy as jnp
from jax import lax
import numpy as np

D_MODEL = 1024
BATCH = 1
SEQ = 512
DEPTH = 1

D_MIX = D_MODEL
D_RWKV = D_MIX // 2
RWKV_HEAD = 64
N_RWKV_HEADS = D_RWKV // RWKV_HEAD
D_ATT = D_MIX - D_RWKV
ATT_HEAD = 64
N_ATT_HEADS = D_ATT // ATT_HEAD
RANK_DECAY = 64
RANK_A = 64
RANK_GATE = 128
RWKV_GN_EPS = 64e-5
Q_LORA = D_MODEL // 4
KV_LORA = D_MODEL // 8
IDX_HEADS = 8
IDX_DIM = 64
TOPK_MAX = 256
Q_BLOCK = 128
N_EXPERTS = 32
TOP_K_EXPERTS = 4
D_FF = D_MODEL
SWIGLU_LIMIT = 7.0
SWIGLU_ALPHA = 1.702
MOE_BLOCK = 128
NEG_INF = -1e30

SPLIT_SHIFT = (D_RWKV, D_RWKV, D_RWKV, RANK_DECAY, RANK_A, RANK_GATE)
SPLIT_ATT = (Q_LORA, KV_LORA, IDX_DIM, IDX_HEADS)
N_SHIFT = sum(SPLIT_SHIFT)
N_IN = N_SHIFT + sum(SPLIT_ATT)

kernel_name = "hymba_rwkv7_dsa_moe_deepnorm_adaln"

def _split(z, sizes):
    idx = list(np.cumsum(sizes)[:-1])
    return jnp.split(z, idx, axis=-1)

def _layernorm(x, g, b, eps=1e-5):
    xf = x.astype(jnp.float32)
    mu = jnp.mean(xf, axis=-1, keepdims=True)
    var = jnp.mean(jnp.square(xf - mu), axis=-1, keepdims=True)
    return ((xf - mu) * lax.rsqrt(var + eps)).astype(x.dtype) * g + b

def _rmsnorm(x, g, eps=1e-6):
    xf = x.astype(jnp.float32)
    ms = jnp.mean(jnp.square(xf), axis=-1, keepdims=True)
    return (xf * lax.rsqrt(ms + eps)).astype(x.dtype) * g

def _alibi_slopes(n_heads):
    return jnp.asarray([2.0 ** (-8.0 * (h + 1) / n_heads) for h in range(n_heads)], jnp.float32)

def _rwkv7_scan(r, w, k, v, a, b):
    B, _, H, N = r.shape

    def step(state, inp):
        r_t, w_t, k_t, v_t, a_t, b_t = inp
        sa = jnp.einsum('bhvk,bhk->bhv', state, a_t)
        state = (state * w_t[:, :, None, :] + sa[..., None] * b_t[:, :, None, :]
                 + v_t[..., None] * k_t[:, :, None, :])
        return state, jnp.einsum('bhvk,bhk->bhv', state, r_t)

    xs = tuple(jnp.moveaxis(z, 1, 0) for z in (r, w, k, v, a, b))
    s0 = jnp.zeros((B, H, N, N), jnp.float32)
    _, o = lax.scan(step, s0, xs)
    return jnp.moveaxis(o, 0, 1)

def _rwkv7_group(pr, pk, pv, pw, pa, pg, w0, w2, a0, a2, g2, k_k, k_a, r_k, ln_w, ln_b):
    B, S, _ = pr.shape
    H, N = N_RWKV_HEADS, RWKV_HEAD
    f32 = jnp.float32
    w_log = -jax.nn.softplus(-(w0 + jnp.tanh(pw) @ w2).astype(f32)) - 0.5
    decay = jnp.exp(-jnp.exp(w_log))
    a = jax.nn.sigmoid((a0 + pa @ a2).astype(f32))
    g = jax.nn.sigmoid(pg) @ g2
    kk = (pk * k_k).astype(f32).reshape(B, S, H, N)
    kk = kk / jnp.maximum(jnp.sqrt(jnp.sum(kk * kk, axis=-1, keepdims=True)), 1e-12)
    k = (pk.astype(f32) * (1.0 + (a - 1.0) * k_a)).reshape(B, S, H, N)
    r = pr.astype(f32).reshape(B, S, H, N)
    v = pv.astype(f32).reshape(B, S, H, N)
    a_h = a.reshape(B, S, H, N)
    o = _rwkv7_scan(r, decay.reshape(B, S, H, N), k, v, -kk, kk * a_h)
    mu = jnp.mean(o, axis=-1, keepdims=True)
    var = jnp.mean(jnp.square(o - mu), axis=-1, keepdims=True)
    o = ((o - mu) * lax.rsqrt(var + RWKV_GN_EPS)).reshape(B, S, D_RWKV) * ln_w + ln_b
    bonus = jnp.sum(r * k * r_k, axis=-1, keepdims=True) * v
    o = (o + bonus.reshape(B, S, D_RWKV)) * g
    return o.astype(pr.dtype)

def _dsa_sparse_attention(q_abs, iq, iw, k_idx, c_lat, topk):
    B, S, H, C = q_abs.shape
    nb = S // Q_BLOCK
    f32 = jnp.float32
    slopes = _alibi_slopes(H)
    spos = jnp.arange(S, dtype=jnp.int32)
    tpos = spos.reshape(nb, Q_BLOCK)
    k_idx_f = k_idx.astype(f32)
    c_f = c_lat.astype(f32)
    idx_scale = IDX_DIM ** -0.5
    att_scale = ATT_HEAD ** -0.5
    gather = jax.vmap(lambda cb, ib: cb[ib])

    def blk(z):
        return jnp.moveaxis(z.reshape((B, nb, Q_BLOCK) + z.shape[2:]), 1, 0)

    def one_block(args):
        qa, iqb, iwb, tp = args
        s_idx = jnp.einsum('bqhd,bsd->bqhs', iqb.astype(f32), k_idx_f) * idx_scale
        score = jnp.einsum('bqh,bqhs->bqs', iwb.astype(f32), jax.nn.relu(s_idx))
        causal = spos[None, :] <= tp[:, None]
        score = jnp.where(causal[None], score, NEG_INF)
        _, sel = lax.top_k(score, topk)
        c_sel = gather(c_f, sel)
        logits = jnp.einsum('bqhc,bqkc->bqhk', qa.astype(f32), c_sel) * att_scale
        dist = tp[None, :, None] - sel
        logits = logits - slopes[None, None, :, None] * dist.astype(f32)[:, :, None, :]
        logits = jnp.where((dist >= 0)[:, :, None, :], logits, NEG_INF)
        p = jax.nn.softmax(logits, axis=-1)
        return jnp.einsum('bqhk,bqkc->bqhc', p, c_sel)

    o_lat = lax.map(one_block, (blk(q_abs), blk(iq), blk(iw), tpos))
    return jnp.moveaxis(o_lat, 0, 1).reshape(B, S, H, C).astype(q_abs.dtype)

def _dsa_group(pq, pkv, pik, piw, q_norm, w_q_up, kv_norm, w_uk, w_uv, idx_w_q, idx_ln_g, idx_ln_b):
    B, S, _ = pq.shape
    topk = min(TOPK_MAX, S // 4)
    q_lat = _rmsnorm(pq, q_norm)
    q = (q_lat @ w_q_up).reshape(B, S, N_ATT_HEADS, ATT_HEAD)
    q_abs = jnp.einsum('bshd,hdc->bshc', q, w_uk)
    c_lat = _rmsnorm(pkv, kv_norm)
    iq = (q_lat @ idx_w_q).reshape(B, S, IDX_HEADS, IDX_DIM)
    ik = _layernorm(pik, idx_ln_g, idx_ln_b)
    iw = piw * (IDX_HEADS ** -0.5)
    o_lat = _dsa_sparse_attention(q_abs, iq, iw, ik, c_lat, topk)
    o = jnp.einsum('bshc,hcd->bshd', o_lat, w_uv)
    return o.reshape(B, S, D_ATT)

def _moe(u, w_router, b_router, w_gu, b_gu, w_dn, b_dn):
    B, S, D = u.shape
    T = B * S
    TK = T * TOP_K_EXPERTS
    xt = u.reshape(T, D)
    logits = (xt @ w_router + b_router).astype(jnp.float32)
    top_val, top_idx = lax.top_k(logits, TOP_K_EXPERTS)
    gates = jax.nn.softmax(top_val, axis=-1)
    flat_e = top_idx.reshape(-1)
    flat_tok = jnp.repeat(jnp.arange(T, dtype=jnp.int32), TOP_K_EXPERTS)
    flat_g = gates.reshape(-1)
    order = jnp.argsort(flat_e)
    e_sorted = flat_e[order]
    counts = jnp.bincount(flat_e, length=N_EXPERTS)
    starts = jnp.cumsum(counts) - counts
    padded = (counts + MOE_BLOCK - 1) // MOE_BLOCK * MOE_BLOCK
    pad_ends = jnp.cumsum(padded)
    pad_starts = pad_ends - padded
    dest = pad_starts[e_sorted] + (jnp.arange(TK, dtype=jnp.int32) - starts[e_sorted])
    n_blocks = -(-TK // MOE_BLOCK) + N_EXPERTS
    n_rows = n_blocks * MOE_BLOCK
    row_tok = jnp.zeros((n_rows,), jnp.int32).at[dest].set(flat_tok[order])
    row_gate = jnp.zeros((n_rows,), jnp.float32).at[dest].set(flat_g[order])
    block_e = jnp.minimum(jnp.searchsorted(pad_ends, jnp.arange(n_blocks) * MOE_BLOCK, side='right'),
                          N_EXPERTS - 1).astype(jnp.int32)

    def expert_block(args):
        e, tok = args
        xb = xt[tok]
        gu = xb @ w_gu[e] + b_gu[e]
        gate = jnp.minimum(gu[:, 0::2], SWIGLU_LIMIT)
        up = jnp.clip(gu[:, 1::2], -SWIGLU_LIMIT, SWIGLU_LIMIT)
        h = (up + 1.0) * (gate * jax.nn.sigmoid(gate * SWIGLU_ALPHA))
        return h @ w_dn[e] + b_dn[e]

    out = lax.map(expert_block, (block_e, row_tok.reshape(n_blocks, MOE_BLOCK)))
    out = out.reshape(n_rows, D).astype(jnp.float32) * row_gate[:, None]
    y = jnp.zeros((T, D), jnp.float32).at[row_tok].add(out)
    return y.reshape(B, S, D).astype(u.dtype)

def setup_inputs(seed: int = 0) -> dict:
    key = jax.random.key(seed)
    ks = iter(jax.random.split(key, 40))
    L = DEPTH
    beta = (8.0 * DEPTH) ** -0.25

    def nrm(shape, scale):
        return jax.random.normal(next(ks), shape, jnp.float32) * scale

    d = D_MODEL
    inp = {}
    inp['x'] = nrm((BATCH, SEQ, d), 1.0)
    inp['c'] = nrm((BATCH, d), 1.0)
    inp['w_ada'] = nrm((L, d, 6 * d), 0.5 * d ** -0.5)
    inp['b_ada'] = nrm((L, 6 * d), 0.01)
    inp['w_in'] = nrm((L, d, N_IN), d ** -0.5)
    inp['shift_mu'] = jax.random.uniform(next(ks), (L, N_SHIFT), jnp.float32)
    inp['rwkv_w0'] = jax.random.uniform(next(ks), (L, D_RWKV), jnp.float32, -6.0, -1.0)
    inp['rwkv_w2'] = nrm((L, RANK_DECAY, D_RWKV), 0.5 * RANK_DECAY ** -0.5)
    inp['rwkv_a0'] = nrm((L, D_RWKV), 0.1)
    inp['rwkv_a2'] = nrm((L, RANK_A, D_RWKV), RANK_A ** -0.5)
    inp['rwkv_g2'] = nrm((L, RANK_GATE, D_RWKV), RANK_GATE ** -0.5)
    inp['rwkv_k_k'] = 0.85 + nrm((L, D_RWKV), 0.05)
    inp['rwkv_k_a'] = 1.0 + nrm((L, D_RWKV), 0.05)
    inp['rwkv_r_k'] = nrm((L, N_RWKV_HEADS, RWKV_HEAD), 0.1)
    inp['rwkv_ln_w'] = 1.0 + nrm((L, D_RWKV), 0.05)
    inp['rwkv_ln_b'] = nrm((L, D_RWKV), 0.01)
    inp['mla_q_norm'] = 1.0 + nrm((L, Q_LORA), 0.05)
    inp['mla_w_q_up'] = nrm((L, Q_LORA, N_ATT_HEADS * ATT_HEAD), Q_LORA ** -0.5)
    inp['mla_kv_norm'] = 1.0 + nrm((L, KV_LORA), 0.05)
    inp['mla_w_uk'] = nrm((L, N_ATT_HEADS, ATT_HEAD, KV_LORA), ATT_HEAD ** -0.5)
    inp['mla_w_uv'] = nrm((L, N_ATT_HEADS, KV_LORA, ATT_HEAD), KV_LORA ** -0.5)
    inp['idx_w_q'] = nrm((L, Q_LORA, IDX_HEADS * IDX_DIM), Q_LORA ** -0.5)
    inp['idx_ln_g'] = 1.0 + nrm((L, IDX_DIM), 0.05)
    inp['idx_ln_b'] = nrm((L, IDX_DIM), 0.01)
    inp['w_out'] = nrm((L, D_MIX, d), beta * D_MIX ** -0.5)
    inp['ln1_g'] = 1.0 + nrm((L, d), 0.05)
    inp['ln1_b'] = nrm((L, d), 0.01)
    inp['w_router'] = nrm((L, d, N_EXPERTS), d ** -0.5)
    inp['b_router'] = nrm((L, N_EXPERTS), 0.01)
    inp['w_gu'] = nrm((L, N_EXPERTS, d, 2 * D_FF), d ** -0.5)
    inp['b_gu'] = nrm((L, N_EXPERTS, 2 * D_FF), 0.01)
    inp['w_dn'] = nrm((L, N_EXPERTS, D_FF, d), beta * D_FF ** -0.5)
    inp['b_dn'] = nrm((L, N_EXPERTS, d), 0.01)
    inp['ln2_g'] = 1.0 + nrm((L, d), 0.05)
    inp['ln2_b'] = nrm((L, d), 0.01)
    return inp

def reference(x, c, w_ada, b_ada, w_in, shift_mu, rwkv_w0, rwkv_w2, rwkv_a0, rwkv_a2, rwkv_g2,
              rwkv_k_k, rwkv_k_a, rwkv_r_k, rwkv_ln_w, rwkv_ln_b, mla_q_norm, mla_w_q_up,
              mla_kv_norm, mla_w_uk, mla_w_uv, idx_w_q, idx_ln_g, idx_ln_b, w_out, ln1_g, ln1_b,
              w_router, b_router, w_gu, b_gu, w_dn, b_dn, ln2_g, ln2_b):
    alpha = (2.0 * DEPTH) ** 0.25
    c_act = jax.nn.silu(c)
    for l in range(DEPTH):
        mod = c_act @ w_ada[l] + b_ada[l]
        sh1, sc1, gt1, sh2, sc2, gt2 = [m[:, None, :] for m in jnp.split(mod, 6, axis=-1)]

        u = x * (1.0 + sc1) + sh1
        p = u @ w_in[l]
        p_sh = p[..., :N_SHIFT]
        p_prev = jnp.pad(p_sh[:, :-1], ((0, 0), (1, 0), (0, 0)))
        p_sh = p_sh + shift_mu[l] * (p_prev - p_sh)
        pr, pk, pv, pw, pa, pg = _split(p_sh, SPLIT_SHIFT)
        pq, pkv, pik, piw = _split(p[..., N_SHIFT:], SPLIT_ATT)
        o_rwkv = _rwkv7_group(pr, pk, pv, pw, pa, pg, rwkv_w0[l], rwkv_w2[l], rwkv_a0[l], rwkv_a2[l],
                              rwkv_g2[l], rwkv_k_k[l], rwkv_k_a[l], rwkv_r_k[l], rwkv_ln_w[l], rwkv_ln_b[l])
        o_dsa = _dsa_group(pq, pkv, pik, piw, mla_q_norm[l], mla_w_q_up[l], mla_kv_norm[l], mla_w_uk[l],
                           mla_w_uv[l], idx_w_q[l], idx_ln_g[l], idx_ln_b[l])
        mix = jnp.concatenate([o_rwkv, o_dsa], axis=-1) @ w_out[l]
        x = _layernorm(alpha * x + (1.0 + gt1) * mix, ln1_g[l], ln1_b[l])

        u = x * (1.0 + sc2) + sh2
        ffn = _moe(u, w_router[l], b_router[l], w_gu[l], b_gu[l], w_dn[l], b_dn[l])
        x = _layernorm(alpha * x + (1.0 + gt2) * ffn, ln2_g[l], ln2_b[l])
    return x


_drawn_inputs = setup_inputs


def setup_inputs(seed=0):
    import zlib

    import numpy as np

    out = dict(_drawn_inputs(seed))
    spreads = {}
    factors = {'rwkv_w2': 3.06,
     'rwkv_a0': 3.171,
     'rwkv_ln_w': 2.699,
     'rwkv_ln_b': 7.681,
     'mla_kv_norm': 2.811,
     'idx_ln_b': 4.033,
     'ln1_b': 2.948,
     'b_router': 3.396,
     'b_gu': 8.0,
     'b_dn': 8.0,
     'ln2_b': 5.709}
    for name, (base, spread) in spreads.items():
        noise = np.random.default_rng([zlib.crc32(name.encode()), seed]).standard_normal(out[name].shape)
        drawn = base * np.exp(spread * noise) if base else spread * noise
        out[name] = __import__('jax').numpy.asarray(drawn.astype(out[name].dtype))
    for name, factor in factors.items():
        out[name] = (out[name] * factor).astype(out[name].dtype)
    return out
```

```python
from contextlib import ExitStack

import numpy as np

import concourse.bass as bass
from concourse import mybir

F32 = mybir.dt.float32
I32 = mybir.dt.int32
BF16 = mybir.dt.bfloat16
ALU = mybir.AluOpType
ACT = mybir.ActivationFunctionType
AX = mybir.AxisListType

P = 128
D = 1024
S = 512
NT = S // P
KC = D // P
C = 64
NCH = S // C
HEADS = 8
D_GROUP = HEADS * C
NPAIR = D_GROUP // P
Q_LORA, KV_LORA, IDX_DIM = 256, 128, 64
N_SHIFT = 3 * D_GROUP + 64 + 64 + 128
N_IN = N_SHIFT + Q_LORA + KV_LORA + IDX_DIM + HEADS
SHIFT_TILES = N_SHIFT // P
COL_TILES = -(-N_IN // P)
TOPK = min(256, S // 4)
N_EXP = 32
TOP_E = 4
FF = 1024
EXTRA = (S * TOP_E // (S - P + 1)) * (S // P - 1)
BLOCKS = N_EXP + EXTRA
NEG = -1e30
TAKEN = -3e38
DECAY = float(np.exp(-0.5))
LEVELS = (4, 8, 16, 32, 64)
GN_EPS = 64e-5
LIMIT, SWIGLU_ALPHA = 7.0, 1.702
ALPHA = 2.0 ** 0.25
SLOPES = [2.0 ** (-8.0 * (h + 1) / HEADS) for h in range(HEADS)]

VEC = {}
_at = 0
for _n, _k in (("c", 8), ("shift_mu", 14), ("rwkv_w0", 4), ("rwkv_a0", 4), ("rwkv_k_k", 4),
               ("rwkv_k_a", 4), ("rwkv_r_k", 4), ("mla_q_norm", 2), ("mla_kv_norm", 1),
               ("idx_ln_g", 1), ("idx_ln_b", 1)):
    VEC[_n] = (_at, _k)
    _at += _k
N_VEC = _at

CONST = {}


def _constants():
    p = np.arange(P)[:, None]
    j = np.arange(P)[None, :]
    half = p // C == j // C
    s512 = np.arange(S)[None, :]
    parts = [("ident", p == j), ("strict", half & (p < j)), ("incl", half & (p <= j)),
             ("low2", (p == j + 1) & (j % 2 == 0)), ("up2", (j == p + 1) & (p % 2 == 0))]
    for n in LEVELS:
        parts.append((f"lev{n}", (p // n == j // n) & (p // (n // 2) != j // (n // 2)) & (p < j)))
    parts += [("half", half), ("ones", np.ones((P, P))), ("before", p < j),
              ("slots", np.broadcast_to(j, (P, P))),
              ("causal", np.where(j <= p, 0.0, NEG)),
              ("dist", np.broadcast_to(s512, (P, S)) - p),
              ("keep", np.broadcast_to(s512 % C != 0, (P, S))),
              ("heads", p // C == np.arange(2)[None, :]),
              ("blocks", np.broadcast_to(np.arange(BLOCKS)[None, :], (P, BLOCKS))),
             ("token", p + 0 * np.arange(NT)[None, :] + P * np.arange(NT)[None, :]),
             ("expert", np.broadcast_to(np.arange(N_EXP)[None, :], (P, N_EXP))),
             ("eps", np.broadcast_to(np.array([[1e-6, 1e-5, GN_EPS]]), (P, 3)))]
    at = 0
    for name, a in parts:
        CONST[name] = (at, a.shape[1])
        at += a.shape[1]
    return np.concatenate([np.asarray(a, np.float32) for _, a in parts], 1)


CONST_ARRAY = _constants()
N_CONST = CONST_ARRAY.shape[1]


class Shared:
    pass


def psum_banks(nc, e, tag):
    return [e(nc.psum_tensor(f"{tag}_bank{i}", [P, 512], F32)) for i in range(8)]


def project(nc, io, sh):
    RING = 4
    HALF = 1024
    W_GROUPS = [(0, 512), (512, 512), (1024, 512), (1536, 512), (2048, N_IN - 2048)]
    WBUF = 3
    with ExitStack() as ctx:
        e = ctx.enter_context
        uT = e(nc.sbuf_tensor("uT", [P, KC, S], F32))
        win = e(nc.sbuf_tensor("w_in_sb", [P, WBUF, KC, 512], F32))
        ada = e(nc.sbuf_tensor("w_ada_sb", [P, RING, HALF], F32))
        rows = e(nc.sbuf_tensor("vec_rows", [N_VEC, P], F32))
        c_act = e(nc.sbuf_tensor("c_act", [P, KC], F32))
        sig_c = e(nc.sbuf_tensor("sig_c", [P, KC], F32))
        mod1 = e(nc.sbuf_tensor("mod1", [P, 2 * KC], F32))
        praw = e(nc.sbuf_tensor("p_raw", [P, 2, S + 1], F32))
        pdif = e(nc.sbuf_tensor("p_dif", [P, 2, S], F32))
        bank = psum_banks(nc, e, "project")
        ps_vec, ps_mod = bank[0], bank[1]
        ps_x, ps_p = bank[2:4], bank[4:8]
        acc0 = sh.pT[:, 0:4, :].rearrange("p a b -> p (a b)")
        accs = [acc0, sh.modb[:, 0:2048], sh.modb[:, 2048:4096]]
        cst, cols = sh.cst, sh.cols

        sem = sh.sem
        consts_in, vec_in, x_in, bias_in = sem("consts_in"), sem("vec_in"), sem("x_in"), sem("bias_in")
        ada_in = [sem(f"ada_in{i}") for i in range(RING)]
        win_in = [sem(f"win_in{i}") for i in range(WBUF)]
        acc_zero, ada_used, acc_done = sem("acc_zero"), sem("ada_used"), sem("acc_done")
        vec_turned, cols_ready, sig_ready, c_ready = sem("vec_turned"), sem("cols_ready"), sem("sig_ready"), sem("c_ready")
        x_turned, uT_ready, mod1_summed, mod1_ready = sem("x_turned"), sem("uT_ready"), sem("mod1_summed"), sem("mod1_ready")
        p_done, p_copied, p_shifted, p_diff = sem("p_done"), sem("p_copied"), sem("p_shifted"), sem("p_diff")
        mod_summed, mod_copied, edge_zero = sem("mod_summed"), sem("mod_copied"), sem("edge_zero")

        w_ada = io["w_ada"][0].rearrange("(c p) n -> p c n", p=P)
        w_in = io["w_in"][0].rearrange("(c p) n -> p c n", p=P)
        N_G = KC * 2
        block = e(nc.Block())

        @block.sync
        def _(sp):
            sp.dma_start(cst[:, :], io["consts"]).then_inc(consts_in, 16)
            for name, (r, k) in VEC.items():
                src = io[name]
                if name == "rwkv_r_k":
                    sp.dma_start(rows[r:r + k, :], src.rearrange("o (r a) d -> (o r) (a d)", a=2)).then_inc(vec_in, 16)
                    continue
                if k * P > src.shape[1]:
                    sp.dma_start(rows[r:r + 1, 0:C], src).then_inc(vec_in, 16)
                    sp.dma_start(rows[r:r + 1, C:P], src).then_inc(vec_in, 16)
                    continue
                sp.dma_start(rows[r:r + k, :], src.rearrange("o (r d) -> (o r) d", d=P)).then_inc(vec_in, 16)
            sp.wait_ge(acc_zero, 1)
            sp.dma_start(acc0[0:1, :], io["b_ada"][:, 0:2048]).then_inc(bias_in, 16)

            def ada_piece(n):
                g, k = divmod(n, N_G)
                if n >= RING:
                    sp.wait_ge(ada_used, n - RING + 1)
                sp.dma_start(ada[:, n % RING, :],
                             w_ada[:, k // 2, g * 2048 + (k % 2) * HALF:g * 2048 + (k % 2 + 1) * HALF]).then_inc(ada_in[n % RING], 16)

            def win_group(g):
                at, n = W_GROUPS[g]
                if g >= WBUF:
                    sp.wait_ge(p_done, 4 * (g - WBUF + 1))
                sp.dma_start(win[:, g % WBUF, :, 0:n], w_in[:, :, at:at + n]).then_inc(win_in[g % WBUF], 16)

            for n in range(N_G):
                ada_piece(n)
                if n % 4 == 3:
                    i = n // 4
                    sp.dma_start(sh.x_tm[:, i, :], io["x"][0, i * P:(i + 1) * P, :]).then_inc(x_in, 16)
            for g in range(WBUF):
                win_group(g)
            sp.wait_ge(acc_zero, 3)
            for g in (1, 2):
                sp.dma_start(accs[g][0:1, :], io["b_ada"][:, g * 2048:(g + 1) * 2048]).then_inc(bias_in, 16)
            for n in range(N_G, 2 * N_G):
                ada_piece(n)
            win_group(3)
            for n in range(2 * N_G, 3 * N_G):
                ada_piece(n)
            win_group(4)

        @block.tensor
        def _(pe):
            ident = sh.const("ident")
            pe.wait_ge(consts_in, 16)
            pe.wait_ge(vec_in, 16 * (len(VEC) + 2))
            pe.transpose(ps_vec[:, 0:N_VEC], rows[:, :], ident[0:N_VEC, 0:N_VEC]).then_inc(vec_turned, 1)
            for c in range(KC):
                if c == 0:
                    pe.wait_ge(x_in, 16 * NT)
                if c >= 2:
                    pe.wait_ge(uT_ready, c - 1)
                for i in range(NT):
                    last = pe.transpose(ps_x[c % 2][:, i * P:(i + 1) * P], sh.x_tm[:, i, c * P:(c + 1) * P], ident)
                last.then_inc(x_turned, 1)
                if c == 1:
                    pe.wait_ge(acc_done, 1)
                    for k in range(2 * KC):
                        last = pe.matmul(ps_mod[:, k:k + 1], acc0[:, k * P:(k + 1) * P], sh.const("ones")[:, 0:1], start=True, stop=True)
                    last.then_inc(mod1_summed, 1)
            pe.wait_ge(uT_ready, KC)

            def mod_rows(g):
                pe.wait_ge(acc_done, g + 1)
                for k in range(4):
                    if (g, k) != (1, 0):
                        pe.wait_ge(mod_copied, 4 * (g - 1) + k)
                    pe.matmul(ps_mod[:, :], sh.const("ones"), accs[g][:, k * 512:(k + 1) * 512],
                              start=True, stop=True).then_inc(mod_summed, 1)

            pe.wait_ge(mod1_ready, 1)
            for j in range(COL_TILES):
                g = j // 4
                m = min(P, N_IN - j * P)
                if j % 4 == 0:
                    pe.wait_ge(win_in[g % WBUF], 16 * (g // WBUF + 1))
                if j >= 4:
                    pe.wait_ge(p_copied, j - 3)
                for c in range(KC):
                    last = pe.matmul(ps_p[j % 4][0:m, :], win[:, g % WBUF, c, (j % 4) * P:(j % 4) * P + m], uT[:, c, :],
                                     start=(c == 0), stop=(c == KC - 1))
                last.then_inc(p_done, 1)
                if j == 11:
                    mod_rows(1)
            mod_rows(2)

        def copy_mod(act, g):
            for k in range(4):
                act.wait_ge(mod_summed, 4 * (g - 1) + k + 1)
                act.copy(accs[g][:, k * 512:(k + 1) * 512], ps_mod[:, :]).then_inc(mod_copied, 1)

        @block.scalar
        def _(act):
            act.wait_ge(cols_ready, 1)
            act.activation(sig_c[:, :], cols[:, 0:KC], ACT.Sigmoid).then_inc(sig_ready, 1)
            act.wait_ge(mod1_ready, 1)
            for c in range(KC):
                act.wait_ge(x_turned, c + 1)
                act.activation(uT[:, c, :], ps_x[c % 2][:, :], ACT.Identity, bias=mod1[:, c:c + 1],
                               scale=mod1[:, KC + c:KC + c + 1]).then_inc(uT_ready, 1)
            act.wait_ge(edge_zero, 1)
            for j in range(COL_TILES):
                m = min(P, N_IN - j * P)
                act.wait_ge(p_done, j + 1)
                if j < SHIFT_TILES:
                    if j >= 2:
                        act.wait_ge(p_shifted, j - 1)
                    act.copy(praw[0:m, j % 2, 1:S + 1], ps_p[j % 4][0:m, :]).then_inc(p_copied, 1)
                else:
                    act.copy(sh.pT[0:m, j, :], ps_p[j % 4][0:m, :]).then_inc(p_copied, 1)
                if j == 11:
                    copy_mod(act, 1)
            copy_mod(act, 2)

        @block.vector
        def _(v):
            v.memset(acc0, 0.0).then_inc(acc_zero, 1)
            v.wait_ge(vec_turned, 1)
            v.tensor_copy(cols[:, 0:N_VEC], ps_vec[:, 0:N_VEC]).then_inc(cols_ready, 1)
            v.wait_ge(sig_ready, 1)
            v.wait_ge(cols_ready, 1)
            v.tensor_tensor(c_act[:, :], cols[:, 0:KC], sig_c[:, :], ALU.mult).then_inc(c_ready, 1)
            v.wait_ge(c_ready, 1)

            def gather_mod(g, k):
                n = g * N_G + k
                if k == 0:
                    v.wait_ge(bias_in, 16 * (1 if g == 0 else 3))
                v.wait_ge(ada_in[n % RING], 16 * (n // RING + 1))
                if k >= 2:
                    v.wait_ge(ada_used, n - 1)
                a = accs[g][:, (k % 2) * HALF:(k % 2 + 1) * HALF]
                v.scalar_tensor_tensor(a, ada[:, n % RING, :], c_act[:, k // 2:k // 2 + 1], a, ALU.mult, ALU.add).then_inc(ada_used, 1)
                if k == N_G - 1:
                    v.wait_ge(ada_used, n + 1)
                    v.engine_nop().then_inc(acc_done, 1)

            for k in range(N_G):
                gather_mod(0, k)
            v.memset(accs[1], 0.0).then_inc(acc_zero, 1)
            v.memset(accs[2], 0.0).then_inc(acc_zero, 1)
            v.memset(praw[:, :, 0:1], 0.0).then_inc(edge_zero, 1)
            v.wait_ge(mod1_summed, 1)
            v.tensor_copy(mod1[:, 0:KC], ps_mod[:, 0:KC])
            v.tensor_scalar(mod1[:, KC:2 * KC], ps_mod[:, KC:2 * KC], 1.0, None, ALU.add).then_inc(mod1_ready, 1)

            k = 0
            for j in range(SHIFT_TILES):
                while k < 32 and k < (j + 1) * 3:
                    gather_mod(1 + k // N_G, k % N_G)
                    k += 1
                v.wait_ge(p_copied, j + 1)
                raw = praw[:, j % 2, :]
                v.tensor_tensor(pdif[:, j % 2, :], raw[:, 0:S], raw[:, 1:S + 1], ALU.subtract).then_inc(p_diff, 1)
                v.wait_ge(p_diff, j + 1)
                mu = sh.col("shift_mu", j)
                v.scalar_tensor_tensor(sh.pT[:, j, :], pdif[:, j % 2, :], mu, raw[:, 1:S + 1], ALU.mult, ALU.add).then_inc(p_shifted, 1)


def attend(nc, io, sh):
    UNITS = [(i, h) for i in range(NT) for h in range(HEADS)]
    SCALE = C ** -0.5
    with ExitStack() as ctx:
        e = ctx.enter_context
        wq = e(nc.sbuf_tensor("w_q_up_sb", [P, 2, D_GROUP], F32))
        wi = e(nc.sbuf_tensor("idx_w_q_sb", [P, 2, D_GROUP], F32))
        wuk = e(nc.sbuf_tensor("w_uk_sb", [P, NPAIR, KV_LORA], F32))
        wuv = e(nc.sbuf_tensor("w_uv_sb", [P, HEADS, C], F32))
        sq = e(nc.sbuf_tensor("squares", [P, 3, S], F32))
        root = e(nc.sbuf_tensor("roots", [P, 3, S], F32))
        q_lat = e(nc.sbuf_tensor("q_lat", [P, 2, S], F32))
        c_lat = e(nc.sbuf_tensor("c_lat", [P, S], F32))
        c_tm = e(nc.sbuf_tensor("c_tm", [P, NT, KV_LORA], F32))
        ikd = e(nc.sbuf_tensor("ik_centred", [C, 2, S], F32))
        ik = e(nc.sbuf_tensor("ik", [P, S], F32))
        iw = e(nc.sbuf_tensor("iw_tm", [P, NT, HEADS], F32))
        qT = e(nc.sbuf_tensor("qT", [P, NPAIR, S], F32))
        iqT = e(nc.sbuf_tensor("iqT", [P, NPAIR, S], F32))
        q_abs = e(nc.sbuf_tensor("q_abs", [P, HEADS, S], F32))
        relu = e(nc.sbuf_tensor("relu", [P, 2, S], F32))
        score = e(nc.sbuf_tensor("score", [P, NT, S], F32))
        bias = e(nc.sbuf_tensor("key_bias", [P, NT, S], F32))
        best = e(nc.sbuf_tensor("best8", [P, 2, 8], F32))
        logit = e(nc.sbuf_tensor("logit", [P, 2, S], F32))
        prob = e(nc.sbuf_tensor("prob", [P, 2, S], F32))
        probT = e(nc.sbuf_tensor("probT", [P, 2, S], F32))
        o_lat = e(nc.sbuf_tensor("o_lat", [P, 2, P], F32))
        stat = e(nc.sbuf_tensor("softmax_stats", [P, 4, NT * HEADS], F32))
        bank = psum_banks(nc, e, "attend")

        sem = sh.sem
        aw_in = sem("attend_w_in")
        squared, summed, rooted, rinv_ready = sem("squared"), sem("summed"), sem("rooted"), sem("rinv_ready")
        lat_ready, ik_step, ik_ready, iw_turned, iw_ready = sem("lat_ready"), sem("ik_step"), sem("ik_ready"), sem("iw_turned"), sem("iw_ready")
        q_done, q_copied, qa_done, qa_copied = sem("q_done"), sem("q_copied"), sem("qa_done"), sem("qa_copied")
        c_turned, c_copied = sem("c_turned"), sem("c_copied")
        idx_done, relu_ready, score_added = sem("idx_done"), sem("relu_ready"), sem("score_added")
        top_step, bias_ready = sem("top_step"), sem("bias_ready")
        zeros_ready, y_zeroed = sem("zeros_ready"), sem("y_zeroed")
        zeros = relu[:, :, :].rearrange("p a b -> p (a b)")
        l_done, l_ready, nmax_ready, prob_ready, prob_turned = sem("l_done"), sem("l_ready"), sem("nmax_ready"), sem("prob_ready"), sem("prob_turned")
        probT_ready, pv_done, olat_ready, o_done, o_ready, rsum_ready = sem("probT_ready"), sem("pv_done"), sem("olat_ready"), sem("o_done"), sem("o_ready"), sem("rsum_ready")
        Q0, KV0, IK0 = SHIFT_TILES, SHIFT_TILES + 2, SHIFT_TILES + 3
        half = lambda h: slice(C * (h % 2), C * (h % 2) + C)
        idx_units = [(i, h) for i in range(1, NT) for h in range(HEADS)]
        block = e(nc.Block())

        @block.sync
        def _(sp):
            sp.dma_start(wq[:, :, :], io["mla_w_q_up"][0].rearrange("(c p) n -> p c n", p=P)).then_inc(aw_in, 16)
            sp.dma_start(wi[:, :, :], io["idx_w_q"][0].rearrange("(c p) n -> p c n", p=P)).then_inc(aw_in, 16)
            sp.dma_start(wuk[:, :, :], io["mla_w_uk"][0].rearrange("(a b) d c -> (b d) a c", b=2)).then_inc(aw_in, 16)
            sp.dma_start(wuv[:, :, :], io["mla_w_uv"][0].rearrange("h c d -> c h d")).then_inc(aw_in, 16)
            sp.wait_ge(zeros_ready, 1)
            for n in range(EXTRA):
                at = (N_EXP + n) * P
                sp.dma_start(sh.y_dram[at:at + P, :], zeros[:, :]).then_inc(y_zeroed, 16)
            sp.wait_ge(y_zeroed, 16 * EXTRA)

        @block.tensor
        def _(pe):
            ident, ones = sh.const("ident"), sh.const("ones")
            pe.matmul(bank[2][0:C, :], ones[0:C, 0:C], sh.pT[0:C, IK0, :], start=True, stop=True).then_inc(summed, 1)
            pe.wait_ge(squared, 3)
            pe.matmul(bank[0][:, :], ones, sq[:, 0, :], start=True, stop=False)
            pe.matmul(bank[0][:, :], ones, sq[:, 1, :], start=False, stop=True).then_inc(summed, 1)
            pe.matmul(bank[1][:, :], ones, sq[:, 2, :], start=True, stop=True).then_inc(summed, 1)
            for i in range(NT):
                last = pe.transpose(bank[4][:, i * HEADS:(i + 1) * HEADS], sh.pT[C:C + HEADS, IK0, i * P:(i + 1) * P],
                                    ident[C:C + HEADS, C:C + HEADS])
            last.then_inc(iw_turned, 1)
            pe.wait_ge(ik_step, 2)
            pe.matmul(bank[3][0:C, :], ones[0:C, 0:C], ikd[:, 1, :], start=True, stop=True).then_inc(summed, 1)
            pe.wait_ge(aw_in, 64)
            pe.wait_ge(lat_ready, 3)
            for i in range(NT):
                last = pe.transpose(bank[5][:, i * P:(i + 1) * P], c_lat[:, i * P:(i + 1) * P], ident)
            last.then_inc(c_turned, 1)
            for n in range(2 * NPAIR):
                w = wq if n < NPAIR else wi
                b = bank[6 + n % 2]
                if n >= 2:
                    pe.wait_ge(q_copied, n - 1)
                for k in range(2):
                    last = pe.matmul(b[:, :], w[:, k, (n % NPAIR) * P:(n % NPAIR + 1) * P], q_lat[:, k, :], start=(k == 0), stop=(k == 1))
                last.then_inc(q_done, 1)
            pe.wait_ge(q_copied, 2 * NPAIR)
            pe.wait_ge(ik_ready, 2)
            for n, (i, h) in enumerate(idx_units):
                b = bank[6 + n % 2]
                if n >= 2:
                    pe.wait_ge(relu_ready, n - 1)
                k = (i + 1) * P
                pe.matmul(b[:, 0:k], iqT[half(h), h // 2, i * P:(i + 1) * P], ik[half(h), 0:k], start=True, stop=True).then_inc(idx_done, 1)
            pe.wait_ge(rooted, 3)
            for h in range(HEADS):
                b = bank[h % 2]
                if h >= 2:
                    pe.wait_ge(qa_copied, h - 1)
                pe.matmul(b[:, :], wuk[half(h), h // 2, :], qT[half(h), h // 2, :], start=True, stop=True).then_inc(qa_done, 1)
            pe.wait_ge(qa_copied, HEADS)
            pe.wait_ge(relu_ready, len(idx_units))
            pe.wait_ge(c_copied, 1)
            pe.wait_ge(iw_ready, 1)
            N = len(UNITS)
            for u in range(N + 3):
                if u < N:
                    i, h = UNITS[u]
                    if u >= 2:
                        pe.wait_ge(l_ready, u - 1)
                    k = (i + 1) * P
                    pe.matmul(bank[u % 2][:, 0:k], q_abs[:, h, i * P:(i + 1) * P], c_lat[:, 0:k], start=True, stop=True).then_inc(l_done, 1)
                if 1 <= u <= N:
                    w = u - 1
                    i, h = UNITS[w]
                    pe.wait_ge(prob_ready, w + 1)
                    if w >= 2:
                        pe.wait_ge(probT_ready, w - 1)
                    for b in range(i + 1):
                        last = pe.transpose(bank[2 + w % 2][:, b * P:(b + 1) * P], prob[:, w % 2, b * P:(b + 1) * P], ident)
                    last.then_inc(prob_turned, 1)
                if 2 <= u <= N + 1:
                    w = u - 2
                    i, h = UNITS[w]
                    pe.wait_ge(probT_ready, w + 1)
                    if w >= 2:
                        pe.wait_ge(olat_ready, w - 1)
                    for b in range(i + 1):
                        last = pe.matmul(bank[4 + w % 2][:, 0:P], c_tm[:, b, :], probT[:, w % 2, b * P:(b + 1) * P], start=(b == 0), stop=(b == i))
                    last.then_inc(pv_done, 1)
                if u >= 3:
                    w = u - 3
                    i, h = UNITS[w]
                    pe.wait_ge(olat_ready, w + 1)
                    if w >= 2:
                        pe.wait_ge(o_ready, w - 1)
                    pe.matmul(bank[6 + w % 2][:, 0:C], o_lat[:, w % 2, :], wuv[:, h, :], start=True, stop=True).then_inc(o_done, 1)

        @block.scalar
        def _(act):
            for n, t in enumerate((Q0, Q0 + 1, KV0)):
                act.activation(sq[:, n, :], sh.pT[:, t, :], ACT.Square).then_inc(squared, 1)
            eps = sh.const("eps")
            act.wait_ge(summed, 2)
            act.activation(root[:, 0, :], bank[0][:, :], ACT.Sqrt, bias=eps[:, 0:1], scale=1.0 / Q_LORA).then_inc(rooted, 1)
            act.wait_ge(summed, 3)
            act.activation(root[:, 1, :], bank[1][:, :], ACT.Sqrt, bias=eps[:, 0:1], scale=1.0 / KV_LORA).then_inc(rooted, 1)
            act.wait_ge(summed, 4)
            act.activation(root[0:C, 2, :], bank[3][0:C, :], ACT.Sqrt, bias=eps[0:C, 1:2], scale=1.0 / IDX_DIM).then_inc(rooted, 1)
            for n in range(2 * NPAIR):
                act.wait_ge(q_done, n + 1)
                dst = qT if n < NPAIR else iqT
                act.copy(dst[:, n % NPAIR, :], bank[6 + n % 2][:, :]).then_inc(q_copied, 1)
            for n, (i, h) in enumerate(idx_units):
                k = (i + 1) * P
                act.wait_ge(idx_done, n + 1)
                if n >= 2:
                    act.wait_ge(score_added, n - 1)
                if n == 0:
                    act.wait_ge(y_zeroed, 16 * EXTRA)
                act.activation(relu[:, n % 2, 0:k], bank[6 + n % 2][:, 0:k], ACT.Relu).then_inc(relu_ready, 1)
            for h in range(HEADS):
                act.wait_ge(qa_done, h + 1)
                act.mul(q_abs[:, h, :], bank[h % 2][:, :], SCALE / SLOPES[h]).then_inc(qa_copied, 1)
            N = len(UNITS)
            for u in range(N + 1):
                if u < N:
                    i, h = UNITS[u]
                    k = (i + 1) * P
                    act.wait_ge(nmax_ready, u + 1)
                    if u >= 2:
                        act.wait_ge(prob_turned, u - 1)
                    act.activation(prob[:, u % 2, 0:k], logit[:, u % 2, 0:k], ACT.Exp, bias=stat[:, 1, u:u + 1],
                                   accum_out=stat[:, 2, u:u + 1]).then_inc(prob_ready, 1)
                if u >= 1:
                    w = u - 1
                    k = (UNITS[w][0] + 1) * P
                    act.wait_ge(prob_turned, w + 1)
                    if w >= 2:
                        act.wait_ge(pv_done, w - 1)
                    act.copy(probT[:, w % 2, 0:k], bank[2 + w % 2][:, 0:k]).then_inc(probT_ready, 1)

        @block.vector
        def _(v):
            v.memset(zeros, 0.0).then_inc(zeros_ready, 1)
            v.wait_ge(summed, 1)
            v.scalar_tensor_tensor(ikd[:, 0, :], bank[2][0:C, :], -1.0 / IDX_DIM, sh.pT[0:C, IK0, :], ALU.mult, ALU.add).then_inc(ik_step, 1)
            v.wait_ge(ik_step, 1)
            v.tensor_tensor(ikd[:, 1, :], ikd[:, 0, :], ikd[:, 0, :], ALU.mult).then_inc(ik_step, 1)
            for n in range(2):
                v.wait_ge(rooted, n + 1)
                v.reciprocal(root[:, n, :], root[:, n, :]).then_inc(rinv_ready, 1)
            v.wait_ge(rinv_ready, 2)
            for n in range(2):
                v.scalar_tensor_tensor(q_lat[:, n, :], sh.pT[:, Q0 + n, :], sh.col("mla_q_norm", n), root[:, 0, :], ALU.mult, ALU.mult).then_inc(lat_ready, 1)
            v.scalar_tensor_tensor(c_lat[:, :], sh.pT[:, KV0, :], sh.col("mla_kv_norm", 0), root[:, 1, :], ALU.mult, ALU.mult).then_inc(lat_ready, 1)
            v.wait_ge(rooted, 3)
            v.reciprocal(root[0:C, 2, :], root[0:C, 2, :]).then_inc(rinv_ready, 1)
            v.wait_ge(rinv_ready, 3)
            v.tensor_tensor(ikd[:, 1, :], ikd[:, 0, :], root[0:C, 2, :], ALU.mult).then_inc(ik_step, 1)
            v.wait_ge(ik_step, 3)
            v.tensor_scalar(ik[0:C, :], ikd[:, 1, :], sh.col("idx_ln_g", 0)[0:C], sh.col("idx_ln_b", 0)[0:C], ALU.mult, ALU.add).then_inc(ik_ready, 1)
            v.wait_ge(ik_ready, 1)
            v.tensor_copy(ik[C:P, :], ik[0:C, :]).then_inc(ik_ready, 1)
            v.wait_ge(iw_turned, 1)
            v.tensor_scalar(iw[:, :, :], bank[4][:, 0:NT * HEADS].rearrange("p (a b) -> p a b", b=HEADS),
                            float(HEADS ** -0.5 * IDX_DIM ** -0.5), None, ALU.mult).then_inc(iw_ready, 1)
            v.wait_ge(c_turned, 1)
            v.tensor_copy(c_tm[:, :, :], bank[5][:, :].rearrange("p (a b) -> p a b", b=P)).then_inc(c_copied, 1)
            v.memset(score[:, :, :], 0.0).then_inc(top_step, 1)
            v.wait_ge(top_step, 1)
            for i in range(NT):
                v.tensor_copy(score[:, i, i * P:(i + 1) * P], sh.const("causal")).then_inc(top_step, 1)
            steps = 1 + NT
            v.wait_ge(top_step, steps)
            v.wait_ge(iw_ready, 1)
            for n, (i, h) in enumerate(idx_units):
                k = (i + 1) * P
                v.wait_ge(relu_ready, n + 1)
                if n:
                    v.wait_ge(score_added, n)
                v.scalar_tensor_tensor(score[:, i, 0:k], relu[:, n % 2, 0:k], iw[:, i, h:h + 1], score[:, i, 0:k], ALU.mult, ALU.add).then_inc(score_added, 1)
            v.wait_ge(score_added, len(idx_units))
            for i in range(1, NT):
                k = (i + 1) * P
                for r in range(TOPK // 8):
                    v.max(best[:, r % 2, :], score[:, i, 0:k]).then_inc(top_step, 1)
                    v.wait_ge(top_step, steps + 1)
                    v.match_replace(score[:, i, 0:k], best[:, r % 2, :], score[:, i, 0:k], TAKEN).then_inc(top_step, 1)
                    steps += 2
                    v.wait_ge(top_step, steps)
            for i in range(1, NT):
                k = (i + 1) * P
                v.tensor_scalar(score[:, i, 0:k], score[:, i, 0:k], TAKEN, NEG, ALU.is_gt, ALU.mult).then_inc(top_step, 1)
                steps += 1
            v.wait_ge(top_step, steps)
            for i in range(NT):
                k = (i + 1) * P
                v.scalar_tensor_tensor(bias[:, i, 0:k], sh.const("dist")[:, 0:k], float(-i * P), score[:, i, 0:k], ALU.add, ALU.add).then_inc(bias_ready, 1)
            v.wait_ge(bias_ready, NT)
            N = len(UNITS)
            for u in range(N + 3):
                if u < N:
                    i, h = UNITS[u]
                    k = (i + 1) * P
                    v.wait_ge(l_done, u + 1)
                    if u >= 2:
                        v.wait_ge(prob_ready, u - 1)
                    v.tensor_tensor_reduce(logit[:, u % 2, 0:k], bank[u % 2][:, 0:k], bias[:, i, 0:k], SLOPES[h], TAKEN,
                                           ALU.add, ALU.max, stat[:, 0, u:u + 1]).then_inc(l_ready, 1)
                    v.wait_ge(l_ready, u + 1)
                    v.tensor_scalar(stat[:, 1, u:u + 1], stat[:, 0, u:u + 1], -1.0, None, ALU.mult).then_inc(nmax_ready, 1)
                if 2 <= u <= N + 1:
                    w = u - 2
                    v.wait_ge(pv_done, w + 1)
                    if w >= 2:
                        v.wait_ge(o_done, w - 1)
                    v.tensor_copy(o_lat[:, w % 2, :], bank[4 + w % 2][:, 0:P]).then_inc(olat_ready, 1)
                    v.reciprocal(stat[:, 3, w:w + 1], stat[:, 2, w:w + 1]).then_inc(rsum_ready, 1)
                if u >= 3:
                    w = u - 3
                    i, h = UNITS[w]
                    v.wait_ge(o_done, w + 1)
                    v.wait_ge(rsum_ready, w + 1)
                    v.tensor_scalar(sh.cat[:, i, D_GROUP + h * C:D_GROUP + (h + 1) * C], bank[6 + w % 2][:, 0:C],
                                    stat[:, 3, w:w + 1], None, ALU.mult).then_inc(o_ready, 1)


def prepare(nc, io, sh):
    with ExitStack() as ctx:
        e = ctx.enter_context
        w2a2 = e(nc.sbuf_tensor("w2_a2_sb", [P, D_GROUP], F32))
        tanh = e(nc.sbuf_tensor("tanh_w", [C, S], F32))
        sig = e(nc.sbuf_tensor("sig_w", [P, NPAIR, S], F32))
        cum = e(nc.sbuf_tensor("cum", [P, NPAIR, S], F32))
        sqk = e(nc.sbuf_tensor("kk_squares", [P, 2, S], F32))
        root = e(nc.sbuf_tensor("kk_root", [P, NPAIR, S], F32))
        rate = e(nc.sbuf_tensor("rate", [P, 2, S], F32))
        prod = e(nc.sbuf_tensor("rk_prod", [P, 2, S], F32))
        grow = e(nc.sbuf_tensor("decays", [P, 3, 2, S], F32))
        bank = psum_banks(nc, e, "prepare")
        b_hat = sh.b_hat
        KK0 = SHIFT_TILES

        sem = sh.sem
        pw_in, tanh_ready, lora_done, sig_ready, gate_ready = sem("prep_w_in"), sem("tanh_ready"), sem("lora_done"), sem("sigw_ready"), sem("gate_sig_ready")
        kk_raw, kk_squared, kk_summed, kk_rooted = sem("kk_raw"), sem("kk_squared"), sem("kk_summed"), sem("kk_rooted")
        root_step, kk_ready, rate_ready, k_ready, b_ready = sem("root_step"), sem("kk_ready"), sem("rate_ready"), sem("k_ready"), sem("b_ready")
        prod_ready, bonus_done, cum_ready, dif_ready, grown, scaled = sem("prod_ready"), sem("bonus_done"), sem("cum_ready"), sem("dif_ready"), sem("grown"), sem("scaled")
        v_turned, v_copied, bonus_copied, end_ready = sem("v_turned"), sem("v_copied"), sem("bonus_copied"), sem("end_ready")
        R0, K0, V0, WA, G0 = 0, NPAIR, 2 * NPAIR, 3 * NPAIR, 3 * NPAIR + 1
        block = e(nc.Block())

        @block.sync
        def _(sp):
            sp.dma_start(w2a2[0:C, :], io["rwkv_w2"][0]).then_inc(pw_in, 16)
            sp.dma_start(w2a2[C:P, :], io["rwkv_a2"][0]).then_inc(pw_in, 16)

        @block.tensor
        def _(pe):
            ident = sh.const("ident")
            pe.wait_ge(pw_in, 32)
            pe.wait_ge(tanh_ready, 1)
            for g in range(NPAIR):
                cs = slice(g * P, (g + 1) * P)
                if g >= 2:
                    pe.wait_ge(sig_ready, 2 * (g - 1))
                pe.matmul(bank[g % 2][:, :], w2a2[0:C, cs], tanh[:, :], start=True, stop=True).then_inc(lora_done, 1)
                pe.matmul(bank[2 + g % 2][:, :], w2a2[C:P, cs], sh.pT[C:P, WA, :], start=True, stop=True).then_inc(lora_done, 1)
            for g in range(NPAIR):
                pe.wait_ge(kk_squared, g + 1)
                if g >= 2:
                    pe.wait_ge(kk_rooted, g - 1)
                pe.matmul(bank[4 + g % 2][:, :], sh.const("half"), sqk[:, g % 2, :], start=True, stop=True).then_inc(kk_summed, 1)
                if g >= 1:
                    pe.wait_ge(v_copied, g)
                for i in range(NT):
                    last = pe.transpose(bank[6][:, i * P:(i + 1) * P], sh.pT[:, V0 + g, i * P:(i + 1) * P], ident)
                last.then_inc(v_turned, 1)
            for g in range(NPAIR):
                pe.wait_ge(prod_ready, g + 1)
                for i in range(NT):
                    last = pe.matmul(bank[7][:, i * HEADS + 2 * g:i * HEADS + 2 * g + 2], prod[:, g % 2, i * P:(i + 1) * P],
                                     sh.const("heads"), start=True, stop=True)
                last.then_inc(bonus_done, 1)

        @block.scalar
        def _(act):
            act.activation(tanh[:, :], sh.pT[0:C, WA, :], ACT.Tanh).then_inc(tanh_ready, 1)
            act.activation(sh.gate_sig[:, :], sh.pT[:, G0, :], ACT.Sigmoid).then_inc(gate_ready, 1)
            for g in range(NPAIR):
                act.wait_ge(lora_done, 2 * g + 2)
                act.activation(sig[:, g, :], bank[g % 2][:, :], ACT.Sigmoid, bias=sh.col("rwkv_w0", g)).then_inc(sig_ready, 1)
                act.activation(b_hat[:, g, :], bank[2 + g % 2][:, :], ACT.Sigmoid, bias=sh.col("rwkv_a0", g)).then_inc(sig_ready, 1)
            for g in range(NPAIR):
                act.wait_ge(kk_raw, g + 1)
                if g >= 2:
                    act.wait_ge(kk_summed, g - 1)
                act.activation(sqk[:, g % 2, :], sh.pT[:, KK0 + g, :], ACT.Square).then_inc(kk_squared, 1)
                act.wait_ge(kk_summed, g + 1)
                act.activation(root[:, g, :], bank[4 + g % 2][:, :], ACT.Sqrt).then_inc(kk_rooted, 1)
                act.wait_ge(v_turned, g + 1)
                act.copy(sh.v_tm[:, :, g * P:(g + 1) * P], bank[6][:, :].rearrange("p (a b) -> p a b", b=P)).then_inc(v_copied, 1)
            for g in range(NPAIR):
                act.wait_ge(cum_ready, g + 1)
                if g >= 2:
                    act.wait_ge(scaled, 4 * (g - 1))
                    act.wait_ge(end_ready, g - 1)
                act.activation(grow[:, 0, g % 2, :], cum[:, g, :], ACT.Exp, scale=-DECAY).then_inc(grown, 1)
                act.activation(grow[:, 1, g % 2, :], cum[:, g, :], ACT.Exp, scale=DECAY).then_inc(grown, 1)
                act.wait_ge(dif_ready, g + 1)
                act.activation(grow[:, 2, g % 2, :], sig[:, g, :], ACT.Exp, scale=-DECAY).then_inc(grown, 1)

        @block.vector
        def _(v):
            keep = sh.const("keep")
            for g in range(NPAIR):
                v.tensor_scalar(sh.pT[:, KK0 + g, :], sh.pT[:, K0 + g, :], sh.col("rwkv_k_k", g), None, ALU.mult).then_inc(kk_raw, 1)
            for g in range(NPAIR):
                v.wait_ge(sig_ready, 2 * g + 2)
                v.tensor_tensor_scan(cum[:, g, :], keep, sig[:, g, :], 0.0, ALU.mult, ALU.add).then_inc(cum_ready, 1)
                v.tensor_scalar(rate[:, g % 2, :], b_hat[:, g, :], -1.0, sh.col("rwkv_k_a", g), ALU.add, ALU.mult).then_inc(rate_ready, 1)
                v.wait_ge(cum_ready, g + 1)
                v.tensor_tensor(sig[:, g, :], cum[:, g, :], sig[:, g, :], ALU.subtract).then_inc(dif_ready, 1)
                v.wait_ge(rate_ready, g + 1)
                v.scalar_tensor_tensor(sh.pT[:, K0 + g, :], rate[:, g % 2, :], 1.0, sh.pT[:, K0 + g, :], ALU.add, ALU.mult).then_inc(k_ready, 1)
                v.wait_ge(k_ready, g + 1)
                if g >= 2:
                    v.wait_ge(bonus_done, g - 1)
                v.scalar_tensor_tensor(prod[:, g % 2, :], sh.pT[:, R0 + g, :], sh.col("rwkv_r_k", g), sh.pT[:, K0 + g, :], ALU.mult, ALU.mult).then_inc(prod_ready, 1)
            for g in range(NPAIR):
                v.wait_ge(kk_rooted, g + 1)
                v.tensor_scalar(root[:, g, :], root[:, g, :], 1e-12, None, ALU.max).then_inc(root_step, 1)
                v.wait_ge(root_step, 2 * g + 1)
                v.reciprocal(root[:, g, :], root[:, g, :]).then_inc(root_step, 1)
                v.wait_ge(root_step, 2 * g + 2)
                v.tensor_tensor(sh.pT[:, KK0 + g, :], sh.pT[:, KK0 + g, :], root[:, g, :], ALU.mult).then_inc(kk_ready, 1)
                v.wait_ge(kk_ready, g + 1)
                v.tensor_tensor(b_hat[:, g, :], b_hat[:, g, :], sh.pT[:, KK0 + g, :], ALU.mult).then_inc(b_ready, 1)
            v.wait_ge(b_ready, NPAIR)
            v.wait_ge(prod_ready, NPAIR)
            for g in range(NPAIR):
                b = g % 2
                v.wait_ge(grown, 3 * g + 1)
                v.tensor_tensor(sh.pT[:, R0 + g, :], sh.pT[:, R0 + g, :], grow[:, 0, b, :], ALU.mult).then_inc(scaled, 1)
                v.tensor_copy(sh.w_end[:, g, :], grow[:, 0, b, C - 1::C]).then_inc(end_ready, 1)
                v.wait_ge(grown, 3 * g + 2)
                v.tensor_tensor(b_hat[:, g, :], b_hat[:, g, :], grow[:, 1, b, :], ALU.mult).then_inc(scaled, 1)
                v.tensor_tensor(sh.pT[:, K0 + g, :], sh.pT[:, K0 + g, :], grow[:, 1, b, :], ALU.mult).then_inc(scaled, 1)
                v.wait_ge(grown, 3 * g + 3)
                v.scalar_tensor_tensor(sh.pT[:, KK0 + g, :], sh.pT[:, KK0 + g, :], -1.0, grow[:, 2, b, :], ALU.mult, ALU.mult).then_inc(scaled, 1)
            v.wait_ge(bonus_done, NPAIR)
            v.tensor_copy(sh.bonus[:, :, :], bank[7][:, 0:NT * HEADS].rearrange("p (a b) -> p a b", b=HEADS)).then_inc(bonus_copied, 1)


PE_STEPS = ["ba", "ab"] + [f"{s}{n}" for n in LEVELS for s in ("z", "t", "tt") if (s, n) != ("t", LEVELS[-1])] + \
           ["ka", "akv", "x", "oo", "rr", "m0", "n0"]
ACT_STEPS = ["abt"] + [f"{s}{n}" for n in LEVELS for s in ("t", "tt") if (s, n) != ("t", LEVELS[-1])] + ["akv", "x", "oo"]
DVE_STEPS = ["arb", "t", "tt"] + [f"z{n}" for n in LEVELS] + ["ka", "rr", "m0", "n0"]
POOL_STEPS = [f"lv{n}" for n in LEVELS]


def scan(nc, io, sh):
    with ExitStack() as ctx:
        e = ctx.enter_context
        two = range(2)
        g2 = e(nc.sbuf_tensor("g2_sb", [P, D_GROUP], F32))
        lnb = e(nc.sbuf_tensor("rwkv_ln_sb", [P, 2, D_GROUP], F32))
        tm = e(nc.sbuf_tensor("abk_tm", [P, 3, NT, P], F32))
        Tm = [e(nc.sbuf_tensor(f"T{h}", [P, NT, P], F32)) for h in two]
        TT = [e(nc.sbuf_tensor(f"TT{h}", [P, NT, P], F32)) for h in two]
        Z1 = [e(nc.sbuf_tensor(f"Z1{h}", [P, NT, P], F32)) for h in two]
        LV = [e(nc.sbuf_tensor(f"LV{h}", [P, NT, P], F32)) for h in two]
        ABT = [e(nc.sbuf_tensor(f"ABT{h}", [P, NT, P], F32)) for h in two]
        ARB = [e(nc.sbuf_tensor(f"ARB{h}", [P, NT, P], F32)) for h in two]
        KA = [e(nc.sbuf_tensor(f"KA{h}", [P, NT, 2, P], F32)) for h in two]
        AKV = [e(nc.sbuf_tensor(f"AKV{h}", [P, NT, C], F32)) for h in two]
        X = [e(nc.sbuf_tensor(f"X{h}", [P, NT, P], F32)) for h in two]
        RR = e(nc.sbuf_tensor("RR", [P, S], F32))
        M0 = e(nc.sbuf_tensor("M0", [P, NCH, C], F32))
        N0 = e(nc.sbuf_tensor("N0", [P, NCH, C], F32))
        ST = e(nc.sbuf_tensor("state", [P, NCH + 1, C], F32))
        gn = e(nc.sbuf_tensor("gn_stats", [P, NT, 4, HEADS], F32))
        bank = psum_banks(nc, e, "scan")
        own = [bank[0:4], bank[4:8]]

        sem = sh.sem
        sw_in, tm_turned, tm_copied = sem("scan_w_in"), sem("tm_turned"), sem("tm_copied")
        pe_step = [sem(f"pe_step{h}") for h in two]
        act_step = [sem(f"act_step{h}") for h in two]
        dve_step = [sem(f"dve_step{h}") for h in two]
        pool_step = [sem(f"pool_step{h}") for h in two]
        dve_half = sem("dve_half")
        state_done, state_ready, carry_done, carry_added = sem("state_done"), sem("state_ready"), sem("carry_done"), sem("carry_added")
        gn_sum, gn_dev, gn_sq, gn_var, gn_root, gn_step, gate_done, gate_free = (sem("gn_sum"), sem("gn_dev"), sem("gn_sq"), sem("gn_var"),
                                                                    sem("gn_root"), sem("gn_step"), sem("gate_done"), sem("gate_free"))
        R0, K0, A0 = 0, NPAIR, SHIFT_TILES
        half = lambda h: slice(C * h, C * h + C)

        def pe_after(eng, h, r, name):
            eng.wait_ge(pe_step[h], r * len(PE_STEPS) + PE_STEPS.index(name) + 1)

        def act_after(eng, h, r, name):
            eng.wait_ge(act_step[h], r * len(ACT_STEPS) + ACT_STEPS.index(name) + 1)

        def dve_after(eng, h, r, name):
            eng.wait_ge(dve_step[h], r * len(DVE_STEPS) + DVE_STEPS.index(name) + 1)

        def pool_after(eng, h, r, name):
            eng.wait_ge(pool_step[h], r * len(POOL_STEPS) + POOL_STEPS.index(name) + 1)

        flat = lambda t: t[:, :, :].rearrange("p a b -> p (a b)")
        dev = lambda i: flat(Tm[i % 2])
        sqd = lambda i: flat(TT[i % 2])

        def tiles(ap):
            return ap.rearrange("p (a b) -> p a b", b=P)

        def bc(ap, n):
            return ap.rearrange("p (a m) -> p a m", a=1).broadcast_to([ap.shape[0], n, ap.shape[1]])

        block = e(nc.Block())

        @block.sync
        def _(sp):
            sp.dma_start(g2[:, :], io["rwkv_g2"][0]).then_inc(sw_in, 16)
            sp.dma_start(lnb[:, 0, :], io["rwkv_ln_w"].broadcast_to([P, D_GROUP])).then_inc(sw_in, 16)
            sp.dma_start(lnb[:, 1, :], io["rwkv_ln_b"].broadcast_to([P, D_GROUP])).then_inc(sw_in, 16)

        @block.tensor
        def _(pe):
            ident = sh.const("ident")
            for r in range(NPAIR):
                for n, src in enumerate((sh.pT[:, A0 + r, :], sh.b_hat[:, r, :], sh.pT[:, K0 + r, :])):
                    if r:
                        pe.wait_ge(carry_added, r)
                        dve_after(pe, 0, r - 1, "n0")
                        dve_after(pe, 1, r - 1, "n0")
                    for i in range(NT):
                        last = pe.transpose(bank[n][:, i * P:(i + 1) * P], src[:, i * P:(i + 1) * P], ident)
                    last.then_inc(tm_turned, 1)
                pe.wait_ge(tm_copied, 3 * (r + 1))
                for h in two:
                    if r:
                        act_after(pe, h, r - 1, "oo")
                    for i in range(NT):
                        ts = slice(i * P, (i + 1) * P)
                        last = pe.matmul(own[h][i // 2][:, (i % 2) * 256:(i % 2) * 256 + 256].rearrange("p (a b) -> p a b", b=P), sh.b_hat[half(h), r, ts],
                                         sh.pT[half(h), R0 + r:A0 + r + 1:A0 - R0, ts],
                                         start=True, stop=True)
                    last.then_inc(pe_step[h], 1)
                for h in two:
                    for i in range(NT):
                        ts = slice(i * P, (i + 1) * P)
                        last = pe.matmul(own[h][2][:, ts], sh.pT[half(h), A0 + r, ts], sh.b_hat[half(h), r, ts], start=True, stop=True)
                    last.then_inc(pe_step[h], 1)
                for n in LEVELS:
                    for h in two:
                        pool_after(pe, h, r, f"lv{n}")
                        if n == LEVELS[0]:
                            dve_after(pe, h, r, "tt")
                        else:
                            act_after(pe, h, r, f"t{n // 2}")
                            act_after(pe, h, r, f"tt{n // 2}")
                        for i in range(NT):
                            last = pe.matmul(own[h][3][:, i * P:(i + 1) * P], LV[h][:, i, :], Tm[h][:, i, :], start=True, stop=True)
                        last.then_inc(pe_step[h], 1)
                    for h in two:
                        dve_after(pe, h, r, f"z{n}")
                        if n != LEVELS[-1]:
                            for i in range(NT):
                                last = pe.matmul(own[h][0][:, i * P:(i + 1) * P], TT[h][:, i, :], Z1[h][:, i, :], start=True, stop=True)
                            last.then_inc(pe_step[h], 1)
                        for i in range(NT):
                            last = pe.matmul(own[h][1][:, i * P:(i + 1) * P], Z1[h][:, i, :], TT[h][:, i, :], start=True, stop=True)
                        last.then_inc(pe_step[h], 1)
                for h in two:
                    for i in range(NT):
                        ts = slice(i * P, (i + 1) * P)
                        last = pe.matmul(own[h][2 + i // 2][:, (i % 2) * 256:(i % 2) * 256 + 256].rearrange("p (a b) -> p a b", b=P), sh.pT[half(h), K0 + r, ts],
                                         sh.pT[half(h), R0 + r:A0 + r + 1:A0 - R0, ts], start=True, stop=True)
                    last.then_inc(pe_step[h], 1)
                vs = lambda h: slice(r * P + h * C, r * P + h * C + C)
                for h in two:
                    dve_after(pe, h, r, "ka")
                    for i in range(NT):
                        last = pe.matmul(own[h][0][:, i * C:(i + 1) * C], KA[h][:, i, 1, :], sh.v_tm[:, i, vs(h)], start=True, stop=True)
                    last.then_inc(pe_step[h], 1)
                for h in two:
                    act_after(pe, h, r, "akv")
                    act_after(pe, h, r, f"tt{LEVELS[-1]}")
                    for i in range(NT):
                        pe.matmul(own[h][1][:, i * P:i * P + C], TT[h][:, i, :], tm[:, 0, i, half(h)], start=True, stop=True)
                        last = pe.matmul(own[h][1][:, i * P + C:(i + 1) * P], TT[h][:, i, :], AKV[h][:, i, :], start=True, stop=True)
                    last.then_inc(pe_step[h], 1)
                for h in two:
                    act_after(pe, h, r, "x")
                    for i in range(NT):
                        pe.matmul(own[h][2][:, i * C:(i + 1) * C], KA[h][:, i, 0, :], sh.v_tm[:, i, vs(h)], start=True, stop=False)
                        last = pe.matmul(own[h][2][:, i * C:(i + 1) * C], ARB[h][:, i, :], X[h][:, i, C:P], start=False, stop=True)
                    last.then_inc(pe_step[h], 1)
                for h in two:
                    for i in range(NT):
                        last = pe.matmul(own[h][3][half(h), i * P:(i + 1) * P], X[h][:, i, 0:C], ARB[h][:, i, :], start=True, stop=True)
                    last.then_inc(pe_step[h], 1)
                for h in two:
                    act_after(pe, h, r, "oo")
                    for n in range(NCH):
                        tok = half(n % 2)
                        last = pe.matmul(own[h][2 * (n % 2)][half(h), n // 2 * C:(n // 2 + 1) * C], X[h][tok, n // 2, 0:C], tm[tok, 1, n // 2, half(h)], start=True, stop=True)
                    last.then_inc(pe_step[h], 1)
                for h in two:
                    dve_after(pe, h, r, "rr")
                    for n in range(NCH):
                        tok = half(n % 2)
                        out = own[h][1 + 2 * (n % 2)][half(h), n // 2 * C:(n // 2 + 1) * C]
                        pe.matmul(out, tm[tok, 2, n // 2, half(h)], sh.v_tm[tok, n // 2, vs(h)], start=True, stop=False)
                        last = pe.matmul(out, tm[tok, 1, n // 2, half(h)], X[h][tok, n // 2, C:P], start=False, stop=True)
                    last.then_inc(pe_step[h], 1)
                for n in range(NCH):
                    pe.wait_ge(state_ready, r * NCH + n + 1)
                    if n < NCH - 1 and n > 0:
                        for h in two:
                            last = pe.matmul(bank[2][half(h), (n % 2) * C:(n % 2) * C + C], M0[half(h), n, :], ST[half(h), n, :], start=True, stop=True)
                        last.then_inc(state_done, 1)
                    for h in two:
                        last = pe.matmul(own[h][3][half(n % 2), (n // 2) * C:(n // 2 + 1) * C], RR[half(h), n * C:(n + 1) * C], ST[half(h), n, :],
                                         start=True, stop=True)
                last.then_inc(carry_done, 1)
            pe.wait_ge(sw_in, 48)
            for i in range(NT):
                pe.wait_ge(carry_added, NPAIR)
                if i >= 2:
                    pe.wait_ge(gate_free, i - 1)
                pe.matmul(bank[i % 2][:, :], sh.gate_sig[:, i * P:(i + 1) * P], g2[:, :], start=True, stop=True).then_inc(gate_done, 1)

        @block.scalar
        def _(act):
            for r in range(NPAIR):
                for n in range(3):
                    act.wait_ge(tm_turned, 3 * r + n + 1)
                    act.copy(tm[:, n, :, :], tiles(bank[n][:, :])).then_inc(tm_copied, 1)
                for h in two:
                    pe_after(act, h, r, "ba")
                    for b in two:
                        last = act.copy(ABT[h][:, 2 * b:2 * b + 2, :], own[h][b][:, :].rearrange("p (a b c) -> p a b c", a=2, b=2)[:, :, 1, :])
                    last.then_inc(act_step[h], 1)
                for n in LEVELS:
                    for h in two:
                        if n != LEVELS[-1]:
                            pe_after(act, h, r, f"t{n}")
                            act.copy(Tm[h][:, :, :], tiles(own[h][0][:, :])).then_inc(act_step[h], 1)
                        pe_after(act, h, r, f"tt{n}")
                        act.copy(TT[h][:, :, :], tiles(own[h][1][:, :])).then_inc(act_step[h], 1)
                for h in two:
                    pe_after(act, h, r, "akv")
                    act.copy(AKV[h][:, :, :], own[h][0][:, 0:NT * C].rearrange("p (a b) -> p a b", b=C)).then_inc(act_step[h], 1)
                for h in two:
                    pe_after(act, h, r, "x")
                    act.copy(X[h][:, :, :], tiles(own[h][1][:, :])).then_inc(act_step[h], 1)
                for h in two:
                    pe_after(act, h, r, "oo")
                    act.copy(sh.cat[:, :, r * P + h * C:r * P + (h + 1) * C], own[h][2][:, 0:NT * C].rearrange("p (a b) -> p a b", b=C)).then_inc(act_step[h], 1)
            for i in range(NT):
                act.wait_ge(gn_dev, i + 1)
                act.activation(sqd(i), dev(i), ACT.Square).then_inc(gn_sq, 1)
                act.wait_ge(gn_var, i + 1)
                act.activation(gn[:, i, 2, :], gn[:, i, 1, :], ACT.Sqrt, bias=sh.const("eps")[:, 2:3], scale=1.0 / C).then_inc(gn_root, 1)

        @block.gpsimd
        def _(pool):
            for r in range(NPAIR):
                for n in LEVELS:
                    for h in two:
                        if n == LEVELS[0]:
                            act_after(pool, h, r, "abt")
                        else:
                            pe_after(pool, h, r, f"z{n // 2}")
                        pool.tensor_tensor(LV[h][:, :, :], ABT[h][:, :, :], bc(sh.const(f"lev{n}"), NT), ALU.mult).then_inc(pool_step[h], 1)

        @block.vector
        def _(v):
            halves = 0
            for r in range(NPAIR):
                for h in two:
                    act_after(v, h, r, "abt")
                    if r:
                        pe_after(v, h, r - 1, "n0")
                    for b in two:
                        last = v.tensor_tensor(ARB[h][:, 2 * b:2 * b + 2, :], own[h][b][:, :].rearrange("p (a b c) -> p a b c", a=2, b=2)[:, :, 0, :],
                                               bc(sh.const("incl"), 2), ALU.mult)
                    last.then_inc(dve_step[h], 1)
                    pe_after(v, h, r, "ab")
                    v.tensor_tensor(Tm[h][:, :, :], tiles(own[h][2][:, :]), bc(sh.const("low2"), NT), ALU.mult).then_inc(dve_half, 1)
                    v.tensor_tensor(TT[h][:, :, :], ABT[h][:, :, :], bc(sh.const("up2"), NT), ALU.mult).then_inc(dve_half, 1)
                    halves += 2
                    v.wait_ge(dve_half, halves)
                    v.tensor_tensor(Tm[h][:, :, :], Tm[h][:, :, :], bc(sh.const("ident"), NT), ALU.add).then_inc(dve_step[h], 1)
                    v.tensor_tensor(TT[h][:, :, :], TT[h][:, :, :], bc(sh.const("ident"), NT), ALU.add).then_inc(dve_step[h], 1)
                for n in LEVELS:
                    for h in two:
                        pe_after(v, h, r, f"z{n}")
                        v.tensor_tensor(Z1[h][:, :, :], tiles(own[h][3][:, :]), bc(sh.const("ident"), NT), ALU.add).then_inc(dve_step[h], 1)
                for h in two:
                    pe_after(v, h, r, "ka")
                    for b in two:
                        for q, m in ((0, "incl"), (1, "strict")):
                            last = v.tensor_tensor(KA[h][:, 2 * b:2 * b + 2, q, :], own[h][2 + b][:, :].rearrange("p (a b c) -> p a b c", a=2, b=2)[:, :, q, :],
                                                   bc(sh.const(m), 2), ALU.mult)
                    last.then_inc(dve_step[h], 1)
                for h in two:
                    pe_after(v, h, r, "rr")
                    if r:
                        v.wait_ge(carry_done, r)
                    v.tensor_tensor(RR[half(h), :], own[h][3][half(h), :], sh.pT[half(h), R0 + r, :], ALU.add).then_inc(dve_step[h], 1)
                for h in two:
                    pe_after(v, h, r, "m0")
                    for b in two:
                        last = v.tensor_tensor(M0[half(h), b::2, :], own[h][2 * b][half(h), 0:NCH // 2 * C].rearrange("p (a b) -> p a b", b=C),
                                               bc(sh.const("ident")[half(h), half(h)], NCH // 2), ALU.add)
                    last.then_inc(dve_step[h], 1)
                for h in two:
                    pe_after(v, h, r, "n0")
                    for b in two:
                        last = v.tensor_tensor(N0[half(h), b::2, :], own[h][1 + 2 * b][half(h), 0:NCH // 2 * C].rearrange("p (a b) -> p a b", b=C),
                                               sh.w_end[half(h), r, b::2].rearrange("p (a b) -> p a b", b=1).broadcast_to([C, NCH // 2, C]), ALU.mult)
                    last.then_inc(dve_step[h], 1)
                dve_after(v, 0, r, "n0")
                dve_after(v, 1, r, "n0")
                v.memset(ST[:, 0, :], 0.0).then_inc(state_ready, 1)
                v.tensor_copy(ST[:, 1, :], N0[:, 0, :]).then_inc(state_ready, 1)
                for n in range(1, NCH - 1):
                    v.wait_ge(state_done, r * (NCH - 2) + n)
                    v.scalar_tensor_tensor(ST[:, n + 1, :], bank[2][:, (n % 2) * C:(n % 2) * C + C], sh.w_end[:, r, n:n + 1], N0[:, n, :],
                                           ALU.mult, ALU.add).then_inc(state_ready, 1)
                v.wait_ge(carry_done, r + 1)
                act_after(v, 0, r, "oo")
                act_after(v, 1, r, "oo")
                for h in two:
                    cat = sh.cat[:, :, r * P + h * C:r * P + (h + 1) * C]
                    last = v.tensor_tensor(cat, cat, own[h][3][:, 0:NT * C].rearrange("p (a b) -> p a b", b=C), ALU.add)
                last.then_inc(carry_added, 1)
            v.wait_ge(carry_added, NPAIR)
            v.wait_ge(sw_in, 48)
            wide = lambda ap: ap.rearrange("p (a b) -> p a b", b=1).broadcast_to([P, HEADS, C])
            heads = lambda ap: ap.rearrange("p (a b) -> p a b", b=C)
            steps = 0
            for i in range(NT):
                o = sh.cat[:, i, 0:D_GROUP]
                v.tensor_reduce(gn[:, i, 0, :], heads(o), AX.X, ALU.add).then_inc(gn_step, 1)
                steps += 1
                v.wait_ge(gn_step, steps)
                v.tensor_scalar(gn[:, i, 3, :], gn[:, i, 0, :], 1.0 / C, None, ALU.mult).then_inc(gn_step, 1)
                steps += 1
                v.wait_ge(gn_step, steps)
                if i >= 2:
                    v.wait_ge(gate_free, i - 1)
                v.tensor_tensor(heads(dev(i)), heads(o), wide(gn[:, i, 3, :]), ALU.subtract).then_inc(gn_dev, 1)
                v.wait_ge(gn_sq, i + 1)
                v.tensor_reduce(gn[:, i, 1, :], heads(sqd(i)), AX.X, ALU.add).then_inc(gn_var, 1)
                v.wait_ge(gn_root, i + 1)
                v.reciprocal(gn[:, i, 3, :], gn[:, i, 2, :]).then_inc(gn_step, 1)
                steps += 1
                v.wait_ge(gn_step, steps)
                for a, b, op in ((heads(dev(i)), wide(gn[:, i, 3, :]), ALU.mult), (dev(i), lnb[:, 0, :], ALU.mult), (dev(i), lnb[:, 1, :], ALU.add)):
                    v.tensor_tensor(a, a, b, op).then_inc(gn_step, 1)
                    steps += 1
                    v.wait_ge(gn_step, steps)
                v.tensor_tensor(heads(sqd(i)), heads(sh.v_tm[:, i, :]), wide(sh.bonus[:, i, :]), ALU.mult).then_inc(gn_step, 1)
                steps += 1
                v.wait_ge(gn_step, steps)
                v.tensor_tensor(dev(i), dev(i), sqd(i), ALU.add).then_inc(gn_step, 1)
                steps += 1
                v.wait_ge(gn_step, steps)
                v.wait_ge(gate_done, i + 1)
                v.tensor_tensor(o, dev(i), bank[i % 2][:, :], ALU.mult).then_inc(gate_free, 1)


def route(nc, io, sh):
    NR = NT * TOP_E
    with ExitStack() as ctx:
        e = ctx.enter_context
        wout = e(nc.sbuf_tensor("w_out_sb", [P, KC, D], F32))
        catT = e(nc.sbuf_tensor("catT", [P, KC, S], F32))
        u2T = e(nc.sbuf_tensor("u2T", [P, KC, S], F32))
        ln = e(nc.sbuf_tensor("ln1_rows", [P, 2, D], F32))
        wr = e(nc.sbuf_tensor("w_router_sb", [P, KC, N_EXP], F32))
        br = e(nc.sbuf_tensor("b_router_sb", [P, N_EXP], F32))
        mixg = e(nc.sbuf_tensor("mix_gated", [P, D], F32))
        u2 = e(nc.sbuf_tensor("u2", [P, 2, D], F32))
        st = e(nc.sbuf_tensor("ln1_stats", [P, NT, 16], F32))
        lg = e(nc.sbuf_tensor("router_logits", [P, NT, N_EXP], F32))
        m8 = e(nc.sbuf_tensor("top8", [P, NT, 8], F32))
        i8 = e(nc.sbuf_tensor("top8_at", [P, NT, 8], mybir.dt.uint32))
        idx = e(nc.sbuf_tensor("top_expert", [P, NT, 8], F32))
        sm = e(nc.sbuf_tensor("gate_stats", [P, NT, 4], F32))
        hot = e(nc.sbuf_tensor("one_hot", [P, TOP_E, NT, N_EXP], F32))
        chosen = e(nc.sbuf_tensor("chosen", [P, NT, N_EXP], F32))
        tmp = e(nc.sbuf_tensor("place_tmp", [P, 8, NT, N_EXP], F32))
        row = e(nc.sbuf_tensor("expert_rows", [P, 8, N_EXP], F32))
        ohx = e(nc.sbuf_tensor("extra_hot", [P, 2, EXTRA, N_EXP], F32))
        xf = e(nc.sbuf_tensor("extra_f", [P, EXTRA + 1], F32))
        slotk = e(nc.sbuf_tensor("slot_of", [P, NT, TOP_E], F32))
        blkk = e(nc.sbuf_tensor("block_of", [P, NT, TOP_E], F32))
        rowf = e(nc.sbuf_tensor("row_of", [P, NT, TOP_E], F32))
        Qh = e(nc.sbuf_tensor("slot_hot", [P, 4, P], F32))
        Rh = e(nc.sbuf_tensor("block_hot", [P, 4, BLOCKS], F32))
        bank = psum_banks(nc, e, "route")

        sem = sh.sem
        rw_in, cat_turned, catT_ready, mix_done = sem("route_w_in"), sem("cat_turned"), sem("catT_ready"), sem("mix_done")
        ln_step, gated, x1_ready, u2_ready, u2_turned, u2T_ready, u2_stored = (sem("ln1_step"), sem("gated"), sem("x1_ready"), sem("u2_ready"),
                                                                              sem("u2_turned"), sem("u2T_ready"), [sem("u2_stored0"), sem("u2_stored1")])
        var_ready, root_ready, logits_done, rt_step, chosen_ready, rank_done = (sem("ln1_var"), sem("ln1_root"), sem("logits_done"), sem("rt_step"),
                                                                              sem("chosen_ready"), sem("rank_done"))
        nmax_ready, exp_ready, hot_ready, ids_done = sem("gate_nmax"), sem("gate_exp"), sem("hot_ready"), sem("ids_done")
        block = e(nc.Block())

        @block.sync
        def _(sp):
            sp.dma_start(wout[:, :, :], io["w_out"][0].rearrange("(c p) n -> p c n", p=P)).then_inc(rw_in, 16)
            sp.dma_start(ln[:, 0, :], io["ln1_g"].broadcast_to([P, D])).then_inc(rw_in, 16)
            sp.dma_start(ln[:, 1, :], io["ln1_b"].broadcast_to([P, D])).then_inc(rw_in, 16)
            sp.dma_start(wr[:, :, :], io["w_router"][0].rearrange("(c p) n -> p c n", p=P)).then_inc(rw_in, 16)
            sp.dma_start(br[:, :], io["b_router"].broadcast_to([P, N_EXP])).then_inc(rw_in, 16)
            for i in range(NT):
                sp.wait_ge(u2_ready, i + 1)
                sp.dma_start(sh.u2_dram[i * P:(i + 1) * P, :], u2[:, i % 2, :]).then_inc(u2_stored[i % 2], 16)
            for k in range(2):
                sp.wait_ge(u2_stored[k], 16 * NT // 2)

        @block.tensor
        def _(pe):
            ident = sh.const("ident")
            for j in range(KC):
                if j >= 2:
                    pe.wait_ge(catT_ready, j - 1)
                for i in range(NT):
                    last = pe.transpose(bank[j % 2][:, i * P:(i + 1) * P], sh.cat[:, i, j * P:(j + 1) * P], ident)
                last.then_inc(cat_turned, 1)
            pe.wait_ge(rw_in, 80)
            pe.wait_ge(catT_ready, KC)

            def turn(i):
                pe.wait_ge(u2_ready, i + 1)
                if i:
                    pe.wait_ge(u2T_ready, 2 * i)
                for j in range(KC):
                    last = pe.transpose(bank[6 + j // 4][:, (j % 4) * P:(j % 4 + 1) * P], u2[:, i % 2, j * P:(j + 1) * P], ident)
                last.then_inc(u2_turned, 1)

            for i in range(NT):
                if i >= 2:
                    pe.wait_ge(gated, 2 * (i - 1))
                for q in range(2):
                    for j in range(KC):
                        last = pe.matmul(bank[2 + 2 * (i % 2) + q][:, :], catT[:, j, i * P:(i + 1) * P], wout[:, j, q * 512:(q + 1) * 512],
                                         start=(j == 0), stop=(j == KC - 1))
                    last.then_inc(mix_done, 1)
                if i:
                    turn(i - 1)
            turn(NT - 1)
            for i in range(NT):
                pe.wait_ge(u2T_ready, 2 * (i + 1))
                for j in range(KC):
                    last = pe.matmul(bank[0][:, i * N_EXP:(i + 1) * N_EXP], u2T[:, j, i * P:(i + 1) * P], wr[:, j, :], start=(j == 0), stop=(j == KC - 1))
            last.then_inc(logits_done, 1)
            pe.wait_ge(chosen_ready, 1)
            for i in range(NT):
                for k in range(i):
                    pe.matmul(bank[1][:, i * N_EXP:(i + 1) * N_EXP], sh.const("ones"), chosen[:, k, :], start=(k == 0), stop=False)
                pe.matmul(bank[1][:, i * N_EXP:(i + 1) * N_EXP], sh.const("before"), chosen[:, i, :], start=(i == 0), stop=True)
            for k in range(NT):
                last = pe.matmul(bank[1][:, NT * N_EXP:(NT + 1) * N_EXP], sh.const("ones"), chosen[:, k, :], start=(k == 0), stop=(k == NT - 1))
            last.then_inc(rank_done, 1)
            for n in range(NR):
                pe.wait_ge(hot_ready, n + 1)
                pe.matmul(bank[2][:, 0:BLOCKS], Qh[:, n % 4, :], Rh[:, n % 4, :], start=(n == 0), stop=(n == NR - 1)).then_inc(ids_done, 1)

        @block.scalar
        def _(act):
            for j in range(KC):
                act.wait_ge(cat_turned, j + 1)
                act.copy(catT[:, j, :], bank[j % 2][:, :]).then_inc(catT_ready, 1)
            for i in range(NT):
                act.wait_ge(var_ready, i + 1)
                act.activation(st[:, i, 14:15], st[:, i, 13:14], ACT.Sqrt, bias=sh.const("eps")[:, 1:2]).then_inc(root_ready, 1)
                act.wait_ge(u2_turned, i + 1)
                for q in range(2):
                    act.copy(u2T[:, 4 * q:4 * q + 4, i * P:(i + 1) * P], bank[6 + q][:, :].rearrange("p (a b) -> p a b", b=P)).then_inc(u2T_ready, 1)
            act.wait_ge(nmax_ready, 1)
            for i in range(NT):
                last = act.activation(sh.gate[:, i, :], m8[:, i, 0:TOP_E], ACT.Exp, bias=sm[:, i, 0:1], accum_out=sm[:, i, 1:2])
            last.then_inc(exp_ready, 1)

        @block.vector
        def _(v):
            count = {"ln": 0, "rt": 0}

            def ln1(ins):
                ins.then_inc(ln_step, 1)
                count["ln"] += 1
                v.wait_ge(ln_step, count["ln"])

            gate1, shift2, scale2, gate2 = (sh.modb[:, k * D:(k + 1) * D] for k in range(4))
            for m in (gate1, scale2, gate2):
                last = v.tensor_scalar(m, m, 1.0, None, ALU.add)
            ln1(last)
            v.wait_ge(rw_in, 80)
            for i in range(NT):
                x = sh.x_tm[:, i, :]
                for q in range(2):
                    v.wait_ge(mix_done, 2 * i + q + 1)
                    v.tensor_tensor(mixg[:, q * 512:(q + 1) * 512], bank[2 + 2 * (i % 2) + q][:, :], gate1[:, q * 512:(q + 1) * 512], ALU.mult).then_inc(gated, 1)
                v.wait_ge(gated, 2 * i + 2)
                ln1(v.scalar_tensor_tensor(x, x, ALPHA, mixg[:, :], ALU.mult, ALU.add))
                v.bn_stats(st[:, i, 0:6], x[:, 0:512])
                ln1(v.bn_stats(st[:, i, 6:12], x[:, 512:D]))
                v.bn_aggr(st[:, i, 12:14], st[:, i, 0:12].rearrange("p (a b) -> p a b", b=6)).then_inc(var_ready, 1)
                v.wait_ge(root_ready, i + 1)
                ln1(v.reciprocal(st[:, i, 15:16], st[:, i, 14:15]))
                ln1(v.tensor_scalar(x, x, st[:, i, 12:13], st[:, i, 15:16], ALU.subtract, ALU.mult))
                ln1(v.tensor_tensor(x, x, ln[:, 0, :], ALU.mult))
                ln1(v.tensor_tensor(x, x, ln[:, 1, :], ALU.add))
                if i >= 2:
                    v.wait_ge(u2_stored[i % 2], 16 * (i // 2))
                    v.wait_ge(u2_turned, i - 1)
                ln1(v.tensor_tensor(u2[:, i % 2, :], x, scale2, ALU.mult))
                v.tensor_tensor(u2[:, i % 2, :], u2[:, i % 2, :], shift2, ALU.add).then_inc(u2_ready, 1)

            def rt(ins):
                ins.then_inc(rt_step, 1)
                count["rt"] += 1
                v.wait_ge(rt_step, count["rt"])

            def along(ap, n, at):
                if at == 1:
                    return ap.rearrange("p (a m) -> p a m", a=1).broadcast_to([P, n, ap.shape[1]])
                return ap.rearrange("p (m a) -> p m a", a=1).broadcast_to([P, ap.shape[1], n])

            v.wait_ge(logits_done, 1)
            rt(v.tensor_tensor(lg[:, :, :], bank[0][:, 0:NT * N_EXP].rearrange("p (a b) -> p a b", b=N_EXP), along(br[:, :], NT, 1), ALU.add))
            for i in range(NT):
                rt(v.max(m8[:, i, :], lg[:, i, :]))
                rt(v.max_index(i8[:, i, :], m8[:, i, :], lg[:, i, :]))
            v.tensor_scalar(sm[:, :, 0:1], m8[:, :, 0:1], -1.0, None, ALU.mult).then_inc(nmax_ready, 1)
            rt(v.tensor_copy(idx[:, :, :], i8[:, :, :]))
            for k in range(TOP_E):
                last = v.tensor_tensor(hot[:, k, :, :], along(sh.const("expert"), NT, 1), along(idx[:, :, k], N_EXP, 2), ALU.is_equal)
            rt(last)
            rt(v.tensor_tensor(tmp[:, 0, :, :], hot[:, 0, :, :], hot[:, 1, :, :], ALU.add))
            rt(v.tensor_tensor(tmp[:, 1, :, :], hot[:, 2, :, :], hot[:, 3, :, :], ALU.add))
            v.tensor_tensor(chosen[:, :, :], tmp[:, 0, :, :], tmp[:, 1, :, :], ALU.add).then_inc(chosen_ready, 1)
            v.wait_ge(exp_ready, 1)
            rt(v.reciprocal(sm[:, :, 2:3], sm[:, :, 1:2]))
            rt(v.tensor_tensor(sh.gate[:, :, :], sh.gate[:, :, :], sm[:, :, 2:3].broadcast_to([P, NT, TOP_E]), ALU.mult))
            v.wait_ge(rank_done, 1)
            total, extra, upto, first, shift = (row[:, k, :] for k in range(5))
            rt(v.tensor_copy(total, bank[1][:, NT * N_EXP:(NT + 1) * N_EXP]))
            rt(v.tensor_scalar(extra, total, float(P) + 0.5, None, ALU.is_gt))
            for m in range(2, NT):
                rt(v.scalar_tensor_tensor(extra, total, float(m * P) + 0.5, extra, ALU.is_gt, ALU.add))
            rt(v.tensor_tensor_scan(upto, sh.const("ones")[:, 0:N_EXP], extra, 0.0, ALU.mult, ALU.add))
            rt(v.tensor_tensor(first, upto, extra, ALU.subtract))
            rt(v.scalar_tensor_tensor(shift, first, float(N_EXP), sh.const("expert"), ALU.add, ALU.subtract))
            pos, past, deep, slot, blk = (tmp[:, k, :, :] for k in range(5))
            rt(v.tensor_copy(pos, bank[1][:, 0:NT * N_EXP].rearrange("p (a b) -> p a b", b=N_EXP)))
            rt(v.tensor_scalar(past, pos, float(P) - 0.5, None, ALU.is_gt))
            rt(v.tensor_scalar(deep, pos, float(2 * P) - 0.5, None, ALU.is_gt))
            for m in range(3, NT):
                rt(v.scalar_tensor_tensor(deep, pos, float(m * P) - 0.5, deep, ALU.is_gt, ALU.add))
            rt(v.tensor_tensor(blk, past, along(shift, NT, 1), ALU.mult))
            rt(v.tensor_tensor(blk, blk, along(sh.const("expert"), NT, 1), ALU.add))
            rt(v.tensor_tensor(blk, blk, deep, ALU.add))
            rt(v.tensor_tensor(past, past, deep, ALU.add))
            rt(v.scalar_tensor_tensor(slot, past, -float(P), pos, ALU.mult, ALU.add))
            for k in range(TOP_E):
                rt(v.tensor_tensor(tmp[:, 5, :, :], hot[:, k, :, :], slot, ALU.mult))
                v.tensor_reduce(slotk[:, :, k], tmp[:, 5, :, :], AX.X, ALU.add)
                rt(v.tensor_tensor(tmp[:, 6, :, :], hot[:, k, :, :], blk, ALU.mult))
                rt(v.tensor_reduce(blkk[:, :, k], tmp[:, 6, :, :], AX.X, ALU.add))
            rt(v.scalar_tensor_tensor(rowf[:, :, :], blkk[:, :, :], float(P), slotk[:, :, :], ALU.mult, ALU.add))
            rt(v.tensor_copy(sh.rows[:, :, :], rowf[:, :, :]))
            for n in range(NR):
                i, k = divmod(n, TOP_E)
                if n >= 4:
                    v.wait_ge(ids_done, n - 3)
                v.tensor_scalar(Qh[:, n % 4, :], sh.const("slots"), slotk[:, i, k:k + 1], None, ALU.is_equal)
                v.tensor_scalar(Rh[:, n % 4, :], sh.const("blocks"), blkk[:, i, k:k + 1], sh.const("token")[:, i:i + 1], ALU.is_equal, ALU.mult).then_inc(hot_ready, 1)
            v.wait_ge(ids_done, NR)
            rt(v.tensor_copy(sh.ids[:, :], bank[2][:, 0:BLOCKS]))
            j_of = along(sh.const("blocks")[:, 0:EXTRA], N_EXP, 2)
            rt(v.tensor_tensor(ohx[:, 0, :, :], j_of, along(first, EXTRA, 1), ALU.is_ge))
            rt(v.tensor_tensor(ohx[:, 1, :, :], j_of, along(upto, EXTRA, 1), ALU.is_lt))
            rt(v.tensor_tensor(ohx[:, 0, :, :], ohx[:, 0, :, :], ohx[:, 1, :, :], ALU.mult))
            rt(v.tensor_tensor(ohx[:, 0, :, :], ohx[:, 0, :, :], along(sh.const("expert"), EXTRA, 1), ALU.mult))
            rt(v.tensor_reduce(xf[:, 0:EXTRA], ohx[:, 0, :, :], AX.X, ALU.add))
            rt(v.tensor_copy(xf[:, EXTRA:EXTRA + 1], upto[:, N_EXP - 1:N_EXP]))
            rt(v.tensor_copy(sh.extra[:, :], xf[0:1, :]))


def experts(nc, io, sh):
    NG, ND = KC, 4
    NY = 4
    with ExitStack() as ctx:
        e = ctx.enter_context
        wg = e(nc.sbuf_tensor("w_gu_sb", [P, NG, 2 * FF], F32))
        wd = e(nc.sbuf_tensor("w_dn_sb", [P, ND, 2, D], F32))
        bias = sh.modb[0:1, 0:3 * FF]
        xg = e(nc.sbuf_tensor("x_gathered", [P, D], F32))
        xT = e(nc.sbuf_tensor("x_gathered_T", [P, KC, P], F32))
        gt = e(nc.sbuf_tensor("gate_clamped", [P, FF], F32))
        up = e(nc.sbuf_tensor("up_clamped", [P, FF], F32))
        sg = e(nc.sbuf_tensor("gate_sigmoid", [P, FF], F32))
        h = e(nc.sbuf_tensor("hidden", [P, FF], F32))
        hT = e(nc.sbuf_tensor("hidden_T", [P, KC, P], F32))
        y = e(nc.sbuf_tensor("y_block", [P, D], F32))
        idb = e(nc.sbuf_tensor("id_block", [P, 1], I32))
        fence = e(nc.sbuf_tensor("fence", [1, 4], F32))
        ps_gu = e(nc.psum_tensor("ps_gu", [P, 4, 512], F32))
        ps_y = e(nc.psum_tensor("ps_y", [P, 2, 512], F32))
        ps_t = e(nc.psum_tensor("ps_t", [P, 2, 4, P], F32))

        sem = sh.sem
        g_in = [sem(f"w_gu_in{n}") for n in range(NG)]
        d_in = [sem(f"w_dn_in{n}") for n in range(ND)]
        bias_in, fence_ready, fenced = sem("expert_bias_in"), sem("fence_ready"), sem("fenced")
        id_ready, x_in, x_turned, xT_ready = sem("id_ready"), sem("xg_in"), sem("xg_turned"), sem("xT_ready")
        g_used, bias_used, d_used, gu_done = sem("w_gu_used"), sem("bias_used"), sem("w_dn_used"), sem("gu_done")
        gt_ready, up_ready, sg_ready, gs_ready, h_ready = sem("gt_ready"), sem("up_ready"), sem("sg_ready"), sem("gs_ready"), sem("h_ready")
        h_turned, hT_ready, y_done, y_ready, y_stored = sem("h_turned"), sem("hT_ready"), sem("y_done"), sem("y_ready"), sem("y_stored")
        w_gu = io["w_gu"][0].rearrange("e (c p) n -> e p c n", p=P)
        w_dn = io["w_dn"][0].rearrange("e (c a p) n -> e p c a n", p=P, a=2)
        block = e(nc.Block())

        def main_blocks(eng, each):
            each(0, 0)
            with eng.Fori(1, N_EXP) as b:
                each(b, b)

        def extra_blocks(eng, each, expert=False):
            n = eng.value_load(sh.extra[0:1, EXTRA:EXTRA + 1], min_val=0, max_val=EXTRA)
            with eng.Fori(0, EXTRA) as j:
                with eng.If(j < n):
                    x = eng.value_load(sh.extra[0:1, bass.ds(j, 1)], min_val=0, max_val=N_EXP - 1) if expert else None
                    each(j + N_EXP, x)

        @block.sync
        def _(sp):
            def load(b, x):
                later = not isinstance(b, int) or b > 0
                for n in range(NG):
                    if later:
                        sp.wait_ge(g_used, b * NG + (n - NG + 1))
                    sp.dma_start(wg[:, n, :], w_gu[bass.ds(x, 1), :, n, :].rearrange("e p n -> (e p) n")).then_inc(g_in[n], 16)
                    if n == 0:
                        if later:
                            sp.wait_ge(bias_used, b)
                        sp.dma_start(bias[:, 0:2 * FF], io["b_gu"][0][bass.ds(x, 1), :]).then_inc(bias_in, 16)
                        sp.dma_start(bias[:, 2 * FF:3 * FF], io["b_dn"][0][bass.ds(x, 1), :]).then_inc(bias_in, 16)
                for n in range(ND):
                    if later:
                        sp.wait_ge(d_used, b * ND + (n - ND + 1))
                    sp.dma_start(wd[:, n, :, :], w_dn[bass.ds(x, 1), :, n, :, :].rearrange("e p a n -> (e p) a n")).then_inc(d_in[n], 16)

            main_blocks(sp, load)
            extra_blocks(sp, load, True)

        @block.gpsimd
        def _(pool):
            def gather(b, x):
                pool.wait_ge(id_ready, b + 1)
                if not isinstance(b, int) or b > 0:
                    pool.wait_ge(x_turned, b)
                pool.tensor_tensor(fence[0:1, 0:1], fence[0:1, 1:2], fence[0:1, 2:3], ALU.add).then_inc(fenced, 1)
                pool.indirect_dma_start(xg[:, :], None, sh.u2_dram, bass.IndirectOffsetOnAxis(ap=idb[:, 0:1], axis=0)).then_inc(x_in, 16)

            pool.memset(fence[:, :], 0.0).then_inc(fence_ready, 1)
            pool.wait_ge(fence_ready, 1)
            main_blocks(pool, gather)
            extra_blocks(pool, gather)

        @block.tensor
        def _(pe):
            ident, ones = sh.const("ident"), sh.const("ones")

            def gate_up(b):
                later = not isinstance(b, int) or b > 0
                pe.wait_ge(x_in, b * 16 + 16)
                if later:
                    pe.wait_ge(hT_ready, b * 2)
                for j in range(KC):
                    last = pe.transpose(ps_t[:, j // 4, j % 4, :], xg[:, j * P:(j + 1) * P], ident)
                last.then_inc(x_turned, 1)
                pe.wait_ge(bias_in, b * 32 + 32)
                if later:
                    pe.wait_ge(up_ready, b)
                for q in range(4):
                    pe.matmul(ps_gu[:, q, :], ones[0:1, :], bias[:, q * 512:(q + 1) * 512], start=True, stop=False)
                pe.wait_ge(xT_ready, b * 2 + 2)
                for n in range(NG):
                    pe.wait_ge(g_in[n], b * 16 + 16)
                    for q in range(4):
                        last = pe.matmul(ps_gu[:, q, :], xT[:, n, :], wg[:, n, q * 512:(q + 1) * 512], start=False, stop=(n == NG - 1))
                    last.then_inc(g_used, 1)

            def down(b):
                later = not isinstance(b, int) or b > 0
                pe.wait_ge(h_ready, b + 1)
                pe.wait_ge(xT_ready, b * 2 + 2)
                for j in range(KC):
                    last = pe.transpose(ps_t[:, j // 4, j % 4, :], h[:, j * P:(j + 1) * P], ident)
                last.then_inc(h_turned, 1)
                if later:
                    pe.wait_ge(y_ready, b)
                for q in range(2):
                    last = pe.matmul(ps_y[:, q, :], ones[0:1, :], bias[:, 2 * FF + q * 512:2 * FF + (q + 1) * 512], start=True, stop=False)
                last.then_inc(bias_used, 1)
                pe.wait_ge(hT_ready, b * 2 + 2)
                for n in range(ND):
                    pe.wait_ge(d_in[n], b * 16 + 16)
                    for a in range(2):
                        for q in range(2):
                            last = pe.matmul(ps_y[:, q, :], hT[:, 2 * n + a, :], wd[:, n, a, q * 512:(q + 1) * 512], start=False, stop=(n == ND - 1 and a == 1))
                    last.then_inc(d_used, 1)

            def both(b, x):
                gate_up(b)
                down(b)

            main_blocks(pe, both)
            extra_blocks(pe, both)

        @block.vector
        def _(v):
            def ids(b):
                if not isinstance(b, int) or b > 0:
                    v.wait_ge(x_in, b * 16)
                    v.wait_ge(fenced, b)
                v.tensor_copy(idb[:, :], sh.ids[:, bass.ds(b, 1)]).then_inc(id_ready, 1)

            def middle(b, x):
                later = not isinstance(b, int) or b > 0
                v.wait_ge(g_used, b * NG + NG)
                halves = ps_gu[:, :, :].rearrange("p q (n two) -> p q n two", two=2)
                wide = lambda t: t[:, :].rearrange("p (q n) -> p q n", q=4)
                v.tensor_scalar(wide(gt), halves[:, :, :, 0], LIMIT, None, ALU.min).then_inc(gt_ready, 1)
                if later:
                    v.wait_ge(h_ready, b)
                v.tensor_scalar(wide(up), halves[:, :, :, 1], LIMIT, -LIMIT, ALU.min, ALU.max).then_inc(up_ready, 1)
                v.wait_ge(sg_ready, b + 1)
                v.tensor_tensor(sg[:, :], gt[:, :], sg[:, :], ALU.mult).then_inc(gs_ready, 1)
                v.wait_ge(gs_ready, b + 1)
                v.wait_ge(up_ready, b + 1)
                if later:
                    v.wait_ge(h_turned, b)
                v.scalar_tensor_tensor(h[:, :], up[:, :], 1.0, sg[:, :], ALU.add, ALU.mult).then_inc(h_ready, 1)

            ids(0)
            middle(0, 0)
            with v.Fori(1, N_EXP) as b:
                ids(b)
                middle(b, b)
            n = v.value_load(sh.extra[0:1, EXTRA:EXTRA + 1], min_val=0, max_val=EXTRA)
            with v.Fori(0, EXTRA) as j:
                with v.If(j < n):
                    ids(j + N_EXP)
                    middle(j + N_EXP, None)

        @block.scalar
        def _(act):
            def copies(b, x):
                later = not isinstance(b, int) or b > 0
                act.wait_ge(x_turned, b + 1)
                for q in range(2):
                    act.copy(xT[:, 4 * q:4 * q + 4, :], ps_t[:, q, :, :]).then_inc(xT_ready, 1)
                act.wait_ge(gt_ready, b + 1)
                act.activation(sg[:, :], gt[:, :], ACT.Sigmoid, scale=SWIGLU_ALPHA).then_inc(sg_ready, 1)
                act.wait_ge(h_turned, b + 1)
                for q in range(2):
                    act.copy(hT[:, 4 * q:4 * q + 4, :], ps_t[:, q, :, :]).then_inc(hT_ready, 1)
                act.wait_ge(d_used, b * ND + ND)
                if later:
                    act.wait_ge(y_stored, b * 16)
                act.copy(y[:, :].rearrange("p (q n) -> p q n", q=2), ps_y[:, :, :]).then_inc(y_ready, 1)
                act.wait_ge(y_ready, b + 1)
                act.dma_start(sh.y_dram[bass.ds(b * P, P), :], y[:, :]).then_inc(y_stored, 16)

            main_blocks(act, copies)
            extra_blocks(act, copies)
            n = act.value_load(sh.extra[0:1, EXTRA:EXTRA + 1], min_val=0, max_val=EXTRA)
            act.wait_ge(y_stored, (n + N_EXP) * 16)
            act.copy(fence[0:1, 3:4], y[0:1, 0:1])


def finish(nc, io, sh):
    NY = 8
    with ExitStack() as ctx:
        e = ctx.enter_context
        ln = e(nc.sbuf_tensor("ln2_rows", [P, 2, D], F32))
        yk = e(nc.sbuf_tensor("y_gathered", [P, NY, D], F32))
        acc = e(nc.sbuf_tensor("ffn", [P, NT, D], F32))
        st = e(nc.sbuf_tensor("ln2_stats", [P, NT, 16], F32))
        sem = sh.sem
        l_in, y_in, y_used, step, var_ready, root_ready, o_ready, o_stored = (sem("ln2_in"), [sem(f"yk_in{n}") for n in range(NY)], sem("yk_used"), sem("ln2_step"),
                                                                             sem("ln2_var"), sem("ln2_root"), sem("out_ready"), sem("out_stored"))
        block = e(nc.Block())

        @block.sync
        def _(sp):
            sp.dma_start(ln[:, 0, :], io["ln2_g"].broadcast_to([P, D])).then_inc(l_in, 16)
            sp.dma_start(ln[:, 1, :], io["ln2_b"].broadcast_to([P, D])).then_inc(l_in, 16)
            for i in range(NT):
                sp.wait_ge(o_ready, i + 1)
                sp.dma_start(io["out"][0, i * P:(i + 1) * P, :], acc[:, i, :]).then_inc(o_stored, 16)
            sp.wait_ge(o_stored, 16 * NT)

        @block.gpsimd
        def _(pool):
            for n in range(NT * TOP_E):
                i, k = divmod(n, TOP_E)
                if n >= NY:
                    pool.wait_ge(y_used, n - NY + 1)
                pool.indirect_dma_start(yk[:, n % NY, :], None, sh.y_dram, bass.IndirectOffsetOnAxis(ap=sh.rows[:, i, k:k + 1], axis=0)).then_inc(y_in[n % NY], 16)

        @block.scalar
        def _(act):
            for i in range(NT):
                act.wait_ge(var_ready, i + 1)
                act.activation(st[:, i, 14:15], st[:, i, 13:14], ACT.Sqrt, bias=sh.const("eps")[:, 1:2]).then_inc(root_ready, 1)

        @block.vector
        def _(v):
            count = [0]

            def link(ins):
                ins.then_inc(step, 1)
                count[0] += 1
                v.wait_ge(step, count[0])

            v.wait_ge(l_in, 32)
            for i in range(NT):
                a = acc[:, i, :]
                for k in range(TOP_E):
                    n = i * TOP_E + k
                    v.wait_ge(y_in[n % NY], 16 * (n // NY + 1))
                    g = sh.gate[:, i, k:k + 1]
                    if k == 0:
                        v.tensor_scalar(a, yk[:, n % NY, :], g, None, ALU.mult).then_inc(y_used, 1)
                    else:
                        v.scalar_tensor_tensor(a, yk[:, n % NY, :], g, a, ALU.mult, ALU.add).then_inc(y_used, 1)
                    v.wait_ge(y_used, n + 1)
                link(v.tensor_tensor(a, a, sh.modb[:, 3 * D:4 * D], ALU.mult))
                link(v.scalar_tensor_tensor(a, sh.x_tm[:, i, :], ALPHA, a, ALU.mult, ALU.add))
                v.bn_stats(st[:, i, 0:6], a[:, 0:512])
                link(v.bn_stats(st[:, i, 6:12], a[:, 512:D]))
                v.bn_aggr(st[:, i, 12:14], st[:, i, 0:12].rearrange("p (a b) -> p a b", b=6)).then_inc(var_ready, 1)
                v.wait_ge(root_ready, i + 1)
                link(v.reciprocal(st[:, i, 15:16], st[:, i, 14:15]))
                link(v.tensor_scalar(a, a, st[:, i, 12:13], st[:, i, 15:16], ALU.subtract, ALU.mult))
                link(v.tensor_tensor(a, a, ln[:, 0, :], ALU.mult))
                v.tensor_tensor(a, a, ln[:, 1, :], ALU.add).then_inc(o_ready, 1)


INPUTS = ["x", "c", "w_ada", "b_ada", "w_in", "shift_mu", "rwkv_w0", "rwkv_w2", "rwkv_a0", "rwkv_a2", "rwkv_g2",
          "rwkv_k_k", "rwkv_k_a", "rwkv_r_k", "rwkv_ln_w", "rwkv_ln_b", "mla_q_norm", "mla_w_q_up",
          "mla_kv_norm", "mla_w_uk", "mla_w_uv", "idx_w_q", "idx_ln_g", "idx_ln_b", "w_out", "ln1_g", "ln1_b",
          "w_router", "b_router", "w_gu", "b_gu", "w_dn", "b_dn", "ln2_g", "ln2_b"]


def build(nc, io, stages=5):
    with ExitStack() as ctx:
        e = ctx.enter_context
        sh = Shared()
        live = []

        def new_semaphore(name):
            live.append(nc.alloc_semaphore(name=name))
            return live[-1]

        def clear_semaphores():
            nc.clear_and_free_semaphores(live)
            live.clear()
            nc.all_engine_barrier()

        sh.sem = new_semaphore
        sh.cst = e(nc.sbuf_tensor("consts_sb", [P, N_CONST], F32))
        sh.cols = e(nc.sbuf_tensor("cols", [P, N_VEC], F32))
        sh.x_tm = e(nc.sbuf_tensor("x_tm", [P, NT, D], F32))
        sh.modb = e(nc.sbuf_tensor("modb", [P, 4 * D], F32))
        sh.const = lambda n: sh.cst[:, CONST[n][0]:CONST[n][0] + CONST[n][1]]
        sh.col = lambda n, i: sh.cols[:, VEC[n][0] + i:VEC[n][0] + i + 1]
        sh.gate = e(nc.sbuf_tensor("gate", [P, NT, TOP_E], F32))
        sh.rows = e(nc.sbuf_tensor("rows", [P, NT, TOP_E], I32))
        sh.ids = e(nc.sbuf_tensor("ids", [P, BLOCKS], I32))
        sh.extra = e(nc.sbuf_tensor("extra", [1, EXTRA + 1], I32))
        sh.u2_dram = nc.dram_tensor("u2_dram", (S, D), F32, kind="Internal").ap()
        sh.y_dram = nc.dram_tensor("y_dram", (BLOCKS * P, D), F32, kind="Internal").ap()
        mixing = ctx.enter_context(ExitStack())
        sh.cat = mixing.enter_context(nc.sbuf_tensor("cat_tm", [P, NT, D], F32))
        with ExitStack() as front:
            sh.pT = front.enter_context(nc.sbuf_tensor("pT", [P, COL_TILES, S], F32))
            project(nc, io, sh)
            if stages >= 2:
                attend(nc, io, sh)
            if stages >= 3:
                sh.b_hat = front.enter_context(nc.sbuf_tensor("b_hat", [P, NPAIR, S], F32))
                sh.v_tm = front.enter_context(nc.sbuf_tensor("v_tm", [P, NT, D_GROUP], F32))
                sh.gate_sig = front.enter_context(nc.sbuf_tensor("gate_sig", [P, S], F32))
                sh.w_end = front.enter_context(nc.sbuf_tensor("w_end", [P, NPAIR, NCH], F32))
                sh.bonus = front.enter_context(nc.sbuf_tensor("bonus", [P, NT, HEADS], F32))
                prepare(nc, io, sh)
                scan(nc, io, sh)
                clear_semaphores()
        if stages >= 4:
            route(nc, io, sh)
        mixing.close()
        if stages >= 5:
            experts(nc, io, sh)
            finish(nc, io, sh)


def kernel(**inputs):
    import concourse.bacc as bacc
    from concourse.bass_utils import run_bass_kernel_spmd

    nc = bacc.Bacc("TRN2", target_bir_lowering=False, num_devices=1)
    arrays, io = {}, {}
    for name in INPUTS:
        a = np.ascontiguousarray(inputs[name])
        arrays[f"{name}_dram"] = a
        io[name] = nc.dram_tensor(f"{name}_dram", a.shape, mybir.dt.from_np(a.dtype), kind="ExternalInput").ap()
    arrays["consts_dram"] = CONST_ARRAY
    io["consts"] = nc.dram_tensor("consts_dram", CONST_ARRAY.shape, F32, kind="ExternalInput").ap()
    io["out"] = nc.dram_tensor("out_dram", (1, S, D), F32, kind="ExternalOutput").ap()
    build(nc, io)
    r = run_bass_kernel_spmd(nc, [arrays], core_ids=[0])
    return r.results[0]["out_dram"]
```

```python
from contextlib import ExitStack

import numpy as np

import concourse.bass as bass
from concourse import mybir

F32 = mybir.dt.float32
F32R = mybir.dt.float32r
I32 = mybir.dt.int32
BF16 = mybir.dt.bfloat16
ALU = mybir.AluOpType
ACT = mybir.ActivationFunctionType
AX = mybir.AxisListType

P = 128
D = 1024
S = 512
NT = S // P
KC = D // P
C = 64
NCH = S // C
HEADS = 8
D_GROUP = HEADS * C
NPAIR = D_GROUP // P
Q_LORA, KV_LORA, IDX_DIM = 256, 128, 64
N_SHIFT = 3 * D_GROUP + 64 + 64 + 128
N_IN = N_SHIFT + Q_LORA + KV_LORA + IDX_DIM + HEADS
SHIFT_TILES = N_SHIFT // P
COL_TILES = -(-N_IN // P)
TOPK = min(256, S // 4)
N_EXP = 32
TOP_E = 4
FF = 1024
EXTRA = (S * TOP_E // (S - P + 1)) * (S // P - 1)
BLOCKS = N_EXP + EXTRA + 1
NEG = -1e30
TAKEN = -3e38
DECAY = float(np.exp(-0.5))
LEVELS = (4, 8, 16, 32, 64)
GN_EPS = 64e-5
LIMIT, SWIGLU_ALPHA = 7.0, 1.702
ALPHA = 2.0 ** 0.25
SLOPES = [2.0 ** (-8.0 * (h + 1) / HEADS) for h in range(HEADS)]

VEC = {}
_at = 0
for _n, _k in (("c", 8), ("shift_mu", 14), ("rwkv_w0", 4), ("rwkv_a0", 4), ("rwkv_k_k", 4),
               ("rwkv_k_a", 4), ("rwkv_r_k", 4), ("mla_q_norm", 2), ("mla_kv_norm", 1),
               ("idx_ln_g", 1), ("idx_ln_b", 1)):
    VEC[_n] = (_at, _k)
    _at += _k
N_VEC = _at

CONST = {}


def _constants():
    p = np.arange(P)[:, None]
    j = np.arange(P)[None, :]
    half = p // C == j // C
    s512 = np.arange(S)[None, :]
    parts = [("ident", p == j), ("strict", half & (p < j)), ("incl", half & (p <= j)),
             ("low2", (p == j + 1) & (j % 2 == 0)), ("up2", (j == p + 1) & (p % 2 == 0))]
    for n in LEVELS:
        parts.append((f"lev{n}", (p // n == j // n) & (p // (n // 2) != j // (n // 2)) & (p < j)))
    parts += [("half", half), ("ones", np.ones((P, P))), ("before", p < j),
              ("slots", np.broadcast_to(j, (P, P))),
              ("causal", np.where(j <= p, 0.0, NEG)),
              ("dist", np.broadcast_to(s512, (P, S)) - p),
              ("keep", np.broadcast_to(s512 % C != 0, (P, S))),
              ("heads", p // C == np.arange(2)[None, :]),
              ("blocks", np.broadcast_to(np.arange(BLOCKS)[None, :], (P, BLOCKS))),
             ("token", p + 0 * np.arange(NT)[None, :] + P * np.arange(NT)[None, :]),
             ("expert", np.broadcast_to(np.arange(N_EXP)[None, :], (P, N_EXP))),
             ("picks", p % N_EXP == np.arange(N_EXP)[None, :]),
             ("eps", np.broadcast_to(np.array([[1e-6, 1e-5, GN_EPS]]), (P, 3)))]
    at = 0
    for name, a in parts:
        CONST[name] = (at, a.shape[1])
        at += a.shape[1]
    return np.concatenate([np.asarray(a, np.float32) for _, a in parts], 1)


CONST_ARRAY = _constants()
N_CONST = CONST_ARRAY.shape[1]


class Shared:
    pass


def psum_banks(nc, e, tag):
    return [e(nc.psum_tensor(f"{tag}_bank{i}", [P, 512], F32)) for i in range(8)]


def project(nc, io, sh):
    RING = 4
    HALF = 1024
    W_GROUPS = [(0, 512), (512, 512), (1024, 512), (1536, 512), (2048, N_IN - 2048)]
    WBUF = 3
    with ExitStack() as ctx:
        e = ctx.enter_context
        uT = e(nc.sbuf_tensor("uT", [P, KC, S], F32))
        win = e(nc.sbuf_tensor("w_in_sb", [P, WBUF, KC, 512], F32))
        ada = e(nc.sbuf_tensor("w_ada_sb", [P, RING, HALF], F32))
        rows = e(nc.sbuf_tensor("vec_rows", [N_VEC, P], F32))
        c_act = e(nc.sbuf_tensor("c_act", [P, KC], F32))
        sig_c = e(nc.sbuf_tensor("sig_c", [P, KC], F32))
        mod1 = e(nc.sbuf_tensor("mod1", [P, 2 * KC], F32))
        praw = e(nc.sbuf_tensor("p_raw", [P, 2, S + 1], F32))
        pdif = e(nc.sbuf_tensor("p_dif", [P, 2, S], F32))
        bank = psum_banks(nc, e, "project")
        ps_vec, ps_mod = bank[0], bank[1]
        ps_x, ps_p = bank[2:4], bank[4:8]
        acc0 = sh.pT[:, 0:4, :].rearrange("p a b -> p (a b)")
        accs = [acc0, sh.modb[:, 0:2048], sh.modb[:, 2048:4096]]
        cst, cols = sh.cst, sh.cols

        sem = sh.sem
        consts_in, vec_in, x_in, bias_in = sem("consts_in"), sem("vec_in"), sem("x_in"), sem("bias_in")
        ada_in = [sem(f"ada_in{i}") for i in range(RING)]
        win_in = [sem(f"win_in{i}") for i in range(WBUF)]
        acc_zero, ada_used, acc_done = sem("acc_zero"), sem("ada_used"), sem("acc_done")
        vec_turned, cols_ready, sig_ready, c_ready = sem("vec_turned"), sem("cols_ready"), sem("sig_ready"), sem("c_ready")
        x_turned, uT_ready, mod1_summed, mod1_ready = sem("x_turned"), sem("uT_ready"), sem("mod1_summed"), sem("mod1_ready")
        p_done, p_copied, p_shifted, p_diff = sem("p_done"), sem("p_copied"), sem("p_shifted"), sem("p_diff")
        mod_summed, mod_copied, edge_zero = sem("mod_summed"), sem("mod_copied"), sem("edge_zero")

        w_ada = io["w_ada"][0].rearrange("(c p) n -> p c n", p=P)
        w_in = io["w_in"][0].rearrange("(c p) n -> p c n", p=P)
        N_G = KC * 2
        block = e(nc.Block())

        @block.sync
        def _(sp):
            sp.dma_start(cst[:, :], io["consts"]).then_inc(consts_in, 16)
            for name, (r, k) in VEC.items():
                src = io[name]
                if name == "rwkv_r_k":
                    sp.dma_start(rows[r:r + k, :], src.rearrange("o (r a) d -> (o r) (a d)", a=2)).then_inc(vec_in, 16)
                    continue
                if k * P > src.shape[1]:
                    sp.dma_start(rows[r:r + 1, 0:C], src).then_inc(vec_in, 16)
                    sp.dma_start(rows[r:r + 1, C:P], src).then_inc(vec_in, 16)
                    continue
                sp.dma_start(rows[r:r + k, :], src.rearrange("o (r d) -> (o r) d", d=P)).then_inc(vec_in, 16)
            sp.wait_ge(acc_zero, 1)
            sp.dma_start(acc0[0:1, :], io["b_ada"][:, 0:2048]).then_inc(bias_in, 16)

            def ada_piece(n):
                g, k = divmod(n, N_G)
                if n >= RING:
                    sp.wait_ge(ada_used, n - RING + 1)
                sp.dma_start(ada[:, n % RING, :],
                             w_ada[:, k // 2, g * 2048 + (k % 2) * HALF:g * 2048 + (k % 2 + 1) * HALF]).then_inc(ada_in[n % RING], 16)

            def win_group(g):
                at, n = W_GROUPS[g]
                if g >= WBUF:
                    sp.wait_ge(p_done, 4 * (g - WBUF + 1))
                sp.dma_start(win[:, g % WBUF, :, 0:n], w_in[:, :, at:at + n]).then_inc(win_in[g % WBUF], 16)

            for n in range(N_G):
                ada_piece(n)
                if n % 4 == 3:
                    i = n // 4
                    sp.dma_start(sh.x_tm[:, i, :], io["x"][0, i * P:(i + 1) * P, :]).then_inc(x_in, 16)
            for g in range(WBUF):
                win_group(g)
            sp.wait_ge(acc_zero, 3)
            for g in (1, 2):
                sp.dma_start(accs[g][0:1, :], io["b_ada"][:, g * 2048:(g + 1) * 2048]).then_inc(bias_in, 16)
            for n in range(N_G, 2 * N_G):
                ada_piece(n)
            win_group(3)
            for n in range(2 * N_G, 3 * N_G):
                ada_piece(n)
            win_group(4)

        @block.tensor
        def _(pe):
            ident = sh.const("ident")
            pe.wait_ge(consts_in, 16)
            pe.wait_ge(vec_in, 16 * (len(VEC) + 2))
            pe.transpose(ps_vec[:, 0:N_VEC], rows[:, :], ident[0:N_VEC, 0:N_VEC]).then_inc(vec_turned, 1)
            for c in range(KC):
                if c == 0:
                    pe.wait_ge(x_in, 16 * NT)
                if c >= 2:
                    pe.wait_ge(uT_ready, c - 1)
                for i in range(NT):
                    last = pe.transpose(ps_x[c % 2][:, i * P:(i + 1) * P], sh.x_tm[:, i, c * P:(c + 1) * P], ident)
                last.then_inc(x_turned, 1)
                if c == 1:
                    pe.wait_ge(acc_done, 1)
                    for k in range(2 * KC):
                        last = pe.matmul(ps_mod[:, k:k + 1], acc0[:, k * P:(k + 1) * P], sh.const("ones")[:, 0:1], start=True, stop=True)
                    last.then_inc(mod1_summed, 1)
            pe.wait_ge(uT_ready, KC)

            def mod_rows(g):
                pe.wait_ge(acc_done, g + 1)
                for k in range(4):
                    if (g, k) != (1, 0):
                        pe.wait_ge(mod_copied, 4 * (g - 1) + k)
                    pe.matmul(ps_mod[:, :], sh.const("ones"), accs[g][:, k * 512:(k + 1) * 512],
                              start=True, stop=True).then_inc(mod_summed, 1)

            pe.wait_ge(mod1_ready, 1)
            for j in range(COL_TILES):
                g = j // 4
                m = min(P, N_IN - j * P)
                if j % 4 == 0:
                    pe.wait_ge(win_in[g % WBUF], 16 * (g // WBUF + 1))
                if j >= 4:
                    pe.wait_ge(p_copied, j - 3)
                for c in range(KC):
                    last = pe.matmul(ps_p[j % 4][0:m, :], win[:, g % WBUF, c, (j % 4) * P:(j % 4) * P + m], uT[:, c, :],
                                     start=(c == 0), stop=(c == KC - 1))
                last.then_inc(p_done, 1)
                if j == 11:
                    mod_rows(1)
            mod_rows(2)

        def copy_mod(act, g):
            for k in range(4):
                act.wait_ge(mod_summed, 4 * (g - 1) + k + 1)
                act.copy(accs[g][:, k * 512:(k + 1) * 512], ps_mod[:, :]).then_inc(mod_copied, 1)

        @block.scalar
        def _(act):
            act.wait_ge(cols_ready, 1)
            act.activation(sig_c[:, :], cols[:, 0:KC], ACT.Sigmoid).then_inc(sig_ready, 1)
            act.wait_ge(mod1_ready, 1)
            for c in range(KC):
                act.wait_ge(x_turned, c + 1)
                act.activation(uT[:, c, :], ps_x[c % 2][:, :], ACT.Identity, bias=mod1[:, c:c + 1],
                               scale=mod1[:, KC + c:KC + c + 1]).then_inc(uT_ready, 1)
            act.wait_ge(edge_zero, 1)
            for j in range(COL_TILES):
                m = min(P, N_IN - j * P)
                act.wait_ge(p_done, j + 1)
                if j < SHIFT_TILES:
                    if j >= 2:
                        act.wait_ge(p_shifted, j - 1)
                    act.copy(praw[0:m, j % 2, 1:S + 1], ps_p[j % 4][0:m, :]).then_inc(p_copied, 1)
                else:
                    act.copy(sh.pT[0:m, j, :], ps_p[j % 4][0:m, :]).then_inc(p_copied, 1)
                if j == 11:
                    copy_mod(act, 1)
            copy_mod(act, 2)

        @block.vector
        def _(v):
            v.memset(acc0, 0.0).then_inc(acc_zero, 1)
            v.wait_ge(vec_turned, 1)
            v.tensor_copy(cols[:, 0:N_VEC], ps_vec[:, 0:N_VEC]).then_inc(cols_ready, 1)
            v.wait_ge(sig_ready, 1)
            v.wait_ge(cols_ready, 1)
            v.tensor_tensor(c_act[:, :], cols[:, 0:KC], sig_c[:, :], ALU.mult).then_inc(c_ready, 1)
            v.wait_ge(c_ready, 1)

            def gather_mod(g, k):
                n = g * N_G + k
                if k == 0:
                    v.wait_ge(bias_in, 16 * (1 if g == 0 else 3))
                v.wait_ge(ada_in[n % RING], 16 * (n // RING + 1))
                if k >= 2:
                    v.wait_ge(ada_used, n - 1)
                a = accs[g][:, (k % 2) * HALF:(k % 2 + 1) * HALF]
                v.scalar_tensor_tensor(a, ada[:, n % RING, :], c_act[:, k // 2:k // 2 + 1], a, ALU.mult, ALU.add).then_inc(ada_used, 1)
                if k == N_G - 1:
                    v.wait_ge(ada_used, n + 1)
                    v.engine_nop().then_inc(acc_done, 1)

            for k in range(N_G):
                gather_mod(0, k)
            v.memset(accs[1], 0.0).then_inc(acc_zero, 1)
            v.memset(accs[2], 0.0).then_inc(acc_zero, 1)
            v.memset(praw[:, :, 0:1], 0.0).then_inc(edge_zero, 1)
            v.wait_ge(mod1_summed, 1)
            v.tensor_copy(mod1[:, 0:KC], ps_mod[:, 0:KC])
            v.tensor_scalar(mod1[:, KC:2 * KC], ps_mod[:, KC:2 * KC], 1.0, None, ALU.add).then_inc(mod1_ready, 1)

            k = 0
            for j in range(SHIFT_TILES):
                while k < 32 and k < (j + 1) * 3:
                    gather_mod(1 + k // N_G, k % N_G)
                    k += 1
                v.wait_ge(p_copied, j + 1)
                raw = praw[:, j % 2, :]
                v.tensor_tensor(pdif[:, j % 2, :], raw[:, 0:S], raw[:, 1:S + 1], ALU.subtract).then_inc(p_diff, 1)
                v.wait_ge(p_diff, j + 1)
                mu = sh.col("shift_mu", j)
                v.scalar_tensor_tensor(sh.pT[:, j, :], pdif[:, j % 2, :], mu, raw[:, 1:S + 1], ALU.mult, ALU.add).then_inc(p_shifted, 1)


def attend(nc, io, sh):
    UNITS = [(i, h) for i in range(NT) for h in range(HEADS)]
    SCALE = C ** -0.5
    with ExitStack() as ctx:
        e = ctx.enter_context
        wq = e(nc.sbuf_tensor("w_q_up_sb", [P, 2, D_GROUP], F32))
        wi = e(nc.sbuf_tensor("idx_w_q_sb", [P, 2, D_GROUP], F32))
        wuk = e(nc.sbuf_tensor("w_uk_sb", [P, NPAIR, KV_LORA], F32))
        wuv = e(nc.sbuf_tensor("w_uv_sb", [P, HEADS, C], F32))
        sq = e(nc.sbuf_tensor("squares", [P, 3, S], F32))
        root = e(nc.sbuf_tensor("roots", [P, 3, S], F32))
        q_lat = e(nc.sbuf_tensor("q_lat", [P, 2, S], F32))
        c_lat = e(nc.sbuf_tensor("c_lat", [P, S], F32))
        c_tm = e(nc.sbuf_tensor("c_tm", [P, NT, KV_LORA], F32))
        ikd = e(nc.sbuf_tensor("ik_centred", [C, 2, S], F32))
        ik = e(nc.sbuf_tensor("ik", [P, S], F32))
        iw = e(nc.sbuf_tensor("iw_tm", [P, NT, HEADS], F32))
        qT = e(nc.sbuf_tensor("qT", [P, NPAIR, S], F32))
        iqT = e(nc.sbuf_tensor("iqT", [P, NPAIR, S], F32))
        q_abs = e(nc.sbuf_tensor("q_abs", [P, HEADS, S], F32))
        relu = e(nc.sbuf_tensor("relu", [P, 2, S], F32))
        score = e(nc.sbuf_tensor("score", [P, NT, S], F32))
        bias = e(nc.sbuf_tensor("key_bias", [P, NT, S], F32))
        best = e(nc.sbuf_tensor("best8", [P, 2, 8], F32))
        logit = e(nc.sbuf_tensor("logit", [P, 2, S], F32))
        prob = e(nc.sbuf_tensor("prob", [P, 2, S], F32))
        probT = e(nc.sbuf_tensor("probT", [P, 2, S], F32))
        o_lat = e(nc.sbuf_tensor("o_lat", [P, 2, P], F32))
        stat = e(nc.sbuf_tensor("softmax_stats", [P, 4, NT * HEADS], F32))
        bank = psum_banks(nc, e, "attend")

        sem = sh.sem
        aw_in = sem("attend_w_in")
        squared, summed, rooted, rinv_ready = sem("squared"), sem("summed"), sem("rooted"), sem("rinv_ready")
        lat_ready, ik_step, ik_ready, iw_turned, iw_ready = sem("lat_ready"), sem("ik_step"), sem("ik_ready"), sem("iw_turned"), sem("iw_ready")
        q_done, q_copied, qa_done, qa_copied = sem("q_done"), sem("q_copied"), sem("qa_done"), sem("qa_copied")
        c_turned, c_copied = sem("c_turned"), sem("c_copied")
        idx_done, relu_ready, score_added = sem("idx_done"), sem("relu_ready"), sem("score_added")
        top_step, bias_ready = sem("top_step"), sem("bias_ready")
        zeros_ready, y_zeroed = sem("zeros_ready"), sem("y_zeroed")
        zeros = relu[:, :, :].rearrange("p a b -> p (a b)")
        l_done, l_ready, nmax_ready, prob_ready, prob_turned = sem("l_done"), sem("l_ready"), sem("nmax_ready"), sem("prob_ready"), sem("prob_turned")
        probT_ready, pv_done, olat_ready, o_done, o_ready, rsum_ready = sem("probT_ready"), sem("pv_done"), sem("olat_ready"), sem("o_done"), sem("o_ready"), sem("rsum_ready")
        Q0, KV0, IK0 = SHIFT_TILES, SHIFT_TILES + 2, SHIFT_TILES + 3
        half = lambda h: slice(C * (h % 2), C * (h % 2) + C)
        idx_units = [(i, h) for i in range(1, NT) for h in range(HEADS)]
        block = e(nc.Block())

        @block.sync
        def _(sp):
            sp.dma_start(wq[:, :, :], io["mla_w_q_up"][0].rearrange("(c p) n -> p c n", p=P)).then_inc(aw_in, 16)
            sp.dma_start(wi[:, :, :], io["idx_w_q"][0].rearrange("(c p) n -> p c n", p=P)).then_inc(aw_in, 16)
            sp.dma_start(wuk[:, :, :], io["mla_w_uk"][0].rearrange("(a b) d c -> (b d) a c", b=2)).then_inc(aw_in, 16)
            sp.dma_start(wuv[:, :, :], io["mla_w_uv"][0].rearrange("h c d -> c h d")).then_inc(aw_in, 16)
            sp.wait_ge(zeros_ready, 1)
            for n in range(EXTRA):
                at = (N_EXP + n) * P
                sp.dma_start(sh.y_dram[at:at + P, :], zeros[:, :]).then_inc(y_zeroed, 16)
            sp.wait_ge(y_zeroed, 16 * EXTRA)

        @block.tensor
        def _(pe):
            ident, ones = sh.const("ident"), sh.const("ones")
            pe.matmul(bank[2][0:C, :], ones[0:C, 0:C], sh.pT[0:C, IK0, :], start=True, stop=True).then_inc(summed, 1)
            pe.wait_ge(squared, 3)
            pe.matmul(bank[0][:, :], ones, sq[:, 0, :], start=True, stop=False)
            pe.matmul(bank[0][:, :], ones, sq[:, 1, :], start=False, stop=True).then_inc(summed, 1)
            pe.matmul(bank[1][:, :], ones, sq[:, 2, :], start=True, stop=True).then_inc(summed, 1)
            for i in range(NT):
                last = pe.transpose(bank[4][:, i * HEADS:(i + 1) * HEADS], sh.pT[C:C + HEADS, IK0, i * P:(i + 1) * P],
                                    ident[C:C + HEADS, C:C + HEADS])
            last.then_inc(iw_turned, 1)
            pe.wait_ge(ik_step, 2)
            pe.matmul(bank[3][0:C, :], ones[0:C, 0:C], ikd[:, 1, :], start=True, stop=True).then_inc(summed, 1)
            pe.wait_ge(aw_in, 64)
            pe.wait_ge(lat_ready, 3)
            for i in range(NT):
                last = pe.transpose(bank[5][:, i * P:(i + 1) * P], c_lat[:, i * P:(i + 1) * P], ident)
            last.then_inc(c_turned, 1)
            for n in range(2 * NPAIR):
                w = wq if n < NPAIR else wi
                b = bank[6 + n % 2]
                if n >= 2:
                    pe.wait_ge(q_copied, n - 1)
                for k in range(2):
                    last = pe.matmul(b[:, :], w[:, k, (n % NPAIR) * P:(n % NPAIR + 1) * P], q_lat[:, k, :], start=(k == 0), stop=(k == 1))
                last.then_inc(q_done, 1)
            pe.wait_ge(q_copied, 2 * NPAIR)
            pe.wait_ge(ik_ready, 2)
            for n, (i, h) in enumerate(idx_units):
                b = bank[6 + n % 2]
                if n >= 2:
                    pe.wait_ge(relu_ready, n - 1)
                k = (i + 1) * P
                pe.matmul(b[:, 0:k], iqT[half(h), h // 2, i * P:(i + 1) * P], ik[half(h), 0:k], start=True, stop=True).then_inc(idx_done, 1)
            pe.wait_ge(rooted, 3)
            for h in range(HEADS):
                b = bank[h % 2]
                if h >= 2:
                    pe.wait_ge(qa_copied, h - 1)
                pe.matmul(b[:, :], wuk[half(h), h // 2, :], qT[half(h), h // 2, :], start=True, stop=True).then_inc(qa_done, 1)
            pe.wait_ge(qa_copied, HEADS)
            pe.wait_ge(relu_ready, len(idx_units))
            pe.wait_ge(c_copied, 1)
            pe.wait_ge(iw_ready, 1)
            N = len(UNITS)
            for u in range(N + 3):
                if u < N:
                    i, h = UNITS[u]
                    if u >= 2:
                        pe.wait_ge(l_ready, u - 1)
                    k = (i + 1) * P
                    pe.matmul(bank[u % 2][:, 0:k], q_abs[:, h, i * P:(i + 1) * P], c_lat[:, 0:k], start=True, stop=True).then_inc(l_done, 1)
                if 1 <= u <= N:
                    w = u - 1
                    i, h = UNITS[w]
                    pe.wait_ge(prob_ready, w + 1)
                    if w >= 2:
                        pe.wait_ge(probT_ready, w - 1)
                    for b in range(i + 1):
                        last = pe.transpose(bank[2 + w % 2][:, b * P:(b + 1) * P], prob[:, w % 2, b * P:(b + 1) * P], ident)
                    last.then_inc(prob_turned, 1)
                if 2 <= u <= N + 1:
                    w = u - 2
                    i, h = UNITS[w]
                    pe.wait_ge(probT_ready, w + 1)
                    if w >= 2:
                        pe.wait_ge(olat_ready, w - 1)
                    for b in range(i + 1):
                        last = pe.matmul(bank[4 + w % 2][:, 0:P], c_tm[:, b, :], probT[:, w % 2, b * P:(b + 1) * P], start=(b == 0), stop=(b == i))
                    last.then_inc(pv_done, 1)
                if u >= 3:
                    w = u - 3
                    i, h = UNITS[w]
                    pe.wait_ge(olat_ready, w + 1)
                    if w >= 2:
                        pe.wait_ge(o_ready, w - 1)
                    pe.matmul(bank[6 + w % 2][:, 0:C], o_lat[:, w % 2, :], wuv[:, h, :], start=True, stop=True).then_inc(o_done, 1)

        @block.scalar
        def _(act):
            for n, t in enumerate((Q0, Q0 + 1, KV0)):
                act.activation(sq[:, n, :], sh.pT[:, t, :], ACT.Square).then_inc(squared, 1)
            eps = sh.const("eps")
            act.wait_ge(summed, 2)
            act.activation(root[:, 0, :], bank[0][:, :], ACT.Sqrt, bias=eps[:, 0:1], scale=1.0 / Q_LORA).then_inc(rooted, 1)
            act.wait_ge(summed, 3)
            act.activation(root[:, 1, :], bank[1][:, :], ACT.Sqrt, bias=eps[:, 0:1], scale=1.0 / KV_LORA).then_inc(rooted, 1)
            act.wait_ge(summed, 4)
            act.activation(root[0:C, 2, :], bank[3][0:C, :], ACT.Sqrt, bias=eps[0:C, 1:2], scale=1.0 / IDX_DIM).then_inc(rooted, 1)
            for n in range(2 * NPAIR):
                act.wait_ge(q_done, n + 1)
                dst = qT if n < NPAIR else iqT
                act.copy(dst[:, n % NPAIR, :], bank[6 + n % 2][:, :]).then_inc(q_copied, 1)
            for n, (i, h) in enumerate(idx_units):
                k = (i + 1) * P
                act.wait_ge(idx_done, n + 1)
                if n >= 2:
                    act.wait_ge(score_added, n - 1)
                if n == 0:
                    act.wait_ge(y_zeroed, 16 * EXTRA)
                act.activation(relu[:, n % 2, 0:k], bank[6 + n % 2][:, 0:k], ACT.Relu).then_inc(relu_ready, 1)
            for h in range(HEADS):
                act.wait_ge(qa_done, h + 1)
                act.mul(q_abs[:, h, :], bank[h % 2][:, :], SCALE / SLOPES[h]).then_inc(qa_copied, 1)
            N = len(UNITS)
            for u in range(N + 1):
                if u < N:
                    i, h = UNITS[u]
                    k = (i + 1) * P
                    act.wait_ge(nmax_ready, u + 1)
                    if u >= 2:
                        act.wait_ge(prob_turned, u - 1)
                    act.activation(prob[:, u % 2, 0:k], logit[:, u % 2, 0:k], ACT.Exp, bias=stat[:, 1, u:u + 1],
                                   accum_out=stat[:, 2, u:u + 1]).then_inc(prob_ready, 1)
                if u >= 1:
                    w = u - 1
                    k = (UNITS[w][0] + 1) * P
                    act.wait_ge(prob_turned, w + 1)
                    if w >= 2:
                        act.wait_ge(pv_done, w - 1)
                    act.copy(probT[:, w % 2, 0:k], bank[2 + w % 2][:, 0:k]).then_inc(probT_ready, 1)

        @block.vector
        def _(v):
            v.memset(zeros, 0.0).then_inc(zeros_ready, 1)
            v.wait_ge(summed, 1)
            v.scalar_tensor_tensor(ikd[:, 0, :], bank[2][0:C, :], -1.0 / IDX_DIM, sh.pT[0:C, IK0, :], ALU.mult, ALU.add).then_inc(ik_step, 1)
            v.wait_ge(ik_step, 1)
            v.tensor_tensor(ikd[:, 1, :], ikd[:, 0, :], ikd[:, 0, :], ALU.mult).then_inc(ik_step, 1)
            for n in range(2):
                v.wait_ge(rooted, n + 1)
                v.reciprocal(root[:, n, :], root[:, n, :]).then_inc(rinv_ready, 1)
            v.wait_ge(rinv_ready, 2)
            for n in range(2):
                v.scalar_tensor_tensor(q_lat[:, n, :], sh.pT[:, Q0 + n, :], sh.col("mla_q_norm", n), root[:, 0, :], ALU.mult, ALU.mult).then_inc(lat_ready, 1)
            v.scalar_tensor_tensor(c_lat[:, :], sh.pT[:, KV0, :], sh.col("mla_kv_norm", 0), root[:, 1, :], ALU.mult, ALU.mult).then_inc(lat_ready, 1)
            v.wait_ge(rooted, 3)
            v.reciprocal(root[0:C, 2, :], root[0:C, 2, :]).then_inc(rinv_ready, 1)
            v.wait_ge(rinv_ready, 3)
            v.tensor_tensor(ikd[:, 1, :], ikd[:, 0, :], root[0:C, 2, :], ALU.mult).then_inc(ik_step, 1)
            v.wait_ge(ik_step, 3)
            v.tensor_scalar(ik[0:C, :], ikd[:, 1, :], sh.col("idx_ln_g", 0)[0:C], sh.col("idx_ln_b", 0)[0:C], ALU.mult, ALU.add).then_inc(ik_ready, 1)
            v.wait_ge(ik_ready, 1)
            v.tensor_copy(ik[C:P, :], ik[0:C, :]).then_inc(ik_ready, 1)
            v.wait_ge(iw_turned, 1)
            v.tensor_scalar(iw[:, :, :], bank[4][:, 0:NT * HEADS].rearrange("p (a b) -> p a b", b=HEADS),
                            float(HEADS ** -0.5 * IDX_DIM ** -0.5), None, ALU.mult).then_inc(iw_ready, 1)
            v.wait_ge(c_turned, 1)
            v.tensor_copy(c_tm[:, :, :], bank[5][:, :].rearrange("p (a b) -> p a b", b=P)).then_inc(c_copied, 1)
            v.memset(score[:, :, :], 0.0).then_inc(top_step, 1)
            v.wait_ge(top_step, 1)
            for i in range(NT):
                v.tensor_copy(score[:, i, i * P:(i + 1) * P], sh.const("causal")).then_inc(top_step, 1)
            steps = 1 + NT
            v.wait_ge(top_step, steps)
            v.wait_ge(iw_ready, 1)
            for n, (i, h) in enumerate(idx_units):
                k = (i + 1) * P
                v.wait_ge(relu_ready, n + 1)
                if n:
                    v.wait_ge(score_added, n)
                v.scalar_tensor_tensor(score[:, i, 0:k], relu[:, n % 2, 0:k], iw[:, i, h:h + 1], score[:, i, 0:k], ALU.mult, ALU.add).then_inc(score_added, 1)
            v.wait_ge(score_added, len(idx_units))
            for i in range(1, NT):
                k = (i + 1) * P
                for r in range(TOPK // 8):
                    v.max(best[:, r % 2, :], score[:, i, 0:k]).then_inc(top_step, 1)
                    v.wait_ge(top_step, steps + 1)
                    v.match_replace(score[:, i, 0:k], best[:, r % 2, :], score[:, i, 0:k], TAKEN).then_inc(top_step, 1)
                    steps += 2
                    v.wait_ge(top_step, steps)
            for i in range(1, NT):
                k = (i + 1) * P
                v.tensor_scalar(score[:, i, 0:k], score[:, i, 0:k], TAKEN, NEG, ALU.is_gt, ALU.mult).then_inc(top_step, 1)
                steps += 1
            v.wait_ge(top_step, steps)
            for i in range(NT):
                k = (i + 1) * P
                v.scalar_tensor_tensor(bias[:, i, 0:k], sh.const("dist")[:, 0:k], float(-i * P), score[:, i, 0:k], ALU.add, ALU.add).then_inc(bias_ready, 1)
            v.wait_ge(bias_ready, NT)
            N = len(UNITS)
            for u in range(N + 3):
                if u < N:
                    i, h = UNITS[u]
                    k = (i + 1) * P
                    v.wait_ge(l_done, u + 1)
                    if u >= 2:
                        v.wait_ge(prob_ready, u - 1)
                    v.tensor_tensor_reduce(logit[:, u % 2, 0:k], bank[u % 2][:, 0:k], bias[:, i, 0:k], SLOPES[h], TAKEN,
                                           ALU.add, ALU.max, stat[:, 0, u:u + 1]).then_inc(l_ready, 1)
                    v.wait_ge(l_ready, u + 1)
                    v.tensor_scalar(stat[:, 1, u:u + 1], stat[:, 0, u:u + 1], -1.0, None, ALU.mult).then_inc(nmax_ready, 1)
                if 2 <= u <= N + 1:
                    w = u - 2
                    v.wait_ge(pv_done, w + 1)
                    if w >= 2:
                        v.wait_ge(o_done, w - 1)
                    v.tensor_copy(o_lat[:, w % 2, :], bank[4 + w % 2][:, 0:P]).then_inc(olat_ready, 1)
                    v.reciprocal(stat[:, 3, w:w + 1], stat[:, 2, w:w + 1]).then_inc(rsum_ready, 1)
                if u >= 3:
                    w = u - 3
                    i, h = UNITS[w]
                    v.wait_ge(o_done, w + 1)
                    v.wait_ge(rsum_ready, w + 1)
                    v.tensor_scalar(sh.cat[:, i, D_GROUP + h * C:D_GROUP + (h + 1) * C], bank[6 + w % 2][:, 0:C],
                                    stat[:, 3, w:w + 1], None, ALU.mult).then_inc(o_ready, 1)


def prepare(nc, io, sh):
    with ExitStack() as ctx:
        e = ctx.enter_context
        w2a2 = e(nc.sbuf_tensor("w2_a2_sb", [P, D_GROUP], F32))
        tanh = e(nc.sbuf_tensor("tanh_w", [C, S], F32))
        sig = e(nc.sbuf_tensor("sig_w", [P, NPAIR, S], F32))
        cum = e(nc.sbuf_tensor("cum", [P, NPAIR, S], F32))
        sqk = e(nc.sbuf_tensor("kk_squares", [P, 2, S], F32))
        root = e(nc.sbuf_tensor("kk_root", [P, NPAIR, S], F32))
        rate = e(nc.sbuf_tensor("rate", [P, 2, S], F32))
        prod = e(nc.sbuf_tensor("rk_prod", [P, 2, S], F32))
        grow = e(nc.sbuf_tensor("decays", [P, 3, 2, S], F32))
        bank = psum_banks(nc, e, "prepare")
        b_hat = sh.b_hat
        KK0 = SHIFT_TILES

        sem = sh.sem
        pw_in, tanh_ready, lora_done, sig_ready, gate_ready = sem("prep_w_in"), sem("tanh_ready"), sem("lora_done"), sem("sigw_ready"), sem("gate_sig_ready")
        kk_raw, kk_squared, kk_summed, kk_rooted = sem("kk_raw"), sem("kk_squared"), sem("kk_summed"), sem("kk_rooted")
        root_step, kk_ready, rate_ready, k_ready, b_ready = sem("root_step"), sem("kk_ready"), sem("rate_ready"), sem("k_ready"), sem("b_ready")
        prod_ready, bonus_done, cum_ready, dif_ready, grown, scaled = sem("prod_ready"), sem("bonus_done"), sem("cum_ready"), sem("dif_ready"), sem("grown"), sem("scaled")
        v_turned, v_copied, bonus_copied, end_ready = sem("v_turned"), sem("v_copied"), sem("bonus_copied"), sem("end_ready")
        R0, K0, V0, WA, G0 = 0, NPAIR, 2 * NPAIR, 3 * NPAIR, 3 * NPAIR + 1
        block = e(nc.Block())

        @block.sync
        def _(sp):
            sp.dma_start(w2a2[0:C, :], io["rwkv_w2"][0]).then_inc(pw_in, 16)
            sp.dma_start(w2a2[C:P, :], io["rwkv_a2"][0]).then_inc(pw_in, 16)

        @block.tensor
        def _(pe):
            ident = sh.const("ident")
            pe.wait_ge(pw_in, 32)
            pe.wait_ge(tanh_ready, 1)
            for g in range(NPAIR):
                cs = slice(g * P, (g + 1) * P)
                if g >= 2:
                    pe.wait_ge(sig_ready, 2 * (g - 1))
                pe.matmul(bank[g % 2][:, :], w2a2[0:C, cs], tanh[:, :], start=True, stop=True).then_inc(lora_done, 1)
                pe.matmul(bank[2 + g % 2][:, :], w2a2[C:P, cs], sh.pT[C:P, WA, :], start=True, stop=True).then_inc(lora_done, 1)
            for g in range(NPAIR):
                pe.wait_ge(kk_squared, g + 1)
                if g >= 2:
                    pe.wait_ge(kk_rooted, g - 1)
                pe.matmul(bank[4 + g % 2][:, :], sh.const("half"), sqk[:, g % 2, :], start=True, stop=True).then_inc(kk_summed, 1)
                if g >= 1:
                    pe.wait_ge(v_copied, g)
                for i in range(NT):
                    last = pe.transpose(bank[6][:, i * P:(i + 1) * P], sh.pT[:, V0 + g, i * P:(i + 1) * P], ident)
                last.then_inc(v_turned, 1)
            for g in range(NPAIR):
                pe.wait_ge(prod_ready, g + 1)
                for i in range(NT):
                    last = pe.matmul(bank[7][:, i * HEADS + 2 * g:i * HEADS + 2 * g + 2], prod[:, g % 2, i * P:(i + 1) * P],
                                     sh.const("heads"), start=True, stop=True)
                last.then_inc(bonus_done, 1)

        @block.scalar
        def _(act):
            act.activation(tanh[:, :], sh.pT[0:C, WA, :], ACT.Tanh).then_inc(tanh_ready, 1)
            act.activation(sh.gate_sig[:, :], sh.pT[:, G0, :], ACT.Sigmoid).then_inc(gate_ready, 1)
            for g in range(NPAIR):
                act.wait_ge(lora_done, 2 * g + 2)
                act.activation(sig[:, g, :], bank[g % 2][:, :], ACT.Sigmoid, bias=sh.col("rwkv_w0", g)).then_inc(sig_ready, 1)
                act.activation(b_hat[:, g, :], bank[2 + g % 2][:, :], ACT.Sigmoid, bias=sh.col("rwkv_a0", g)).then_inc(sig_ready, 1)
            for g in range(NPAIR):
                act.wait_ge(kk_raw, g + 1)
                if g >= 2:
                    act.wait_ge(kk_summed, g - 1)
                act.activation(sqk[:, g % 2, :], sh.pT[:, KK0 + g, :], ACT.Square).then_inc(kk_squared, 1)
                act.wait_ge(kk_summed, g + 1)
                act.activation(root[:, g, :], bank[4 + g % 2][:, :], ACT.Sqrt).then_inc(kk_rooted, 1)
                act.wait_ge(v_turned, g + 1)
                act.copy(sh.v_tm[:, :, g * P:(g + 1) * P], bank[6][:, :].rearrange("p (a b) -> p a b", b=P)).then_inc(v_copied, 1)
            for g in range(NPAIR):
                act.wait_ge(cum_ready, g + 1)
                if g >= 2:
                    act.wait_ge(scaled, 4 * (g - 1))
                    act.wait_ge(end_ready, g - 1)
                act.activation(grow[:, 0, g % 2, :], cum[:, g, :], ACT.Exp, scale=-DECAY).then_inc(grown, 1)
                act.activation(grow[:, 1, g % 2, :], cum[:, g, :], ACT.Exp, scale=DECAY).then_inc(grown, 1)
                act.wait_ge(dif_ready, g + 1)
                act.activation(grow[:, 2, g % 2, :], sig[:, g, :], ACT.Exp, scale=-DECAY).then_inc(grown, 1)

        @block.vector
        def _(v):
            keep = sh.const("keep")
            for g in range(NPAIR):
                v.tensor_scalar(sh.pT[:, KK0 + g, :], sh.pT[:, K0 + g, :], sh.col("rwkv_k_k", g), None, ALU.mult).then_inc(kk_raw, 1)
            for g in range(NPAIR):
                v.wait_ge(sig_ready, 2 * g + 2)
                v.tensor_tensor_scan(cum[:, g, :], keep, sig[:, g, :], 0.0, ALU.mult, ALU.add).then_inc(cum_ready, 1)
                v.tensor_scalar(rate[:, g % 2, :], b_hat[:, g, :], -1.0, sh.col("rwkv_k_a", g), ALU.add, ALU.mult).then_inc(rate_ready, 1)
                v.wait_ge(cum_ready, g + 1)
                v.tensor_tensor(sig[:, g, :], cum[:, g, :], sig[:, g, :], ALU.subtract).then_inc(dif_ready, 1)
                v.wait_ge(rate_ready, g + 1)
                v.scalar_tensor_tensor(sh.pT[:, K0 + g, :], rate[:, g % 2, :], 1.0, sh.pT[:, K0 + g, :], ALU.add, ALU.mult).then_inc(k_ready, 1)
                v.wait_ge(k_ready, g + 1)
                if g >= 2:
                    v.wait_ge(bonus_done, g - 1)
                v.scalar_tensor_tensor(prod[:, g % 2, :], sh.pT[:, R0 + g, :], sh.col("rwkv_r_k", g), sh.pT[:, K0 + g, :], ALU.mult, ALU.mult).then_inc(prod_ready, 1)
            for g in range(NPAIR):
                v.wait_ge(kk_rooted, g + 1)
                v.tensor_scalar(root[:, g, :], root[:, g, :], 1e-12, None, ALU.max).then_inc(root_step, 1)
                v.wait_ge(root_step, 2 * g + 1)
                v.reciprocal(root[:, g, :], root[:, g, :]).then_inc(root_step, 1)
                v.wait_ge(root_step, 2 * g + 2)
                v.tensor_tensor(sh.pT[:, KK0 + g, :], sh.pT[:, KK0 + g, :], root[:, g, :], ALU.mult).then_inc(kk_ready, 1)
                v.wait_ge(kk_ready, g + 1)
                v.tensor_tensor(b_hat[:, g, :], b_hat[:, g, :], sh.pT[:, KK0 + g, :], ALU.mult).then_inc(b_ready, 1)
            v.wait_ge(b_ready, NPAIR)
            v.wait_ge(prod_ready, NPAIR)
            for g in range(NPAIR):
                b = g % 2
                v.wait_ge(grown, 3 * g + 1)
                v.tensor_tensor(sh.pT[:, R0 + g, :], sh.pT[:, R0 + g, :], grow[:, 0, b, :], ALU.mult).then_inc(scaled, 1)
                v.tensor_copy(sh.w_end[:, g, :], grow[:, 0, b, C - 1::C]).then_inc(end_ready, 1)
                v.wait_ge(grown, 3 * g + 2)
                v.tensor_tensor(b_hat[:, g, :], b_hat[:, g, :], grow[:, 1, b, :], ALU.mult).then_inc(scaled, 1)
                v.tensor_tensor(sh.pT[:, K0 + g, :], sh.pT[:, K0 + g, :], grow[:, 1, b, :], ALU.mult).then_inc(scaled, 1)
                v.wait_ge(grown, 3 * g + 3)
                v.scalar_tensor_tensor(sh.pT[:, KK0 + g, :], sh.pT[:, KK0 + g, :], -1.0, grow[:, 2, b, :], ALU.mult, ALU.mult).then_inc(scaled, 1)
            v.wait_ge(bonus_done, NPAIR)
            v.tensor_copy(sh.bonus[:, :, :], bank[7][:, 0:NT * HEADS].rearrange("p (a b) -> p a b", b=HEADS)).then_inc(bonus_copied, 1)


PE_STEPS = ["ba", "ab"] + [f"{s}{n}" for n in LEVELS for s in ("z", "t", "tt") if (s, n) != ("t", LEVELS[-1])] + \
           ["ka", "akv", "x", "oo", "rr", "m0", "n0"]
ACT_STEPS = ["abt"] + [f"{s}{n}" for n in LEVELS for s in ("t", "tt") if (s, n) != ("t", LEVELS[-1])] + ["akv", "x", "oo"]
DVE_STEPS = ["arb", "t", "tt"] + [f"z{n}" for n in LEVELS] + ["ka", "rr", "m0", "n0"]
POOL_STEPS = [f"lv{n}" for n in LEVELS]


def scan(nc, io, sh):
    with ExitStack() as ctx:
        e = ctx.enter_context
        two = range(2)
        g2 = e(nc.sbuf_tensor("g2_sb", [P, D_GROUP], F32))
        lnb = e(nc.sbuf_tensor("rwkv_ln_sb", [P, 2, D_GROUP], F32))
        tm = e(nc.sbuf_tensor("abk_tm", [P, 3, NT, P], F32))
        Tm = [e(nc.sbuf_tensor(f"T{h}", [P, NT, P], F32)) for h in two]
        TT = [e(nc.sbuf_tensor(f"TT{h}", [P, NT, P], F32)) for h in two]
        Z1 = [e(nc.sbuf_tensor(f"Z1{h}", [P, NT, P], F32)) for h in two]
        LV = [e(nc.sbuf_tensor(f"LV{h}", [P, NT, P], F32)) for h in two]
        ABT = [e(nc.sbuf_tensor(f"ABT{h}", [P, NT, P], F32)) for h in two]
        ARB = [e(nc.sbuf_tensor(f"ARB{h}", [P, NT, P], F32)) for h in two]
        KA = [e(nc.sbuf_tensor(f"KA{h}", [P, NT, 2, P], F32)) for h in two]
        AKV = [e(nc.sbuf_tensor(f"AKV{h}", [P, NT, C], F32)) for h in two]
        X = [e(nc.sbuf_tensor(f"X{h}", [P, NT, P], F32)) for h in two]
        RR = e(nc.sbuf_tensor("RR", [P, S], F32))
        M0 = e(nc.sbuf_tensor("M0", [P, NCH, C], F32))
        N0 = e(nc.sbuf_tensor("N0", [P, NCH, C], F32))
        ST = e(nc.sbuf_tensor("state", [P, NCH + 1, C], F32))
        gn = e(nc.sbuf_tensor("gn_stats", [P, NT, 4, HEADS], F32))
        bank = psum_banks(nc, e, "scan")
        own = [bank[0:4], bank[4:8]]

        sem = sh.sem
        sw_in, tm_turned, tm_copied = sem("scan_w_in"), sem("tm_turned"), sem("tm_copied")
        pe_step = [sem(f"pe_step{h}") for h in two]
        act_step = [sem(f"act_step{h}") for h in two]
        dve_step = [sem(f"dve_step{h}") for h in two]
        pool_step = [sem(f"pool_step{h}") for h in two]
        dve_half = sem("dve_half")
        state_done, state_ready, carry_done, carry_added = sem("state_done"), sem("state_ready"), sem("carry_done"), sem("carry_added")
        gn_sum, gn_dev, gn_sq, gn_var, gn_root, gn_step, gate_done, gate_free = (sem("gn_sum"), sem("gn_dev"), sem("gn_sq"), sem("gn_var"),
                                                                    sem("gn_root"), sem("gn_step"), sem("gate_done"), sem("gate_free"))
        R0, K0, A0 = 0, NPAIR, SHIFT_TILES
        half = lambda h: slice(C * h, C * h + C)

        def pe_after(eng, h, r, name):
            eng.wait_ge(pe_step[h], r * len(PE_STEPS) + PE_STEPS.index(name) + 1)

        def act_after(eng, h, r, name):
            eng.wait_ge(act_step[h], r * len(ACT_STEPS) + ACT_STEPS.index(name) + 1)

        def dve_after(eng, h, r, name):
            eng.wait_ge(dve_step[h], r * len(DVE_STEPS) + DVE_STEPS.index(name) + 1)

        def pool_after(eng, h, r, name):
            eng.wait_ge(pool_step[h], r * len(POOL_STEPS) + POOL_STEPS.index(name) + 1)

        flat = lambda t: t[:, :, :].rearrange("p a b -> p (a b)")
        dev = lambda i: flat(Tm[i % 2])
        sqd = lambda i: flat(TT[i % 2])

        def tiles(ap):
            return ap.rearrange("p (a b) -> p a b", b=P)

        def bc(ap, n):
            return ap.rearrange("p (a m) -> p a m", a=1).broadcast_to([ap.shape[0], n, ap.shape[1]])

        block = e(nc.Block())

        @block.sync
        def _(sp):
            sp.dma_start(g2[:, :], io["rwkv_g2"][0]).then_inc(sw_in, 16)
            sp.dma_start(lnb[:, 0, :], io["rwkv_ln_w"].broadcast_to([P, D_GROUP])).then_inc(sw_in, 16)
            sp.dma_start(lnb[:, 1, :], io["rwkv_ln_b"].broadcast_to([P, D_GROUP])).then_inc(sw_in, 16)

        @block.tensor
        def _(pe):
            ident = sh.const("ident")
            for r in range(NPAIR):
                for n, src in enumerate((sh.pT[:, A0 + r, :], sh.b_hat[:, r, :], sh.pT[:, K0 + r, :])):
                    if r:
                        pe.wait_ge(carry_added, r)
                        dve_after(pe, 0, r - 1, "n0")
                        dve_after(pe, 1, r - 1, "n0")
                    for i in range(NT):
                        last = pe.transpose(bank[n][:, i * P:(i + 1) * P], src[:, i * P:(i + 1) * P], ident)
                    last.then_inc(tm_turned, 1)
                pe.wait_ge(tm_copied, 3 * (r + 1))
                for h in two:
                    if r:
                        act_after(pe, h, r - 1, "oo")
                    for i in range(NT):
                        ts = slice(i * P, (i + 1) * P)
                        last = pe.matmul(own[h][i // 2][:, (i % 2) * 256:(i % 2) * 256 + 256].rearrange("p (a b) -> p a b", b=P), sh.b_hat[half(h), r, ts],
                                         sh.pT[half(h), R0 + r:A0 + r + 1:A0 - R0, ts],
                                         start=True, stop=True)
                    last.then_inc(pe_step[h], 1)
                for h in two:
                    for i in range(NT):
                        ts = slice(i * P, (i + 1) * P)
                        last = pe.matmul(own[h][2][:, ts], sh.pT[half(h), A0 + r, ts], sh.b_hat[half(h), r, ts], start=True, stop=True)
                    last.then_inc(pe_step[h], 1)
                for n in LEVELS:
                    for h in two:
                        pool_after(pe, h, r, f"lv{n}")
                        if n == LEVELS[0]:
                            dve_after(pe, h, r, "tt")
                        else:
                            act_after(pe, h, r, f"t{n // 2}")
                            act_after(pe, h, r, f"tt{n // 2}")
                        for i in range(NT):
                            last = pe.matmul(own[h][3][:, i * P:(i + 1) * P], LV[h][:, i, :], Tm[h][:, i, :], start=True, stop=True)
                        last.then_inc(pe_step[h], 1)
                    for h in two:
                        dve_after(pe, h, r, f"z{n}")
                        if n != LEVELS[-1]:
                            for i in range(NT):
                                last = pe.matmul(own[h][0][:, i * P:(i + 1) * P], TT[h][:, i, :], Z1[h][:, i, :], start=True, stop=True)
                            last.then_inc(pe_step[h], 1)
                        for i in range(NT):
                            last = pe.matmul(own[h][1][:, i * P:(i + 1) * P], Z1[h][:, i, :], TT[h][:, i, :], start=True, stop=True)
                        last.then_inc(pe_step[h], 1)
                for h in two:
                    for i in range(NT):
                        ts = slice(i * P, (i + 1) * P)
                        last = pe.matmul(own[h][2 + i // 2][:, (i % 2) * 256:(i % 2) * 256 + 256].rearrange("p (a b) -> p a b", b=P), sh.pT[half(h), K0 + r, ts],
                                         sh.pT[half(h), R0 + r:A0 + r + 1:A0 - R0, ts], start=True, stop=True)
                    last.then_inc(pe_step[h], 1)
                vs = lambda h: slice(r * P + h * C, r * P + h * C + C)
                for h in two:
                    dve_after(pe, h, r, "ka")
                    for i in range(NT):
                        last = pe.matmul(own[h][0][:, i * C:(i + 1) * C], KA[h][:, i, 1, :], sh.v_tm[:, i, vs(h)], start=True, stop=True)
                    last.then_inc(pe_step[h], 1)
                for h in two:
                    act_after(pe, h, r, "akv")
                    act_after(pe, h, r, f"tt{LEVELS[-1]}")
                    for i in range(NT):
                        pe.matmul(own[h][1][:, i * P:i * P + C], TT[h][:, i, :], tm[:, 0, i, half(h)], start=True, stop=True)
                        last = pe.matmul(own[h][1][:, i * P + C:(i + 1) * P], TT[h][:, i, :], AKV[h][:, i, :], start=True, stop=True)
                    last.then_inc(pe_step[h], 1)
                for h in two:
                    act_after(pe, h, r, "x")
                    for i in range(NT):
                        pe.matmul(own[h][2][:, i * C:(i + 1) * C], KA[h][:, i, 0, :], sh.v_tm[:, i, vs(h)], start=True, stop=False)
                        last = pe.matmul(own[h][2][:, i * C:(i + 1) * C], ARB[h][:, i, :], X[h][:, i, C:P], start=False, stop=True)
                    last.then_inc(pe_step[h], 1)
                for h in two:
                    for i in range(NT):
                        last = pe.matmul(own[h][3][half(h), i * P:(i + 1) * P], X[h][:, i, 0:C], ARB[h][:, i, :], start=True, stop=True)
                    last.then_inc(pe_step[h], 1)
                for h in two:
                    act_after(pe, h, r, "oo")
                    for n in range(NCH):
                        tok = half(n % 2)
                        last = pe.matmul(own[h][2 * (n % 2)][half(h), n // 2 * C:(n // 2 + 1) * C], X[h][tok, n // 2, 0:C], tm[tok, 1, n // 2, half(h)], start=True, stop=True)
                    last.then_inc(pe_step[h], 1)
                for h in two:
                    dve_after(pe, h, r, "rr")
                    for n in range(NCH):
                        tok = half(n % 2)
                        out = own[h][1 + 2 * (n % 2)][half(h), n // 2 * C:(n // 2 + 1) * C]
                        pe.matmul(out, tm[tok, 2, n // 2, half(h)], sh.v_tm[tok, n // 2, vs(h)], start=True, stop=False)
                        last = pe.matmul(out, tm[tok, 1, n // 2, half(h)], X[h][tok, n // 2, C:P], start=False, stop=True)
                    last.then_inc(pe_step[h], 1)
                for n in range(NCH):
                    pe.wait_ge(state_ready, r * NCH + n + 1)
                    if n < NCH - 1 and n > 0:
                        for h in two:
                            last = pe.matmul(bank[2][half(h), (n % 2) * C:(n % 2) * C + C], M0[half(h), n, :], ST[half(h), n, :], start=True, stop=True)
                        last.then_inc(state_done, 1)
                    for h in two:
                        last = pe.matmul(own[h][3][half(n % 2), (n // 2) * C:(n // 2 + 1) * C], RR[half(h), n * C:(n + 1) * C], ST[half(h), n, :],
                                         start=True, stop=True)
                last.then_inc(carry_done, 1)
            pe.wait_ge(sw_in, 48)
            for i in range(NT):
                pe.wait_ge(carry_added, NPAIR)
                if i >= 2:
                    pe.wait_ge(gate_free, i - 1)
                pe.matmul(bank[i % 2][:, :], sh.gate_sig[:, i * P:(i + 1) * P], g2[:, :], start=True, stop=True).then_inc(gate_done, 1)

        @block.scalar
        def _(act):
            for r in range(NPAIR):
                for n in range(3):
                    act.wait_ge(tm_turned, 3 * r + n + 1)
                    act.copy(tm[:, n, :, :], tiles(bank[n][:, :])).then_inc(tm_copied, 1)
                for h in two:
                    pe_after(act, h, r, "ba")
                    for b in two:
                        last = act.copy(ABT[h][:, 2 * b:2 * b + 2, :], own[h][b][:, :].rearrange("p (a b c) -> p a b c", a=2, b=2)[:, :, 1, :])
                    last.then_inc(act_step[h], 1)
                for n in LEVELS:
                    for h in two:
                        if n != LEVELS[-1]:
                            pe_after(act, h, r, f"t{n}")
                            act.copy(Tm[h][:, :, :], tiles(own[h][0][:, :])).then_inc(act_step[h], 1)
                        pe_after(act, h, r, f"tt{n}")
                        act.copy(TT[h][:, :, :], tiles(own[h][1][:, :])).then_inc(act_step[h], 1)
                for h in two:
                    pe_after(act, h, r, "akv")
                    act.copy(AKV[h][:, :, :], own[h][0][:, 0:NT * C].rearrange("p (a b) -> p a b", b=C)).then_inc(act_step[h], 1)
                for h in two:
                    pe_after(act, h, r, "x")
                    act.copy(X[h][:, :, :], tiles(own[h][1][:, :])).then_inc(act_step[h], 1)
                for h in two:
                    pe_after(act, h, r, "oo")
                    act.copy(sh.cat[:, :, r * P + h * C:r * P + (h + 1) * C], own[h][2][:, 0:NT * C].rearrange("p (a b) -> p a b", b=C)).then_inc(act_step[h], 1)
            for i in range(NT):
                act.wait_ge(gn_dev, i + 1)
                act.activation(sqd(i), dev(i), ACT.Square).then_inc(gn_sq, 1)
                act.wait_ge(gn_var, i + 1)
                act.activation(gn[:, i, 2, :], gn[:, i, 1, :], ACT.Sqrt, bias=sh.const("eps")[:, 2:3], scale=1.0 / C).then_inc(gn_root, 1)

        @block.gpsimd
        def _(pool):
            for r in range(NPAIR):
                for n in LEVELS:
                    for h in two:
                        if n == LEVELS[0]:
                            act_after(pool, h, r, "abt")
                        else:
                            pe_after(pool, h, r, f"z{n // 2}")
                        pool.tensor_tensor(LV[h][:, :, :], ABT[h][:, :, :], bc(sh.const(f"lev{n}"), NT), ALU.mult).then_inc(pool_step[h], 1)

        @block.vector
        def _(v):
            halves = 0
            for r in range(NPAIR):
                for h in two:
                    act_after(v, h, r, "abt")
                    if r:
                        pe_after(v, h, r - 1, "n0")
                    for b in two:
                        last = v.tensor_tensor(ARB[h][:, 2 * b:2 * b + 2, :], own[h][b][:, :].rearrange("p (a b c) -> p a b c", a=2, b=2)[:, :, 0, :],
                                               bc(sh.const("incl"), 2), ALU.mult)
                    last.then_inc(dve_step[h], 1)
                    pe_after(v, h, r, "ab")
                    v.tensor_tensor(Tm[h][:, :, :], tiles(own[h][2][:, :]), bc(sh.const("low2"), NT), ALU.mult).then_inc(dve_half, 1)
                    v.tensor_tensor(TT[h][:, :, :], ABT[h][:, :, :], bc(sh.const("up2"), NT), ALU.mult).then_inc(dve_half, 1)
                    halves += 2
                    v.wait_ge(dve_half, halves)
                    v.tensor_tensor(Tm[h][:, :, :], Tm[h][:, :, :], bc(sh.const("ident"), NT), ALU.add).then_inc(dve_step[h], 1)
                    v.tensor_tensor(TT[h][:, :, :], TT[h][:, :, :], bc(sh.const("ident"), NT), ALU.add).then_inc(dve_step[h], 1)
                for n in LEVELS:
                    for h in two:
                        pe_after(v, h, r, f"z{n}")
                        v.tensor_tensor(Z1[h][:, :, :], tiles(own[h][3][:, :]), bc(sh.const("ident"), NT), ALU.add).then_inc(dve_step[h], 1)
                for h in two:
                    pe_after(v, h, r, "ka")
                    for b in two:
                        for q, m in ((0, "incl"), (1, "strict")):
                            last = v.tensor_tensor(KA[h][:, 2 * b:2 * b + 2, q, :], own[h][2 + b][:, :].rearrange("p (a b c) -> p a b c", a=2, b=2)[:, :, q, :],
                                                   bc(sh.const(m), 2), ALU.mult)
                    last.then_inc(dve_step[h], 1)
                for h in two:
                    pe_after(v, h, r, "rr")
                    if r:
                        v.wait_ge(carry_done, r)
                    v.tensor_tensor(RR[half(h), :], own[h][3][half(h), :], sh.pT[half(h), R0 + r, :], ALU.add).then_inc(dve_step[h], 1)
                for h in two:
                    pe_after(v, h, r, "m0")
                    for b in two:
                        last = v.tensor_tensor(M0[half(h), b::2, :], own[h][2 * b][half(h), 0:NCH // 2 * C].rearrange("p (a b) -> p a b", b=C),
                                               bc(sh.const("ident")[half(h), half(h)], NCH // 2), ALU.add)
                    last.then_inc(dve_step[h], 1)
                for h in two:
                    pe_after(v, h, r, "n0")
                    for b in two:
                        last = v.tensor_tensor(N0[half(h), b::2, :], own[h][1 + 2 * b][half(h), 0:NCH // 2 * C].rearrange("p (a b) -> p a b", b=C),
                                               sh.w_end[half(h), r, b::2].rearrange("p (a b) -> p a b", b=1).broadcast_to([C, NCH // 2, C]), ALU.mult)
                    last.then_inc(dve_step[h], 1)
                dve_after(v, 0, r, "n0")
                dve_after(v, 1, r, "n0")
                v.memset(ST[:, 0, :], 0.0).then_inc(state_ready, 1)
                v.tensor_copy(ST[:, 1, :], N0[:, 0, :]).then_inc(state_ready, 1)
                for n in range(1, NCH - 1):
                    v.wait_ge(state_done, r * (NCH - 2) + n)
                    v.scalar_tensor_tensor(ST[:, n + 1, :], bank[2][:, (n % 2) * C:(n % 2) * C + C], sh.w_end[:, r, n:n + 1], N0[:, n, :],
                                           ALU.mult, ALU.add).then_inc(state_ready, 1)
                v.wait_ge(carry_done, r + 1)
                act_after(v, 0, r, "oo")
                act_after(v, 1, r, "oo")
                for h in two:
                    cat = sh.cat[:, :, r * P + h * C:r * P + (h + 1) * C]
                    last = v.tensor_tensor(cat, cat, own[h][3][:, 0:NT * C].rearrange("p (a b) -> p a b", b=C), ALU.add)
                last.then_inc(carry_added, 1)
            v.wait_ge(carry_added, NPAIR)
            v.wait_ge(sw_in, 48)
            wide = lambda ap: ap.rearrange("p (a b) -> p a b", b=1).broadcast_to([P, HEADS, C])
            heads = lambda ap: ap.rearrange("p (a b) -> p a b", b=C)
            steps = 0
            for i in range(NT):
                o = sh.cat[:, i, 0:D_GROUP]
                v.tensor_reduce(gn[:, i, 0, :], heads(o), AX.X, ALU.add).then_inc(gn_step, 1)
                steps += 1
                v.wait_ge(gn_step, steps)
                v.tensor_scalar(gn[:, i, 3, :], gn[:, i, 0, :], 1.0 / C, None, ALU.mult).then_inc(gn_step, 1)
                steps += 1
                v.wait_ge(gn_step, steps)
                if i >= 2:
                    v.wait_ge(gate_free, i - 1)
                v.tensor_tensor(heads(dev(i)), heads(o), wide(gn[:, i, 3, :]), ALU.subtract).then_inc(gn_dev, 1)
                v.wait_ge(gn_sq, i + 1)
                v.tensor_reduce(gn[:, i, 1, :], heads(sqd(i)), AX.X, ALU.add).then_inc(gn_var, 1)
                v.wait_ge(gn_root, i + 1)
                v.reciprocal(gn[:, i, 3, :], gn[:, i, 2, :]).then_inc(gn_step, 1)
                steps += 1
                v.wait_ge(gn_step, steps)
                for a, b, op in ((heads(dev(i)), wide(gn[:, i, 3, :]), ALU.mult), (dev(i), lnb[:, 0, :], ALU.mult), (dev(i), lnb[:, 1, :], ALU.add)):
                    v.tensor_tensor(a, a, b, op).then_inc(gn_step, 1)
                    steps += 1
                    v.wait_ge(gn_step, steps)
                v.tensor_tensor(heads(sqd(i)), heads(sh.v_tm[:, i, :]), wide(sh.bonus[:, i, :]), ALU.mult).then_inc(gn_step, 1)
                steps += 1
                v.wait_ge(gn_step, steps)
                v.tensor_tensor(dev(i), dev(i), sqd(i), ALU.add).then_inc(gn_step, 1)
                steps += 1
                v.wait_ge(gn_step, steps)
                v.wait_ge(gate_done, i + 1)
                v.tensor_tensor(o, dev(i), bank[i % 2][:, :], ALU.mult).then_inc(gate_free, 1)


def route(nc, io, sh):
    NR = NT * TOP_E
    with ExitStack() as ctx:
        e = ctx.enter_context
        wout = e(nc.sbuf_tensor("w_out_sb", [P, KC, D], F32))
        catT = e(nc.sbuf_tensor("catT", [P, KC, S], F32))
        u2T = e(nc.sbuf_tensor("u2T", [P, KC, S], F32))
        ln = e(nc.sbuf_tensor("ln1_rows", [P, 2, D], F32))
        wr = e(nc.sbuf_tensor("w_router_sb", [P, KC, N_EXP], F32))
        br = e(nc.sbuf_tensor("b_router_sb", [P, N_EXP], F32))
        mixg = e(nc.sbuf_tensor("mix_gated", [P, D], F32))
        u2 = e(nc.sbuf_tensor("u2", [P, 2, D], F32))
        st = e(nc.sbuf_tensor("ln1_stats", [P, NT, 16], F32))
        lg = e(nc.sbuf_tensor("router_logits", [P, NT, N_EXP], F32))
        m8 = e(nc.sbuf_tensor("top8", [P, NT, 8], F32))
        i8 = e(nc.sbuf_tensor("top8_at", [P, NT, 8], mybir.dt.uint32))
        idx = e(nc.sbuf_tensor("top_expert", [P, NT, 8], F32))
        sm = e(nc.sbuf_tensor("gate_stats", [P, NT, 4], F32))
        hot = e(nc.sbuf_tensor("one_hot", [P, TOP_E, NT, N_EXP], F32))
        chosen = e(nc.sbuf_tensor("chosen", [P, NT, N_EXP], F32))
        tmp = e(nc.sbuf_tensor("place_tmp", [P, 8, NT, N_EXP], F32))
        row = e(nc.sbuf_tensor("expert_rows", [P, 8, N_EXP], F32))
        ohx = e(nc.sbuf_tensor("extra_hot", [P, 2, EXTRA, N_EXP], F32))
        xf = e(nc.sbuf_tensor("extra_f", [P, EXTRA + 1], F32))
        slotk = e(nc.sbuf_tensor("slot_of", [P, NT, TOP_E], F32))
        blkk = e(nc.sbuf_tensor("block_of", [P, NT, TOP_E], F32))
        rowf = e(nc.sbuf_tensor("row_of", [P, NT, TOP_E], F32))
        Qh = e(nc.sbuf_tensor("slot_hot", [P, 4, P], F32))
        Rh = e(nc.sbuf_tensor("block_hot", [P, 4, BLOCKS], F32))
        bank = psum_banks(nc, e, "route")

        sem = sh.sem
        rw_in, cat_turned, catT_ready, mix_done = sem("route_w_in"), sem("cat_turned"), sem("catT_ready"), sem("mix_done")
        ln_step, gated, x1_ready, u2_ready, u2_turned, u2T_ready, u2_stored = (sem("ln1_step"), sem("gated"), sem("x1_ready"), sem("u2_ready"),
                                                                              sem("u2_turned"), sem("u2T_ready"), [sem("u2_stored0"), sem("u2_stored1")])
        var_ready, root_ready, logits_done, rt_step, chosen_ready, rank_done = (sem("ln1_var"), sem("ln1_root"), sem("logits_done"), sem("rt_step"),
                                                                              sem("chosen_ready"), sem("rank_done"))
        nmax_ready, exp_ready, hot_ready, ids_done = sem("gate_nmax"), sem("gate_exp"), sem("hot_ready"), sem("ids_done")
        block = e(nc.Block())

        @block.sync
        def _(sp):
            sp.dma_start(wout[:, :, :], io["w_out"][0].rearrange("(c p) n -> p c n", p=P)).then_inc(rw_in, 16)
            sp.dma_start(ln[:, 0, :], io["ln1_g"].broadcast_to([P, D])).then_inc(rw_in, 16)
            sp.dma_start(ln[:, 1, :], io["ln1_b"].broadcast_to([P, D])).then_inc(rw_in, 16)
            sp.dma_start(wr[:, :, :], io["w_router"][0].rearrange("(c p) n -> p c n", p=P)).then_inc(rw_in, 16)
            sp.dma_start(br[:, :], io["b_router"].broadcast_to([P, N_EXP])).then_inc(rw_in, 16)
            for i in range(NT):
                sp.wait_ge(u2_ready, i + 1)
                sp.dma_start(sh.u2_dram[i * P:(i + 1) * P, :], u2[:, i % 2, :]).then_inc(u2_stored[i % 2], 16)
            for k in range(2):
                sp.wait_ge(u2_stored[k], 16 * NT // 2)

        @block.tensor
        def _(pe):
            ident = sh.const("ident")
            for j in range(KC):
                if j >= 2:
                    pe.wait_ge(catT_ready, j - 1)
                for i in range(NT):
                    last = pe.transpose(bank[j % 2][:, i * P:(i + 1) * P], sh.cat[:, i, j * P:(j + 1) * P], ident)
                last.then_inc(cat_turned, 1)
            pe.wait_ge(rw_in, 80)
            pe.wait_ge(catT_ready, KC)

            def turn(i):
                pe.wait_ge(u2_ready, i + 1)
                if i:
                    pe.wait_ge(u2T_ready, 2 * i)
                for j in range(KC):
                    last = pe.transpose(bank[6 + j // 4][:, (j % 4) * P:(j % 4 + 1) * P], u2[:, i % 2, j * P:(j + 1) * P], ident)
                last.then_inc(u2_turned, 1)

            for i in range(NT):
                if i >= 2:
                    pe.wait_ge(gated, 2 * (i - 1))
                for q in range(2):
                    for j in range(KC):
                        last = pe.matmul(bank[2 + 2 * (i % 2) + q][:, :], catT[:, j, i * P:(i + 1) * P], wout[:, j, q * 512:(q + 1) * 512],
                                         start=(j == 0), stop=(j == KC - 1))
                    last.then_inc(mix_done, 1)
                if i:
                    turn(i - 1)
            turn(NT - 1)
            for i in range(NT):
                pe.wait_ge(u2T_ready, 2 * (i + 1))
                for j in range(KC):
                    last = pe.matmul(bank[0][:, i * N_EXP:(i + 1) * N_EXP], u2T[:, j, i * P:(i + 1) * P], wr[:, j, :], start=(j == 0), stop=(j == KC - 1))
            last.then_inc(logits_done, 1)
            pe.wait_ge(chosen_ready, 1)
            for i in range(NT):
                for k in range(i):
                    pe.matmul(bank[1][:, i * N_EXP:(i + 1) * N_EXP], sh.const("ones"), chosen[:, k, :], start=(k == 0), stop=False)
                pe.matmul(bank[1][:, i * N_EXP:(i + 1) * N_EXP], sh.const("before"), chosen[:, i, :], start=(i == 0), stop=True)
            for k in range(NT):
                last = pe.matmul(bank[1][:, NT * N_EXP:(NT + 1) * N_EXP], sh.const("ones"), chosen[:, k, :], start=(k == 0), stop=(k == NT - 1))
            last.then_inc(rank_done, 1)
            for n in range(NR):
                pe.wait_ge(hot_ready, n + 1)
                pe.matmul(bank[2][:, 0:BLOCKS], Qh[:, n % 4, :], Rh[:, n % 4, :], start=(n == 0), stop=(n == NR - 1)).then_inc(ids_done, 1)

        @block.scalar
        def _(act):
            for j in range(KC):
                act.wait_ge(cat_turned, j + 1)
                act.copy(catT[:, j, :], bank[j % 2][:, :]).then_inc(catT_ready, 1)
            for i in range(NT):
                act.wait_ge(var_ready, i + 1)
                act.activation(st[:, i, 14:15], st[:, i, 13:14], ACT.Sqrt, bias=sh.const("eps")[:, 1:2]).then_inc(root_ready, 1)
                act.wait_ge(u2_turned, i + 1)
                for q in range(2):
                    act.copy(u2T[:, 4 * q:4 * q + 4, i * P:(i + 1) * P], bank[6 + q][:, :].rearrange("p (a b) -> p a b", b=P)).then_inc(u2T_ready, 1)
            act.wait_ge(nmax_ready, 1)
            for i in range(NT):
                last = act.activation(sh.gate[:, i, :], m8[:, i, 0:TOP_E], ACT.Exp, bias=sm[:, i, 0:1], accum_out=sm[:, i, 1:2])
            last.then_inc(exp_ready, 1)

        @block.vector
        def _(v):
            count = {"ln": 0, "rt": 0}

            def ln1(ins):
                ins.then_inc(ln_step, 1)
                count["ln"] += 1
                v.wait_ge(ln_step, count["ln"])

            gate1, shift2, scale2, gate2 = (sh.modb[:, k * D:(k + 1) * D] for k in range(4))
            for m in (gate1, scale2, gate2):
                last = v.tensor_scalar(m, m, 1.0, None, ALU.add)
            ln1(last)
            v.wait_ge(rw_in, 80)
            for i in range(NT):
                x = sh.x_tm[:, i, :]
                for q in range(2):
                    v.wait_ge(mix_done, 2 * i + q + 1)
                    v.tensor_tensor(mixg[:, q * 512:(q + 1) * 512], bank[2 + 2 * (i % 2) + q][:, :], gate1[:, q * 512:(q + 1) * 512], ALU.mult).then_inc(gated, 1)
                v.wait_ge(gated, 2 * i + 2)
                ln1(v.scalar_tensor_tensor(x, x, ALPHA, mixg[:, :], ALU.mult, ALU.add))
                v.bn_stats(st[:, i, 0:6], x[:, 0:512])
                ln1(v.bn_stats(st[:, i, 6:12], x[:, 512:D]))
                v.bn_aggr(st[:, i, 12:14], st[:, i, 0:12].rearrange("p (a b) -> p a b", b=6)).then_inc(var_ready, 1)
                v.wait_ge(root_ready, i + 1)
                ln1(v.reciprocal(st[:, i, 15:16], st[:, i, 14:15]))
                ln1(v.tensor_scalar(x, x, st[:, i, 12:13], st[:, i, 15:16], ALU.subtract, ALU.mult))
                ln1(v.tensor_tensor(x, x, ln[:, 0, :], ALU.mult))
                ln1(v.tensor_tensor(x, x, ln[:, 1, :], ALU.add))
                if i >= 2:
                    v.wait_ge(u2_stored[i % 2], 16 * (i // 2))
                    v.wait_ge(u2_turned, i - 1)
                ln1(v.tensor_tensor(u2[:, i % 2, :], x, scale2, ALU.mult))
                v.tensor_tensor(u2[:, i % 2, :], u2[:, i % 2, :], shift2, ALU.add).then_inc(u2_ready, 1)

            def rt(ins):
                ins.then_inc(rt_step, 1)
                count["rt"] += 1
                v.wait_ge(rt_step, count["rt"])

            def along(ap, n, at):
                if at == 1:
                    return ap.rearrange("p (a m) -> p a m", a=1).broadcast_to([P, n, ap.shape[1]])
                return ap.rearrange("p (m a) -> p m a", a=1).broadcast_to([P, ap.shape[1], n])

            v.wait_ge(logits_done, 1)
            rt(v.tensor_tensor(lg[:, :, :], bank[0][:, 0:NT * N_EXP].rearrange("p (a b) -> p a b", b=N_EXP), along(br[:, :], NT, 1), ALU.add))
            for i in range(NT):
                rt(v.max(m8[:, i, :], lg[:, i, :]))
                rt(v.max_index(i8[:, i, :], m8[:, i, :], lg[:, i, :]))
            v.tensor_scalar(sm[:, :, 0:1], m8[:, :, 0:1], -1.0, None, ALU.mult).then_inc(nmax_ready, 1)
            rt(v.tensor_copy(idx[:, :, :], i8[:, :, :]))
            for k in range(TOP_E):
                last = v.tensor_tensor(hot[:, k, :, :], along(sh.const("expert"), NT, 1), along(idx[:, :, k], N_EXP, 2), ALU.is_equal)
            rt(last)
            rt(v.tensor_tensor(tmp[:, 0, :, :], hot[:, 0, :, :], hot[:, 1, :, :], ALU.add))
            rt(v.tensor_tensor(tmp[:, 1, :, :], hot[:, 2, :, :], hot[:, 3, :, :], ALU.add))
            v.tensor_tensor(chosen[:, :, :], tmp[:, 0, :, :], tmp[:, 1, :, :], ALU.add).then_inc(chosen_ready, 1)
            v.wait_ge(exp_ready, 1)
            rt(v.reciprocal(sm[:, :, 2:3], sm[:, :, 1:2]))
            rt(v.tensor_tensor(sh.gate[:, :, :], sh.gate[:, :, :], sm[:, :, 2:3].broadcast_to([P, NT, TOP_E]), ALU.mult))
            v.wait_ge(rank_done, 1)
            total, extra, upto, first, shift = (row[:, k, :] for k in range(5))
            rt(v.tensor_copy(total, bank[1][:, NT * N_EXP:(NT + 1) * N_EXP]))
            rt(v.tensor_scalar(extra, total, float(P) + 0.5, None, ALU.is_gt))
            for m in range(2, NT):
                rt(v.scalar_tensor_tensor(extra, total, float(m * P) + 0.5, extra, ALU.is_gt, ALU.add))
            rt(v.tensor_tensor_scan(upto, sh.const("ones")[:, 0:N_EXP], extra, 0.0, ALU.mult, ALU.add))
            rt(v.tensor_tensor(first, upto, extra, ALU.subtract))
            rt(v.scalar_tensor_tensor(shift, first, float(N_EXP), sh.const("expert"), ALU.add, ALU.subtract))
            pos, past, deep, slot, blk = (tmp[:, k, :, :] for k in range(5))
            rt(v.tensor_copy(pos, bank[1][:, 0:NT * N_EXP].rearrange("p (a b) -> p a b", b=N_EXP)))
            rt(v.tensor_scalar(past, pos, float(P) - 0.5, None, ALU.is_gt))
            rt(v.tensor_scalar(deep, pos, float(2 * P) - 0.5, None, ALU.is_gt))
            for m in range(3, NT):
                rt(v.scalar_tensor_tensor(deep, pos, float(m * P) - 0.5, deep, ALU.is_gt, ALU.add))
            rt(v.tensor_tensor(blk, past, along(shift, NT, 1), ALU.mult))
            rt(v.tensor_tensor(blk, blk, along(sh.const("expert"), NT, 1), ALU.add))
            rt(v.tensor_tensor(blk, blk, deep, ALU.add))
            rt(v.tensor_tensor(past, past, deep, ALU.add))
            rt(v.scalar_tensor_tensor(slot, past, -float(P), pos, ALU.mult, ALU.add))
            for k in range(TOP_E):
                rt(v.tensor_tensor(tmp[:, 5, :, :], hot[:, k, :, :], slot, ALU.mult))
                v.tensor_reduce(slotk[:, :, k], tmp[:, 5, :, :], AX.X, ALU.add)
                rt(v.tensor_tensor(tmp[:, 6, :, :], hot[:, k, :, :], blk, ALU.mult))
                rt(v.tensor_reduce(blkk[:, :, k], tmp[:, 6, :, :], AX.X, ALU.add))
            rt(v.scalar_tensor_tensor(rowf[:, :, :], blkk[:, :, :], float(P), slotk[:, :, :], ALU.mult, ALU.add))
            rt(v.tensor_copy(sh.rows[:, :, :], rowf[:, :, :]))
            for n in range(NR):
                i, k = divmod(n, TOP_E)
                if n >= 4:
                    v.wait_ge(ids_done, n - 3)
                v.tensor_scalar(Qh[:, n % 4, :], sh.const("slots"), slotk[:, i, k:k + 1], None, ALU.is_equal)
                v.tensor_scalar(Rh[:, n % 4, :], sh.const("blocks"), blkk[:, i, k:k + 1], sh.const("token")[:, i:i + 1], ALU.is_equal, ALU.mult).then_inc(hot_ready, 1)
            v.wait_ge(ids_done, NR)
            rt(v.tensor_copy(sh.ids[:, :], bank[2][:, 0:BLOCKS]))
            j_of = along(sh.const("blocks")[:, 0:EXTRA], N_EXP, 2)
            rt(v.tensor_tensor(ohx[:, 0, :, :], j_of, along(first, EXTRA, 1), ALU.is_ge))
            rt(v.tensor_tensor(ohx[:, 1, :, :], j_of, along(upto, EXTRA, 1), ALU.is_lt))
            rt(v.tensor_tensor(ohx[:, 0, :, :], ohx[:, 0, :, :], ohx[:, 1, :, :], ALU.mult))
            rt(v.tensor_tensor(ohx[:, 0, :, :], ohx[:, 0, :, :], along(sh.const("expert"), EXTRA, 1), ALU.mult))
            rt(v.tensor_reduce(xf[:, 0:EXTRA], ohx[:, 0, :, :], AX.X, ALU.add))
            rt(v.tensor_copy(xf[:, EXTRA:EXTRA + 1], upto[:, N_EXP - 1:N_EXP]))
            rt(v.tensor_copy(sh.extra[:, :], xf[0:1, :]))


def experts(nc, io, sh):
    NG, ND, RAW = KC, KC // 2, 4
    GH, DH, STAGE = 2 * NG, 2 * ND, 4
    STEP = GH + DH
    HB = 1024
    with ExitStack() as ctx:
        e = ctx.enter_context
        wg = e(nc.sbuf_tensor("w_gu_raw", [P, RAW, 2, HB], F32))
        wd = e(nc.sbuf_tensor("w_dn_raw", [P, RAW, 2, HB], F32))
        wh = e(nc.sbuf_tensor("w_high", [P, STAGE, HB], F32R))
        wl = e(nc.sbuf_tensor("w_low", [P, STAGE, HB], F32R))
        bias = e(nc.sbuf_tensor("bias_rows", [2 * N_EXP, 2 * FF + D], F32R))
        pick_g = e(nc.sbuf_tensor("pick_gu", [2 * N_EXP, P], F32R))
        pick_d = e(nc.sbuf_tensor("pick_dn", [2 * N_EXP, P], F32R))
        xh = e(nc.sbuf_tensor("xT_high", [P, KC, P], F32R))
        xl = e(nc.sbuf_tensor("xT_low", [P, KC, P], F32R))
        hh = e(nc.sbuf_tensor("hT_high", [P, KC, P], F32R))
        hl = e(nc.sbuf_tensor("hT_low", [P, KC, P], F32R))
        gt = e(nc.sbuf_tensor("gate_clamped", [P, FF], F32))
        sg = e(nc.sbuf_tensor("gate_sigmoid", [P, FF], F32))
        idb = e(nc.sbuf_tensor("id_block", [P, 1], I32))
        fence = e(nc.sbuf_tensor("fence", [1, 4], F32))
        xg, y, up = (sh.modb[:, k * D:(k + 1) * D] for k in range(3))
        ps_gu = e(nc.psum_tensor("ps_gu", [P, 4, 512], F32))
        ps_y = e(nc.psum_tensor("ps_y", [P, 2, 512], F32))
        ps_t = e(nc.psum_tensor("ps_t", [P, KC, P], F32))

        sem = sh.sem
        g_in = [sem(f"w_gu_in{n}") for n in range(RAW)]
        d_in = [sem(f"w_dn_in{n}") for n in range(RAW)]
        bias_in, bias_high, bias_ready = sem("expert_bias_in"), sem("expert_bias_high"), sem("expert_bias_ready")
        pg_ready, pd_ready, pg_used, pd_used = sem("pick_gu_ready"), sem("pick_dn_ready"), sem("pick_gu_used"), sem("pick_dn_used")
        high_ready, low_ready, half_used = sem("high_ready"), sem("low_ready"), sem("half_used")
        id_ready, x_in, x_turned, xh_ready, xl_ready = sem("id_ready"), sem("xg_in"), sem("xg_turned"), sem("xh_ready"), sem("xl_ready")
        gt_ready, up_ready, sg_ready, gs_ready, h_ready = sem("gt_ready"), sem("up_ready"), sem("sg_ready"), sem("gs_ready"), sem("h_ready")
        h_turned, hh_ready, hl_ready, y_ready, y_stored = sem("h_turned"), sem("hh_ready"), sem("hl_ready"), sem("y_ready"), sem("y_stored")
        fence_ready, fenced = sem("fence_ready"), sem("fenced")
        bias_raw = wd[0:2 * N_EXP, 0:2, :, :].rearrange("p r a n -> p (r a n)")[:, 0:2 * FF + D]
        w_gu = io["w_gu"][0].rearrange("e (c p) n -> e p c n", p=P)
        w_dn = io["w_dn"][0].rearrange("e (c a p) n -> e p c a n", p=P, a=2)

        def gate_at(b, extra=False):
            return (b + 1) * STEP if extra else b * STEP

        def down_at(b):
            return (b + 1) * STEP + GH

        def extra_count(eng):
            return eng.value_load(sh.extra[0:1, EXTRA:EXTRA + 1], min_val=0, max_val=EXTRA)

        LAST = N_EXP - 1
        block = e(nc.Block())

        @block.sync
        def _(sp):
            def load_gate(b, x, extra=False):
                first = isinstance(b, int) and b == 0
                for n in range(NG):
                    if n >= RAW:
                        sp.wait_ge(low_ready, gate_at(b, extra) + 2 * (n - RAW) + 2)
                    elif not first:
                        before = gate_at(b - 1, extra) if not (extra == "first") else gate_at(b - 1)
                        sp.wait_ge(low_ready, before + 2 * (n + NG - RAW) + 2)
                    sp.dma_start(wg[:, n % RAW, :, :].rearrange("p a n -> p (a n)"),
                                 w_gu[bass.ds(x, 1), :, n, :].rearrange("e p n -> (e p) n")).then_inc(g_in[n % RAW], 16)

            def load_down(b, x):
                first = isinstance(b, int) and b == 0
                if first:
                    sp.wait_ge(bias_ready, 1)
                for n in range(ND):
                    if not first:
                        sp.wait_ge(low_ready, down_at(b - 1) + 2 * n + 2)
                    sp.dma_start(wd[:, n, :, :], w_dn[bass.ds(x, 1), :, n, :, :].rearrange("e p a n -> (e p) a n")).then_inc(d_in[n], 16)

            for at in (0, N_EXP):
                sp.dma_start(bias_raw[at:at + N_EXP, 0:2 * FF], io["b_gu"][0]).then_inc(bias_in, 16)
                sp.dma_start(bias_raw[at:at + N_EXP, 2 * FF:2 * FF + D], io["b_dn"][0]).then_inc(bias_in, 16)
            load_gate(0, 0)
            load_gate(1, 1)
            load_down(0, 0)
            with sp.Fori(2, N_EXP) as b:
                load_gate(b, b)
                load_down(b - 1, b - 1)
            load_down(LAST, LAST)
            n = extra_count(sp)
            with sp.Fori(0, EXTRA) as j:
                with sp.If(j < n):
                    x = sp.value_load(sh.extra[0:1, bass.ds(j, 1)], min_val=0, max_val=N_EXP - 1)
                    load_gate(j + N_EXP, x, True)
                    load_down(j + N_EXP, x)

        @block.gpsimd
        def _(pool):
            def gather(b):
                pool.wait_ge(id_ready, b + 1)
                if not isinstance(b, int) or b > 0:
                    pool.wait_ge(x_turned, b)
                pool.tensor_tensor(fence[0:1, 0:1], fence[0:1, 1:2], fence[0:1, 2:3], ALU.add).then_inc(fenced, 1)
                pool.indirect_dma_start(xg, None, sh.u2_dram, bass.IndirectOffsetOnAxis(ap=idb[:, 0:1], axis=0)).then_inc(x_in, 16)

            pool.memset(fence[:, :], 0.0).then_inc(fence_ready, 1)
            pool.wait_ge(fence_ready, 1)
            gather(0)
            with pool.Fori(1, N_EXP + 1) as b:
                gather(b)
            n = extra_count(pool)
            with pool.Fori(0, EXTRA) as j:
                with pool.If(j < n):
                    gather(j + N_EXP + 1)

        @block.tensor
        def _(pe):
            ident = sh.const("ident")

            def turn_x(b):
                pe.wait_ge(x_in, b * 16 + 16)
                if not isinstance(b, int) or b > 1:
                    pe.wait_ge(hl_ready, b - 1)
                for j in range(KC):
                    last = pe.transpose(ps_t[:, j, :], xg[:, j * P:(j + 1) * P], ident)
                last.then_inc(x_turned, 1)

            def turn_h(b):
                pe.wait_ge(h_ready, b + 1)
                pe.wait_ge(xl_ready, b + 2)
                for j in range(KC):
                    last = pe.transpose(ps_t[:, j, :], up[:, j * P:(j + 1) * P], ident)
                last.then_inc(h_turned, 1)

            def three(out, ah, al, n, stage, stop):
                for a, w in ((ah, wh), (ah, wl), (al, wh)):
                    for q in range(2):
                        last = pe.matmul(out[:, q, :], a[:, n, :], w[:, stage, q * 512:(q + 1) * 512], start=False, stop=(stop and a is al))
                return last

            def gate(b, extra=False, gap=0):
                if not isinstance(b, int) or b > 0:
                    pe.wait_ge(up_ready, b)
                pe.wait_ge(pg_ready, b + 1)
                for q in range(4):
                    last = pe.matmul(ps_gu[:, q, :], pick_g[:, :], bias[:, q * 512:(q + 1) * 512], start=True, stop=False)
                last.then_inc(pg_used, 1)
                pe.wait_ge(xl_ready, b + 1)
                for k in range(GH):
                    pe.wait_ge(low_ready, gate_at(b, extra) + k + 1)
                    last = three(ps_gu[:, 2 * (k % 2):2 * (k % 2) + 2, :], xh, xl, k // 2, k % STAGE, k // 2 == NG - 1)
                    last.then_inc(half_used, 1 + (gap if k == GH - 1 else 0))
                turn_x(b + 1)

            def down(b, gap=0):
                pe.wait_ge(y_ready, b + 1)
                pe.wait_ge(pd_ready, b + 1)
                for q in range(2):
                    last = pe.matmul(ps_y[:, q, :], pick_d[:, :], bias[:, 2 * FF + q * 512:2 * FF + (q + 1) * 512], start=True, stop=False)
                last.then_inc(pd_used, 1)
                pe.wait_ge(hl_ready, b + 1)
                for k in range(DH):
                    pe.wait_ge(low_ready, down_at(b) + k + 1)
                    last = three(ps_y, hh, hl, k, k % STAGE, k == DH - 1)
                    last.then_inc(half_used, 1 + (gap if k == DH - 1 else 0))

            turn_x(0)
            gate(0, gap=DH)
            with pe.Fori(1, LAST) as b:
                turn_h(b - 1)
                gate(b)
                down(b - 1)
            turn_h(LAST - 1)
            gate(LAST)
            down(LAST - 1, gap=GH)
            turn_h(LAST)
            down(LAST)
            n = extra_count(pe)
            with pe.Fori(0, EXTRA) as j:
                with pe.If(j < n):
                    gate(j + N_EXP, True)
                    turn_h(j + N_EXP)
                    down(j + N_EXP)

        def raw_half(g, k):
            return (wg if g else wd)[:, k // 2 % RAW, k % 2, :]

        @block.scalar
        def _(act):
            def high(g, b, ks, extra=False, gap=0):
                at = gate_at(b, extra) if g else down_at(b)
                for k in ks:
                    if k % 2 == 0:
                        if g:
                            act.wait_ge(g_in[k // 2 % RAW], b * 32 + (16 if k // 2 < RAW else 32))
                        else:
                            act.wait_ge(d_in[k // 2], b * 16 + 16)
                    if not (isinstance(b, int) and b == 0 and g and k < STAGE):
                        act.wait_ge(half_used, at + k - STAGE + 1)
                    act.copy(wh[:, k % STAGE, :], raw_half(g, k)).then_inc(high_ready, 1 + (gap if k == ks[-1] else 0))

            def x_high(b):
                act.wait_ge(x_turned, b + 1)
                act.copy(xh[:, :, :], ps_t[:, :, :]).then_inc(xh_ready, 1)

            def h_high(b):
                act.wait_ge(h_turned, b + 1)
                act.copy(hh[:, :, :], ps_t[:, :, :]).then_inc(hh_ready, 1)

            def sigmoid(b):
                act.wait_ge(gt_ready, b + 1)
                act.activation(sg[:, :], gt[:, :], ACT.Sigmoid, scale=SWIGLU_ALPHA).then_inc(sg_ready, 1)

            def store(b, used):
                act.wait_ge(half_used, used)
                act.wait_ge(y_stored, b * 16 + 16)
                act.copy(y.rearrange("p (q n) -> p q n", q=2), ps_y[:, :, :]).then_inc(y_ready, 1)
                act.wait_ge(y_ready, b + 2)
                act.dma_start(sh.y_dram[bass.ds(b * P, P), :], y).then_inc(y_stored, 16)

            act.wait_ge(fence_ready, 1)
            act.copy(fence[0:1, 3:4], fence[0:1, 2:3]).then_inc(y_ready, 1)
            act.wait_ge(y_ready, 1)
            act.copy(fence[0:1, 3:4], fence[0:1, 2:3]).then_inc(y_stored, 16)
            x_high(0)
            high(True, 0, range(GH), gap=DH)
            x_high(1)
            sigmoid(0)
            high(True, 1, range(4))

            def main(b, tail):
                h_high(b - 1)
                high(True, b, range(4, GH))
                high(False, b - 1, range(4))
                x_high(b + 1)
                sigmoid(b)
                high(False, b - 1, range(4, DH), gap=0 if tail else GH)
                if tail:
                    high(True, b + 1, range(4))
                store(b - 1, (b + 1) * STEP)

            with act.Fori(1, LAST) as b:
                main(b, True)
            main(LAST, False)
            h_high(LAST)
            high(False, LAST, range(DH))
            store(LAST, (LAST + 2) * STEP)
            n = extra_count(act)
            with act.Fori(0, EXTRA) as j:
                with act.If(j < n):
                    b = j + N_EXP
                    high(True, b, range(GH), True)
                    high(False, b, range(4))
                    x_high(b + 1)
                    sigmoid(b)
                    h_high(b)
                    high(False, b, range(4, DH))
                    store(b, (b + 2) * STEP)
            act.wait_ge(y_stored, (n + N_EXP + 1) * 16)
            act.copy(fence[0:1, 3:4], fence[0:1, 2:3])

        @block.vector
        def _(v):
            def ids(b):
                if not isinstance(b, int) or b > 0:
                    v.wait_ge(x_in, b * 16)
                    v.wait_ge(fenced, b)
                v.tensor_copy(idb[:, :], sh.ids[:, bass.ds(b, 1)]).then_inc(id_ready, 1)

            def low(g, b, ks, extra=False, gap=0):
                at = gate_at(b, extra) if g else down_at(b)
                for k in ks:
                    v.wait_ge(high_ready, at + k + 1)
                    v.tensor_tensor(wl[:, k % STAGE, :], raw_half(g, k), wh[:, k % STAGE, :].bitcast(F32), ALU.subtract).then_inc(
                        low_ready, 1 + (gap if k == ks[-1] else 0))

            def x_low(b):
                v.wait_ge(xh_ready, b + 1)
                v.tensor_tensor(xl[:, :, :], ps_t[:, :, :], xh[:, :, :].bitcast(F32), ALU.subtract).then_inc(xl_ready, 1)

            def h_low(b):
                v.wait_ge(hh_ready, b + 1)
                v.tensor_tensor(hl[:, :, :], ps_t[:, :, :], hh[:, :, :].bitcast(F32), ALU.subtract).then_inc(hl_ready, 1)

            def clamp(b, used):
                v.wait_ge(half_used, used)
                if not isinstance(b, int) or b > 0:
                    v.wait_ge(h_turned, b)
                halves = ps_gu[:, :, :].rearrange("p q (n two) -> p q n two", two=2)
                v.tensor_scalar(gt[:, :].rearrange("p (q n) -> p q n", q=4), halves[:, :, :, 0], LIMIT, None, ALU.min).then_inc(gt_ready, 1)
                v.tensor_scalar(up.rearrange("p (q n) -> p q n", q=4), halves[:, :, :, 1], LIMIT, -LIMIT, ALU.min, ALU.max).then_inc(up_ready, 1)

            def hidden(b):
                v.wait_ge(sg_ready, b + 1)
                v.tensor_tensor(sg[:, :], gt[:, :], sg[:, :], ALU.mult).then_inc(gs_ready, 1)
                v.wait_ge(gs_ready, b + 1)
                v.wait_ge(up_ready, b + 1)
                v.scalar_tensor_tensor(up, up, 1.0, sg[:, :], ALU.add, ALU.mult).then_inc(h_ready, 1)

            def pick(g, b, x):
                if not isinstance(b, int) or b > 0:
                    v.wait_ge(pg_used if g else pd_used, b)
                p, ready = (pick_g, pg_ready) if g else (pick_d, pd_ready)
                v.tensor_scalar(p[:, :], sh.const("ones")[0:2 * N_EXP, :], sh.const("picks")[0:2 * N_EXP, bass.ds(x, 1)],
                                None, ALU.mult).then_inc(ready, 1)

            ids(0)
            v.wait_ge(bias_in, 64)
            v.tensor_copy(bias[:, :], bias_raw).then_inc(bias_high, 1)
            v.wait_ge(bias_high, 1)
            v.tensor_tensor(bias[N_EXP:2 * N_EXP, :], bias_raw[N_EXP:2 * N_EXP, :], bias[N_EXP:2 * N_EXP, :].bitcast(F32), ALU.subtract).then_inc(bias_ready, 1)
            v.wait_ge(bias_ready, 1)
            pick(True, 0, 0)
            pick(False, 0, 0)
            x_low(0)
            ids(1)
            low(True, 0, range(GH), gap=DH)
            clamp(0, STEP)
            x_low(1)
            hidden(0)
            low(True, 1, range(4))

            def main(b, tail):
                ids(b + 1)
                pick(True, b, b)
                h_low(b - 1)
                low(True, b, range(4, GH))
                low(False, b - 1, range(4))
                clamp(b, gate_at(b) + GH)
                x_low(b + 1)
                pick(False, b, b)
                low(False, b - 1, range(4, 6))
                hidden(b)
                low(False, b - 1, range(6, DH), gap=0 if tail else GH)
                if tail:
                    low(True, b + 1, range(4))

            with v.Fori(1, LAST) as b:
                main(b, True)
            main(LAST, False)
            h_low(LAST)
            low(False, LAST, range(DH))
            n = extra_count(v)
            with v.Fori(0, EXTRA) as j:
                with v.If(j < n):
                    b = j + N_EXP
                    x = v.value_load(sh.extra[0:1, bass.ds(j, 1)], min_val=0, max_val=N_EXP - 1)
                    ids(b + 1)
                    pick(True, b, x)
                    pick(False, b, x)
                    low(True, b, range(GH), True)
                    low(False, b, range(4))
                    clamp(b, gate_at(b, True) + GH)
                    x_low(b + 1)
                    hidden(b)
                    h_low(b)
                    low(False, b, range(4, DH))


def finish(nc, io, sh):
    NY = 8
    with ExitStack() as ctx:
        e = ctx.enter_context
        ln = e(nc.sbuf_tensor("ln2_rows", [P, 2, D], F32))
        yk = e(nc.sbuf_tensor("y_gathered", [P, NY, D], F32))
        acc = e(nc.sbuf_tensor("ffn", [P, NT, D], F32))
        st = e(nc.sbuf_tensor("ln2_stats", [P, NT, 16], F32))
        sem = sh.sem
        l_in, y_in, y_used, step, var_ready, root_ready, o_ready, o_stored = (sem("ln2_in"), [sem(f"yk_in{n}") for n in range(NY)], sem("yk_used"), sem("ln2_step"),
                                                                             sem("ln2_var"), sem("ln2_root"), sem("out_ready"), sem("out_stored"))
        block = e(nc.Block())

        @block.sync
        def _(sp):
            sp.dma_start(ln[:, 0, :], io["ln2_g"].broadcast_to([P, D])).then_inc(l_in, 16)
            sp.dma_start(ln[:, 1, :], io["ln2_b"].broadcast_to([P, D])).then_inc(l_in, 16)
            for i in range(NT):
                sp.wait_ge(o_ready, i + 1)
                sp.dma_start(io["out"][0, i * P:(i + 1) * P, :], acc[:, i, :]).then_inc(o_stored, 16)
            sp.wait_ge(o_stored, 16 * NT)

        @block.gpsimd
        def _(pool):
            for n in range(NT * TOP_E):
                i, k = divmod(n, TOP_E)
                if n >= NY:
                    pool.wait_ge(y_used, n - NY + 1)
                pool.indirect_dma_start(yk[:, n % NY, :], None, sh.y_dram, bass.IndirectOffsetOnAxis(ap=sh.rows[:, i, k:k + 1], axis=0)).then_inc(y_in[n % NY], 16)

        @block.scalar
        def _(act):
            for i in range(NT):
                act.wait_ge(var_ready, i + 1)
                act.activation(st[:, i, 14:15], st[:, i, 13:14], ACT.Sqrt, bias=sh.const("eps")[:, 1:2]).then_inc(root_ready, 1)

        @block.vector
        def _(v):
            count = [0]

            def link(ins):
                ins.then_inc(step, 1)
                count[0] += 1
                v.wait_ge(step, count[0])

            v.wait_ge(l_in, 32)
            for i in range(NT):
                a = acc[:, i, :]
                for k in range(TOP_E):
                    n = i * TOP_E + k
                    v.wait_ge(y_in[n % NY], 16 * (n // NY + 1))
                    g = sh.gate[:, i, k:k + 1]
                    if k == 0:
                        v.tensor_scalar(a, yk[:, n % NY, :], g, None, ALU.mult).then_inc(y_used, 1)
                    else:
                        v.scalar_tensor_tensor(a, yk[:, n % NY, :], g, a, ALU.mult, ALU.add).then_inc(y_used, 1)
                    v.wait_ge(y_used, n + 1)
                link(v.tensor_tensor(a, a, sh.modb[:, 3 * D:4 * D], ALU.mult))
                link(v.scalar_tensor_tensor(a, sh.x_tm[:, i, :], ALPHA, a, ALU.mult, ALU.add))
                v.bn_stats(st[:, i, 0:6], a[:, 0:512])
                link(v.bn_stats(st[:, i, 6:12], a[:, 512:D]))
                v.bn_aggr(st[:, i, 12:14], st[:, i, 0:12].rearrange("p (a b) -> p a b", b=6)).then_inc(var_ready, 1)
                v.wait_ge(root_ready, i + 1)
                link(v.reciprocal(st[:, i, 15:16], st[:, i, 14:15]))
                link(v.tensor_scalar(a, a, st[:, i, 12:13], st[:, i, 15:16], ALU.subtract, ALU.mult))
                link(v.tensor_tensor(a, a, ln[:, 0, :], ALU.mult))
                v.tensor_tensor(a, a, ln[:, 1, :], ALU.add).then_inc(o_ready, 1)


INPUTS = ["x", "c", "w_ada", "b_ada", "w_in", "shift_mu", "rwkv_w0", "rwkv_w2", "rwkv_a0", "rwkv_a2", "rwkv_g2",
          "rwkv_k_k", "rwkv_k_a", "rwkv_r_k", "rwkv_ln_w", "rwkv_ln_b", "mla_q_norm", "mla_w_q_up",
          "mla_kv_norm", "mla_w_uk", "mla_w_uv", "idx_w_q", "idx_ln_g", "idx_ln_b", "w_out", "ln1_g", "ln1_b",
          "w_router", "b_router", "w_gu", "b_gu", "w_dn", "b_dn", "ln2_g", "ln2_b"]


def build(nc, io, stages=5):
    with ExitStack() as ctx:
        e = ctx.enter_context
        sh = Shared()
        live = []

        def new_semaphore(name):
            live.append(nc.alloc_semaphore(name=name))
            return live[-1]

        def clear_semaphores():
            nc.clear_and_free_semaphores(live)
            live.clear()
            nc.all_engine_barrier()

        sh.sem = new_semaphore
        sh.cst = e(nc.sbuf_tensor("consts_sb", [P, N_CONST], F32))
        sh.cols = e(nc.sbuf_tensor("cols", [P, N_VEC], F32))
        sh.x_tm = e(nc.sbuf_tensor("x_tm", [P, NT, D], F32))
        sh.modb = e(nc.sbuf_tensor("modb", [P, 4 * D], F32))
        sh.const = lambda n: sh.cst[:, CONST[n][0]:CONST[n][0] + CONST[n][1]]
        sh.col = lambda n, i: sh.cols[:, VEC[n][0] + i:VEC[n][0] + i + 1]
        sh.gate = e(nc.sbuf_tensor("gate", [P, NT, TOP_E], F32))
        sh.rows = e(nc.sbuf_tensor("rows", [P, NT, TOP_E], I32))
        sh.ids = e(nc.sbuf_tensor("ids", [P, BLOCKS], I32))
        sh.extra = e(nc.sbuf_tensor("extra", [1, EXTRA + 1], I32))
        sh.u2_dram = nc.dram_tensor("u2_dram", (S, D), F32, kind="Internal").ap()
        sh.y_dram = nc.dram_tensor("y_dram", ((BLOCKS - 1) * P, D), F32, kind="Internal").ap()
        mixing = ctx.enter_context(ExitStack())
        sh.cat = mixing.enter_context(nc.sbuf_tensor("cat_tm", [P, NT, D], F32))
        with ExitStack() as front:
            sh.pT = front.enter_context(nc.sbuf_tensor("pT", [P, COL_TILES, S], F32))
            project(nc, io, sh)
            if stages >= 2:
                attend(nc, io, sh)
            if stages >= 3:
                sh.b_hat = front.enter_context(nc.sbuf_tensor("b_hat", [P, NPAIR, S], F32))
                sh.v_tm = front.enter_context(nc.sbuf_tensor("v_tm", [P, NT, D_GROUP], F32))
                sh.gate_sig = front.enter_context(nc.sbuf_tensor("gate_sig", [P, S], F32))
                sh.w_end = front.enter_context(nc.sbuf_tensor("w_end", [P, NPAIR, NCH], F32))
                sh.bonus = front.enter_context(nc.sbuf_tensor("bonus", [P, NT, HEADS], F32))
                prepare(nc, io, sh)
                scan(nc, io, sh)
                clear_semaphores()
        if stages >= 4:
            route(nc, io, sh)
        mixing.close()
        if stages >= 5:
            experts(nc, io, sh)
            finish(nc, io, sh)


def kernel(**inputs):
    import concourse.bacc as bacc
    from concourse.bass_utils import run_bass_kernel_spmd

    nc = bacc.Bacc("TRN2", target_bir_lowering=False, num_devices=1)
    arrays, io = {}, {}
    for name in INPUTS:
        a = np.ascontiguousarray(inputs[name])
        arrays[f"{name}_dram"] = a
        io[name] = nc.dram_tensor(f"{name}_dram", a.shape, mybir.dt.from_np(a.dtype), kind="ExternalInput").ap()
    arrays["consts_dram"] = CONST_ARRAY
    io["consts"] = nc.dram_tensor("consts_dram", CONST_ARRAY.shape, F32, kind="ExternalInput").ap()
    io["out"] = nc.dram_tensor("out_dram", (1, S, D), F32, kind="ExternalOutput").ap()
    build(nc, io)
    r = run_bass_kernel_spmd(nc, [arrays], core_ids=[0])
    return r.results[0]["out_dram"]
```

```python
from contextlib import ExitStack, nullcontext

import numpy as np

import concourse.bass as bass
from concourse import mybir

F32 = mybir.dt.float32
F32R = mybir.dt.float32r
I32 = mybir.dt.int32
BF16 = mybir.dt.bfloat16
ALU = mybir.AluOpType
ACT = mybir.ActivationFunctionType
AX = mybir.AxisListType

P = 128
D = 1024
S = 512
NT = S // P
KC = D // P
C = 64
NCH = S // C
HEADS = 8
D_GROUP = HEADS * C
NPAIR = D_GROUP // P
Q_LORA, KV_LORA, IDX_DIM = 256, 128, 64
N_SHIFT = 3 * D_GROUP + 64 + 64 + 128
N_IN = N_SHIFT + Q_LORA + KV_LORA + IDX_DIM + HEADS
SHIFT_TILES = N_SHIFT // P
COL_TILES = -(-N_IN // P)
TOPK = min(256, S // 4)
N_EXP = 32
TOP_E = 4
FF = 1024
EXTRA = (S * TOP_E // (S - P + 1)) * (S // P - 1)
EARLY = 6
BLOCKS = N_EXP + EXTRA + 1
NEG = -1e30
TAKEN = -3e38
DECAY = float(np.exp(-0.5))
LEVELS = (4, 8, 16, 32, 64)
GN_EPS = 64e-5
LIMIT, SWIGLU_ALPHA = 7.0, 1.702
ALPHA = 2.0 ** 0.25
SLOPES = [2.0 ** (-8.0 * (h + 1) / HEADS) for h in range(HEADS)]

VEC = {}
_at = 0
for _n, _k in (("c", 8), ("shift_mu", 14), ("rwkv_w0", 4), ("rwkv_a0", 4), ("rwkv_k_k", 4),
               ("rwkv_k_a", 4), ("rwkv_r_k", 4), ("mla_q_norm", 2), ("mla_kv_norm", 1),
               ("idx_ln_g", 1), ("idx_ln_b", 1)):
    VEC[_n] = (_at, _k)
    _at += _k
N_VEC = _at

CONST = {}


def _constants():
    p = np.arange(P)[:, None]
    j = np.arange(P)[None, :]
    half = p // C == j // C
    s512 = np.arange(S)[None, :]
    parts = [("strict", half & (p < j)), ("incl", half & (p <= j)),
             ("low2", (p == j + 1) & (j % 2 == 0)), ("up2", (j == p + 1) & (p % 2 == 0))]
    for n in LEVELS:
        parts.append((f"lev{n}", (p // n == j // n) & (p // (n // 2) != j // (n // 2)) & (p < j)))
    parts += [("half", half), ("before", p < j),
              ("slots", np.broadcast_to(j, (P, P))),
              ("causal", np.where(j <= p, 0.0, NEG)),
              ("dist", np.broadcast_to(s512, (P, S)) - p),
              ("keep", np.broadcast_to(s512 % C != 0, (P, S))),
              ("heads", p // C == np.arange(2)[None, :]),
              ("ident", p == j), ("ones", np.ones((P, P))),
              ("blocks", np.broadcast_to(np.arange(BLOCKS)[None, :], (P, BLOCKS))),
             ("token", p + 0 * np.arange(NT)[None, :] + P * np.arange(NT)[None, :]),
             ("expert", np.broadcast_to(np.arange(N_EXP)[None, :], (P, N_EXP))),
             ("picks", p % N_EXP == np.arange(N_EXP)[None, :]),
             ("eps", np.broadcast_to(np.array([[1e-6, 1e-5, GN_EPS]]), (P, 3)))]
    at = 0
    for name, a in parts:
        CONST[name] = (at, a.shape[1])
        at += a.shape[1]
    return np.concatenate([np.asarray(a, np.float32) for _, a in parts], 1)


CONST_ARRAY = _constants()
N_CONST = CONST_ARRAY.shape[1]


class Shared:
    pass


def psum_banks(nc, e, tag):
    return [e(nc.psum_tensor(f"{tag}_bank{i}", [P, 512], F32)) for i in range(8)]


def project(nc, io, sh):
    RING = 8
    HALF = 1024
    GT = 2
    W_GROUPS = [(at, min(GT * P, N_IN - at)) for at in range(0, N_IN, GT * P)]
    WBUF = 3
    with ExitStack() as ctx:
        e = ctx.enter_context
        uh = e(nc.sbuf_tensor("uT_high", [P, KC, S], F32R))
        ul = e(nc.sbuf_tensor("uT_low", [P, KC, S], F32R))
        wh = e(nc.sbuf_tensor("w_in_high", [P, 2, KC, P], F32R))
        wl = e(nc.sbuf_tensor("w_in_low", [P, 2, KC, P], F32R))
        win = e(nc.sbuf_tensor("w_in_sb", [P, WBUF, KC, GT * P], F32))
        ada = sh.w_out
        rows = e(nc.sbuf_tensor("vec_rows", [N_VEC, P], F32))
        c_act = e(nc.sbuf_tensor("c_act", [P, KC], F32))
        sig_c = e(nc.sbuf_tensor("sig_c", [P, KC], F32))
        mod1 = e(nc.sbuf_tensor("mod1", [P, 2 * KC], F32))
        room = sh.cat[:, :, :].rearrange("p a b -> p (a b)")
        praw = room[:, 0:2 * (S + 1)].rearrange("p (a b) -> p a b", a=2)
        pdif = room[:, 3 * S:5 * S].rearrange("p (a b) -> p a b", a=2)
        ut = room[:, 5 * S:7 * S].rearrange("p (a b) -> p a b", a=2)
        bank = psum_banks(nc, e, "project")
        ps_vec, ps_mod = bank[0], bank[1]
        ps_x, ps_p = bank[2:4], bank[4:8]
        acc0 = sh.pT[:, 0:4, :].rearrange("p a b -> p (a b)")
        accs = [acc0, sh.modb[:, 0:2048], sh.modb[:, 2048:4096]]
        cst, cols = sh.cst, sh.cols

        sem = sh.sem
        late_in = sem("late_consts_in")
        consts_in, vec_in, x_in, bias_in = sem("consts_in"), sem("vec_in"), sem("x_in"), sem("bias_in")
        ada_in = [sem(f"ada_in{i}") for i in range(RING)]
        win_in = [sem(f"win_in{i}") for i in range(WBUF)]
        acc_zero, ada_used, acc_done = sem("acc_zero"), sem("ada_used"), sem("acc_done")
        vec_turned, cols_ready, sig_ready, c_ready = sem("vec_turned"), sem("cols_ready"), sem("sig_ready"), sem("c_ready")
        ul_ready, uh_ready, wh_ready, wl_ready = sem("ul_ready"), sem("uh_ready"), sem("w_in_high_ready"), sem("w_in_low_ready")
        x_turned, uT_ready, mod1_summed, mod1_ready = sem("x_turned"), sem("uT_ready"), sem("mod1_summed"), sem("mod1_ready")
        p_done, p_copied, p_shifted, p_diff = sem("p_done"), sem("p_copied"), sem("p_shifted"), sem("p_diff")
        mod_summed, mod_copied, edge_zero = sem("mod_summed"), sem("mod_copied"), sem("edge_zero")

        w_ada = io["w_ada"][0].rearrange("(c p) n -> p c n", p=P)
        w_in = io["w_in"][0].rearrange("(c p) n -> p c n", p=P)
        N_G = KC * 2
        def win_group(eng, g):
            at, n = W_GROUPS[g]
            if g >= WBUF:
                eng.wait_ge(wl_ready, GT * (g - WBUF + 1))
            eng.dma_start(win[:, g % WBUF, :, 0:n], w_in[:, :, at:at + n]).then_inc(win_in[g % WBUF], 16)

        block = e(nc.Block())

        @block.sync
        def _(sp):
            early = CONST["ident"][0]
            sp.dma_start(cst[:, early:], io["consts"][:, early:]).then_inc(consts_in, 16)
            for name, (r, k) in VEC.items():
                src = io[name]
                if name == "rwkv_r_k":
                    sp.dma_start(rows[r:r + k, :], src.rearrange("o (r a) d -> (o r) (a d)", a=2)).then_inc(vec_in, 16)
                    continue
                if k * P > src.shape[1]:
                    sp.dma_start(rows[r:r + 1, 0:C], src).then_inc(vec_in, 16)
                    sp.dma_start(rows[r:r + 1, C:P], src).then_inc(vec_in, 16)
                    continue
                sp.dma_start(rows[r:r + k, :], src.rearrange("o (r d) -> (o r) d", d=P)).then_inc(vec_in, 16)
            sp.wait_ge(acc_zero, 1)
            sp.dma_start(acc0[0:1, :], io["b_ada"][:, 0:2048]).then_inc(bias_in, 16)

            def ada_piece(n):
                g, k = divmod(n, N_G)
                if n >= RING:
                    sp.wait_ge(ada_used, n - RING + 1)
                sp.dma_start(ada[:, n % RING, :],
                             w_ada[:, k // 2, g * 2048 + (k % 2) * HALF:g * 2048 + (k % 2 + 1) * HALF]).then_inc(ada_in[n % RING], 16)

            for n in range(N_G):
                ada_piece(n)
                if n % 4 == 3:
                    i = n // 4
                    sp.dma_start(sh.x_tm[:, i, :], io["x"][0, i * P:(i + 1) * P, :]).then_inc(x_in, 16)
            win_group(sp, 0)
            sp.dma_start(cst[:, 0:early], io["consts"][:, 0:early]).then_inc(late_in, 16)
            for g in range(1, WBUF):
                win_group(sp, g)
            sp.wait_ge(acc_zero, 3)
            for g in (1, 2):
                sp.dma_start(accs[g][0:1, :], io["b_ada"][:, g * 2048:(g + 1) * 2048]).then_inc(bias_in, 16)
            for n in range(N_G, 3 * N_G):
                ada_piece(n)
            sp.wait_ge(late_in, 16)

        @block.tensor
        def _(pe):
            ident = sh.const("ident")
            pe.wait_ge(consts_in, 16)
            pe.wait_ge(vec_in, 16 * (len(VEC) + 2))
            pe.transpose(ps_vec[:, 0:N_VEC], rows[:, :], ident[0:N_VEC, 0:N_VEC]).then_inc(vec_turned, 1)
            for c in range(KC):
                if c == 0:
                    pe.wait_ge(x_in, 16 * NT)
                if c >= 2:
                    pe.wait_ge(uT_ready, c - 1)
                for i in range(NT):
                    last = pe.transpose(ps_x[c % 2][:, i * P:(i + 1) * P], sh.x_tm[:, i, c * P:(c + 1) * P], ident)
                last.then_inc(x_turned, 1)
                if c == 1:
                    pe.wait_ge(acc_done, 1)
                    for k in range(2 * KC):
                        last = pe.matmul(ps_mod[:, k:k + 1], acc0[:, k * P:(k + 1) * P], sh.const("ones")[:, 0:1], start=True, stop=True)
                    last.then_inc(mod1_summed, 1)

            def mod_rows(g):
                pe.wait_ge(acc_done, g + 1)
                for k in range(4):
                    if (g, k) != (1, 0):
                        pe.wait_ge(mod_copied, 4 * (g - 1) + k)
                    pe.matmul(ps_mod[:, :], sh.const("ones"), accs[g][:, k * 512:(k + 1) * 512],
                              start=True, stop=True).then_inc(mod_summed, 1)

            pe.wait_ge(mod1_ready, 1)
            for j in range(COL_TILES):
                g = j // 4
                m = min(P, N_IN - j * P)
                pe.wait_ge(wl_ready, j + 1)
                if j >= 4:
                    pe.wait_ge(p_copied, j - 3)
                for c in range(KC):
                    if j == 0:
                        pe.wait_ge(ul_ready, c + 1)
                    for w, u in ((wh, uh), (wh, ul), (wl, uh)):
                        last = pe.matmul(ps_p[j % 4][0:m, :], w[:, j % 2, c, 0:m], u[:, c, :],
                                         start=(c == 0 and w is wh and u is uh), stop=(c == KC - 1 and w is wl))
                last.then_inc(p_done, 1)
                if j == 11:
                    mod_rows(1)
            mod_rows(2)

        def copy_mod(act, g):
            for k in range(4):
                act.wait_ge(mod_summed, 4 * (g - 1) + k + 1)
                act.copy(accs[g][:, k * 512:(k + 1) * 512], ps_mod[:, :]).then_inc(mod_copied, 1)

        @block.scalar
        def _(act):
            act.wait_ge(cols_ready, 1)
            act.activation(sig_c[:, :], cols[:, 0:KC], ACT.Sigmoid).then_inc(sig_ready, 1)

            def high(j):
                g = j // GT
                m = min(P, N_IN - j * P)
                if j % GT == 0:
                    act.wait_ge(win_in[g % WBUF], 16 * (g // WBUF + 1))
                if j >= 2:
                    act.wait_ge(p_done, j - 1)
                act.copy(wh[:, j % 2, :, 0:m], win[:, g % WBUF, :, (j % GT) * P:(j % GT) * P + m]).then_inc(wh_ready, 1)

            high(0)
            high(1)
            act.wait_ge(mod1_ready, 1)
            for c in range(KC):
                act.wait_ge(x_turned, c + 1)
                if c >= 2:
                    act.wait_ge(ul_ready, c - 1)
                act.activation(ut[:, c % 2, :], ps_x[c % 2][:, :], ACT.Identity, bias=mod1[:, c:c + 1],
                               scale=mod1[:, KC + c:KC + c + 1]).then_inc(uT_ready, 1)
                act.wait_ge(uT_ready, c + 1)
                act.copy(uh[:, c, :], ut[:, c % 2, :]).then_inc(uh_ready, 1)
            act.wait_ge(edge_zero, 1)
            for j in range(COL_TILES):
                m = min(P, N_IN - j * P)
                act.wait_ge(p_done, j + 1)
                if j < SHIFT_TILES:
                    if j >= 2:
                        act.wait_ge(p_shifted, j - 1)
                    act.copy(praw[0:m, j % 2, 1:S + 1], ps_p[j % 4][0:m, :]).then_inc(p_copied, 1)
                else:
                    act.copy(sh.pT[0:m, j, :], ps_p[j % 4][0:m, :]).then_inc(p_copied, 1)
                if j + 2 < COL_TILES:
                    high(j + 2)
                if j % GT == GT - 1 and WBUF + j // GT < len(W_GROUPS):
                    win_group(act, WBUF + j // GT)
                if j == 11:
                    copy_mod(act, 1)
            copy_mod(act, 2)

        @block.gpsimd
        def _(pool):
            for j in range(COL_TILES):
                m = min(P, N_IN - j * P)
                pool.wait_ge(wh_ready, j + 1)
                pool.tensor_tensor(wl[:, j % 2, :, 0:m], win[:, j // GT % WBUF, :, (j % GT) * P:(j % GT) * P + m],
                                   wh[:, j % 2, :, 0:m].bitcast(F32), ALU.subtract).then_inc(wl_ready, 1)

        @block.vector
        def _(v):
            v.memset(acc0, 0.0).then_inc(acc_zero, 1)
            v.wait_ge(vec_turned, 1)
            v.tensor_copy(cols[:, 0:N_VEC], ps_vec[:, 0:N_VEC]).then_inc(cols_ready, 1)
            v.wait_ge(sig_ready, 1)
            v.wait_ge(cols_ready, 1)
            v.tensor_tensor(c_act[:, :], cols[:, 0:KC], sig_c[:, :], ALU.mult).then_inc(c_ready, 1)
            v.wait_ge(c_ready, 1)

            def gather_mod(g, k):
                n = g * N_G + k
                if k == 0:
                    v.wait_ge(bias_in, 16 * (1 if g == 0 else 3))
                v.wait_ge(ada_in[n % RING], 16 * (n // RING + 1))
                if k >= 2:
                    v.wait_ge(ada_used, n - 1)
                a = accs[g][:, (k % 2) * HALF:(k % 2 + 1) * HALF]
                v.scalar_tensor_tensor(a, ada[:, n % RING, :], c_act[:, k // 2:k // 2 + 1], a, ALU.mult, ALU.add).then_inc(ada_used, 1)
                if k == N_G - 1:
                    v.wait_ge(ada_used, n + 1)
                    v.engine_nop().then_inc(acc_done, 1)

            for k in range(N_G):
                gather_mod(0, k)
            v.memset(accs[1], 0.0).then_inc(acc_zero, 1)
            v.memset(accs[2], 0.0).then_inc(acc_zero, 1)
            v.memset(praw[:, :, 0:1], 0.0).then_inc(edge_zero, 1)
            v.wait_ge(mod1_summed, 1)
            v.tensor_copy(mod1[:, 0:KC], ps_mod[:, 0:KC])
            v.tensor_scalar(mod1[:, KC:2 * KC], ps_mod[:, KC:2 * KC], 1.0, None, ALU.add).then_inc(mod1_ready, 1)
            for c in range(KC):
                v.wait_ge(uh_ready, c + 1)
                v.tensor_tensor(ul[:, c, :], ut[:, c % 2, :], uh[:, c, :].bitcast(F32), ALU.subtract).then_inc(ul_ready, 1)

            k = 0
            for j in range(SHIFT_TILES):
                while k < 2 * N_G and k < 3 * (j + 2):
                    gather_mod(1 + k // N_G, k % N_G)
                    k += 1
                v.wait_ge(p_copied, j + 1)
                raw = praw[:, j % 2, :]
                v.tensor_tensor(pdif[:, j % 2, :], raw[:, 0:S], raw[:, 1:S + 1], ALU.subtract).then_inc(p_diff, 1)
                v.wait_ge(p_diff, j + 1)
                mu = sh.col("shift_mu", j)
                v.scalar_tensor_tensor(sh.pT[:, j, :], pdif[:, j % 2, :], mu, raw[:, 1:S + 1], ALU.mult, ALU.add).then_inc(p_shifted, 1)


def attend(nc, io, sh):
    UNITS = [(i, h) for i in range(NT) for h in range(HEADS)]
    SCALE = C ** -0.5
    with ExitStack() as ctx:
        e = ctx.enter_context
        wq = e(nc.sbuf_tensor("w_q_up_sb", [P, 2, D_GROUP], F32))
        wi = e(nc.sbuf_tensor("idx_w_q_sb", [P, 2, D_GROUP], F32))
        wuk = e(nc.sbuf_tensor("w_uk_sb", [P, NPAIR, KV_LORA], F32))
        wuv = e(nc.sbuf_tensor("w_uv_sb", [P, HEADS, C], F32))
        sq = e(nc.sbuf_tensor("squares", [P, 3, S], F32))
        root = e(nc.sbuf_tensor("roots", [P, 3, S], F32))
        q_lat = e(nc.sbuf_tensor("q_lat", [P, 2, S], F32))
        c_lat = e(nc.sbuf_tensor("c_lat", [P, S], F32))
        c_tm = e(nc.sbuf_tensor("c_tm", [P, NT, KV_LORA], F32))
        ikd = e(nc.sbuf_tensor("ik_centred", [C, 2, S], F32))
        ik = e(nc.sbuf_tensor("ik", [P, S], F32))
        iw = e(nc.sbuf_tensor("iw_tm", [P, NT, HEADS], F32))
        qT = e(nc.sbuf_tensor("qT", [P, NPAIR, S], F32))
        q_abs = e(nc.sbuf_tensor("q_abs", [P, HEADS, S], F32))
        iqT = q_abs[:, NPAIR:2 * NPAIR, :]
        relu = e(nc.sbuf_tensor("relu", [P, 2, S], F32))
        score = e(nc.sbuf_tensor("score", [P, NT, S], F32))
        best = e(nc.sbuf_tensor("best8", [P, NT, 8], F32))
        logit = relu
        prob, probT = sq[:, 0:2, :], root[:, 0:2, :]
        o_lat = e(nc.sbuf_tensor("o_lat", [P, 2, P], F32))
        stat = e(nc.sbuf_tensor("softmax_stats", [P, 4, NT * HEADS], F32))
        bank = psum_banks(nc, e, "attend")

        sem = sh.sem
        aw_in = sem("attend_w_in")
        squared, summed, rooted, rinv_ready = sem("squared"), sem("summed"), sem("rooted"), sem("rinv_ready")
        lat_ready, ik_step, ik_ready, iw_turned, iw_ready = sem("lat_ready"), sem("ik_step"), sem("ik_ready"), sem("iw_turned"), sem("iw_ready")
        q_done, q_copied, qa_done, qa_copied = sem("q_done"), sem("q_copied"), sem("qa_done"), sem("qa_copied")
        c_turned, c_copied = sem("c_turned"), sem("c_copied")
        idx_done, relu_ready, score_added = sem("idx_done"), sem("relu_ready"), sem("score_added")
        top_step, bias_ready = sem("top_step"), sem("bias_ready")
        sh.w_out_in = sem("w_out_in")
        zeros_ready, y_zeroed = sem("zeros_ready"), sem("y_zeroed")
        zeros = relu[:, :, :].rearrange("p a b -> p (a b)")
        l_done, l_ready, nmax_ready, prob_ready, prob_turned = sem("l_done"), sem("l_ready"), sem("nmax_ready"), sem("prob_ready"), sem("prob_turned")
        probT_ready, pv_done, olat_ready, o_done, o_ready, rsum_ready = sem("probT_ready"), sem("pv_done"), sem("olat_ready"), sem("o_done"), sem("o_ready"), sem("rsum_ready")
        Q0, KV0, IK0 = SHIFT_TILES, SHIFT_TILES + 2, SHIFT_TILES + 3
        half = lambda h: slice(C * (h % 2), C * (h % 2) + C)
        idx_units = [(i, h) for i in range(1, NT) for h in range(HEADS)]
        block = e(nc.Block())

        @block.sync
        def _(sp):
            sp.dma_start(wq[:, :, :], io["mla_w_q_up"][0].rearrange("(c p) n -> p c n", p=P)).then_inc(aw_in, 16)
            sp.dma_start(wi[:, :, :], io["idx_w_q"][0].rearrange("(c p) n -> p c n", p=P)).then_inc(aw_in, 16)
            sp.dma_start(wuk[:, :, :], io["mla_w_uk"][0].rearrange("(a b) d c -> (b d) a c", b=2)).then_inc(aw_in, 16)
            sp.dma_start(wuv[:, :, :], io["mla_w_uv"][0].rearrange("h c d -> c h d")).then_inc(aw_in, 16)
            sp.wait_ge(zeros_ready, 1)
            for n in range(EXTRA):
                at = (N_EXP + n) * P
                sp.dma_start(sh.y_dram[at:at + P, :], zeros[:, :]).then_inc(y_zeroed, 16)
            sp.dma_start(sh.w_out[:, :, :], io["w_out"][0].rearrange("(c p) n -> p c n", p=P)).then_inc(sh.w_out_in, 16)
            sp.wait_ge(y_zeroed, 16 * EXTRA)

        @block.tensor
        def _(pe):
            ident, ones = sh.const("ident"), sh.const("ones")
            pe.matmul(bank[2][0:C, :], ones[0:C, 0:C], sh.pT[0:C, IK0, :], start=True, stop=True).then_inc(summed, 1)
            pe.wait_ge(squared, 3)
            pe.matmul(bank[0][:, :], ones, sq[:, 0, :], start=True, stop=False)
            pe.matmul(bank[0][:, :], ones, sq[:, 1, :], start=False, stop=True).then_inc(summed, 1)
            pe.matmul(bank[1][:, :], ones, sq[:, 2, :], start=True, stop=True).then_inc(summed, 1)
            for i in range(NT):
                last = pe.transpose(bank[4][:, i * HEADS:(i + 1) * HEADS], sh.pT[C:C + HEADS, IK0, i * P:(i + 1) * P],
                                    ident[C:C + HEADS, C:C + HEADS])
            last.then_inc(iw_turned, 1)
            pe.wait_ge(ik_step, 2)
            pe.matmul(bank[3][0:C, :], ones[0:C, 0:C], ikd[:, 1, :], start=True, stop=True).then_inc(summed, 1)
            pe.wait_ge(aw_in, 64)
            pe.wait_ge(lat_ready, 3)
            for i in range(NT):
                last = pe.transpose(bank[5][:, i * P:(i + 1) * P], c_lat[:, i * P:(i + 1) * P], ident)
            last.then_inc(c_turned, 1)
            for n in range(2 * NPAIR):
                w = wq if n < NPAIR else wi
                b = bank[6 + n % 2]
                if n >= 2:
                    pe.wait_ge(q_copied, n - 1)
                for k in range(2):
                    last = pe.matmul(b[:, :], w[:, k, (n % NPAIR) * P:(n % NPAIR + 1) * P], q_lat[:, k, :], start=(k == 0), stop=(k == 1))
                last.then_inc(q_done, 1)
            pe.wait_ge(q_copied, 2 * NPAIR)
            pe.wait_ge(ik_ready, 2)
            for n, (i, h) in enumerate(idx_units):
                b = bank[6 + n % 2]
                if n >= 2:
                    pe.wait_ge(relu_ready, n - 1)
                k = (i + 1) * P
                pe.matmul(b[:, 0:k], iqT[half(h), h // 2, i * P:(i + 1) * P], ik[half(h), 0:k], start=True, stop=True).then_inc(idx_done, 1)
            pe.wait_ge(rooted, 3)
            for h in range(HEADS):
                b = bank[h % 2]
                if h >= 2:
                    pe.wait_ge(qa_copied, h - 1)
                pe.matmul(b[:, :], wuk[half(h), h // 2, :], qT[half(h), h // 2, :], start=True, stop=True).then_inc(qa_done, 1)
            pe.wait_ge(qa_copied, HEADS)
            pe.wait_ge(relu_ready, len(idx_units))
            pe.wait_ge(c_copied, 1)
            pe.wait_ge(iw_ready, 1)
            N = len(UNITS)
            for u in range(N + 3):
                if u < N:
                    i, h = UNITS[u]
                    if u >= 2:
                        pe.wait_ge(l_ready, u - 1)
                    k = (i + 1) * P
                    pe.matmul(bank[u % 2][:, 0:k], q_abs[:, h, i * P:(i + 1) * P], c_lat[:, 0:k], start=True, stop=True).then_inc(l_done, 1)
                if 1 <= u <= N:
                    w = u - 1
                    i, h = UNITS[w]
                    pe.wait_ge(prob_ready, w + 1)
                    if w >= 2:
                        pe.wait_ge(probT_ready, w - 1)
                    for b in range(i + 1):
                        last = pe.transpose(bank[2 + w % 2][:, b * P:(b + 1) * P], prob[:, w % 2, b * P:(b + 1) * P], ident)
                    last.then_inc(prob_turned, 1)
                if 2 <= u <= N + 1:
                    w = u - 2
                    i, h = UNITS[w]
                    pe.wait_ge(probT_ready, w + 1)
                    if w >= 2:
                        pe.wait_ge(olat_ready, w - 1)
                    for b in range(i + 1):
                        last = pe.matmul(bank[4 + w % 2][:, 0:P], c_tm[:, b, :], probT[:, w % 2, b * P:(b + 1) * P], start=(b == 0), stop=(b == i))
                    last.then_inc(pv_done, 1)
                if u >= 3:
                    w = u - 3
                    i, h = UNITS[w]
                    pe.wait_ge(olat_ready, w + 1)
                    if w >= 2:
                        pe.wait_ge(o_ready, w - 1)
                    pe.matmul(bank[6 + w % 2][:, 0:C], o_lat[:, w % 2, :], wuv[:, h, :], start=True, stop=True).then_inc(o_done, 1)

        @block.scalar
        def _(act):
            for n, t in enumerate((Q0, Q0 + 1, KV0)):
                act.activation(sq[:, n, :], sh.pT[:, t, :], ACT.Square).then_inc(squared, 1)
            eps = sh.const("eps")
            act.wait_ge(summed, 2)
            act.activation(root[:, 0, :], bank[0][:, :], ACT.Sqrt, bias=eps[:, 0:1], scale=1.0 / Q_LORA).then_inc(rooted, 1)
            act.wait_ge(summed, 3)
            act.activation(root[:, 1, :], bank[1][:, :], ACT.Sqrt, bias=eps[:, 0:1], scale=1.0 / KV_LORA).then_inc(rooted, 1)
            act.wait_ge(summed, 4)
            act.activation(root[0:C, 2, :], bank[3][0:C, :], ACT.Sqrt, bias=eps[0:C, 1:2], scale=1.0 / IDX_DIM).then_inc(rooted, 1)
            for n in range(2 * NPAIR):
                act.wait_ge(q_done, n + 1)
                dst = qT if n < NPAIR else iqT
                act.copy(dst[:, n % NPAIR, :], bank[6 + n % 2][:, :]).then_inc(q_copied, 1)
            for n, (i, h) in enumerate(idx_units):
                k = (i + 1) * P
                act.wait_ge(idx_done, n + 1)
                if n >= 2:
                    act.wait_ge(score_added, n - 1)
                if n == 0:
                    act.wait_ge(y_zeroed, 16 * EXTRA)
                act.activation(relu[:, n % 2, 0:k], bank[6 + n % 2][:, 0:k], ACT.Relu).then_inc(relu_ready, 1)
            for h in range(HEADS):
                act.wait_ge(qa_done, h + 1)
                act.mul(q_abs[:, h, :], bank[h % 2][:, :], SCALE / SLOPES[h]).then_inc(qa_copied, 1)
            N = len(UNITS)
            for u in range(N + 1):
                if u < N:
                    i, h = UNITS[u]
                    k = (i + 1) * P
                    act.wait_ge(nmax_ready, u + 1)
                    if u >= 2:
                        act.wait_ge(prob_turned, u - 1)
                    act.activation(prob[:, u % 2, 0:k], logit[:, u % 2, 0:k], ACT.Exp, bias=stat[:, 1, u:u + 1],
                                   accum_out=stat[:, 2, u:u + 1]).then_inc(prob_ready, 1)
                if u >= 1:
                    w = u - 1
                    k = (UNITS[w][0] + 1) * P
                    act.wait_ge(prob_turned, w + 1)
                    if w >= 2:
                        act.wait_ge(pv_done, w - 1)
                    act.copy(probT[:, w % 2, 0:k], bank[2 + w % 2][:, 0:k]).then_inc(probT_ready, 1)

        @block.vector
        def _(v):
            v.memset(zeros, 0.0).then_inc(zeros_ready, 1)
            v.wait_ge(summed, 1)
            v.scalar_tensor_tensor(ikd[:, 0, :], bank[2][0:C, :], -1.0 / IDX_DIM, sh.pT[0:C, IK0, :], ALU.mult, ALU.add).then_inc(ik_step, 1)
            v.wait_ge(ik_step, 1)
            v.tensor_tensor(ikd[:, 1, :], ikd[:, 0, :], ikd[:, 0, :], ALU.mult).then_inc(ik_step, 1)
            for n in range(2):
                v.wait_ge(rooted, n + 1)
                v.reciprocal(root[:, n, :], root[:, n, :]).then_inc(rinv_ready, 1)
            v.wait_ge(rinv_ready, 2)
            for n in range(2):
                v.scalar_tensor_tensor(q_lat[:, n, :], sh.pT[:, Q0 + n, :], sh.col("mla_q_norm", n), root[:, 0, :], ALU.mult, ALU.mult).then_inc(lat_ready, 1)
            v.scalar_tensor_tensor(c_lat[:, :], sh.pT[:, KV0, :], sh.col("mla_kv_norm", 0), root[:, 1, :], ALU.mult, ALU.mult).then_inc(lat_ready, 1)
            v.wait_ge(rooted, 3)
            v.reciprocal(root[0:C, 2, :], root[0:C, 2, :]).then_inc(rinv_ready, 1)
            v.wait_ge(rinv_ready, 3)
            v.tensor_tensor(ikd[:, 1, :], ikd[:, 0, :], root[0:C, 2, :], ALU.mult).then_inc(ik_step, 1)
            v.wait_ge(ik_step, 3)
            v.tensor_scalar(ik[0:C, :], ikd[:, 1, :], sh.col("idx_ln_g", 0)[0:C], sh.col("idx_ln_b", 0)[0:C], ALU.mult, ALU.add).then_inc(ik_ready, 1)
            v.wait_ge(ik_ready, 1)
            v.tensor_copy(ik[C:P, :], ik[0:C, :]).then_inc(ik_ready, 1)
            v.wait_ge(iw_turned, 1)
            v.tensor_scalar(iw[:, :, :], bank[4][:, 0:NT * HEADS].rearrange("p (a b) -> p a b", b=HEADS),
                            float(HEADS ** -0.5 * IDX_DIM ** -0.5), None, ALU.mult).then_inc(iw_ready, 1)
            v.wait_ge(c_turned, 1)
            v.tensor_copy(c_tm[:, :, :], bank[5][:, :].rearrange("p (a b) -> p a b", b=P)).then_inc(c_copied, 1)
            v.memset(score[:, :, :], 0.0).then_inc(top_step, 1)
            v.wait_ge(top_step, 1)
            for i in range(NT):
                v.tensor_copy(score[:, i, i * P:(i + 1) * P], sh.const("causal")).then_inc(top_step, 1)
            steps = 1 + NT
            v.wait_ge(top_step, steps)
            v.wait_ge(iw_ready, 1)
            for n, (i, h) in enumerate(idx_units):
                k = (i + 1) * P
                v.wait_ge(relu_ready, n + 1)
                if n:
                    v.wait_ge(score_added, n)
                v.scalar_tensor_tensor(score[:, i, 0:k], relu[:, n % 2, 0:k], iw[:, i, h:h + 1], score[:, i, 0:k], ALU.mult, ALU.add).then_inc(score_added, 1)
            v.wait_ge(score_added, len(idx_units))
            for r in range(TOPK // 8):
                for i in range(1, NT):
                    k = (i + 1) * P
                    if r:
                        v.wait_ge(top_step, steps - NT + 2)
                    v.max(best[:, i, :], score[:, i, 0:k]).then_inc(top_step, 1)
                    steps += 1
                for i in range(1, NT):
                    k = (i + 1) * P
                    v.wait_ge(top_step, steps - NT + 2)
                    v.match_replace(score[:, i, 0:k], best[:, i, :], score[:, i, 0:k], TAKEN).then_inc(top_step, 1)
                    steps += 1
            v.wait_ge(top_step, steps)
            for i in range(1, NT):
                k = (i + 1) * P
                v.tensor_scalar(score[:, i, 0:k], score[:, i, 0:k], TAKEN, NEG, ALU.is_gt, ALU.mult).then_inc(top_step, 1)
                steps += 1
            v.wait_ge(top_step, steps)
            for i in range(NT):
                k = (i + 1) * P
                v.scalar_tensor_tensor(score[:, i, 0:k], sh.const("dist")[:, 0:k], float(-i * P), score[:, i, 0:k], ALU.add, ALU.add).then_inc(bias_ready, 1)
            v.wait_ge(bias_ready, NT)
            N = len(UNITS)
            for u in range(N + 3):
                if u < N:
                    i, h = UNITS[u]
                    k = (i + 1) * P
                    v.wait_ge(l_done, u + 1)
                    if u >= 2:
                        v.wait_ge(prob_ready, u - 1)
                    v.tensor_tensor_reduce(logit[:, u % 2, 0:k], bank[u % 2][:, 0:k], score[:, i, 0:k], SLOPES[h], TAKEN,
                                           ALU.add, ALU.max, stat[:, 0, u:u + 1]).then_inc(l_ready, 1)
                    v.wait_ge(l_ready, u + 1)
                    v.tensor_scalar(stat[:, 1, u:u + 1], stat[:, 0, u:u + 1], -1.0, None, ALU.mult).then_inc(nmax_ready, 1)
                if 2 <= u <= N + 1:
                    w = u - 2
                    v.wait_ge(pv_done, w + 1)
                    if w >= 2:
                        v.wait_ge(o_done, w - 1)
                    v.tensor_copy(o_lat[:, w % 2, :], bank[4 + w % 2][:, 0:P]).then_inc(olat_ready, 1)
                    v.reciprocal(stat[:, 3, w:w + 1], stat[:, 2, w:w + 1]).then_inc(rsum_ready, 1)
                if u >= 3:
                    w = u - 3
                    i, h = UNITS[w]
                    v.wait_ge(o_done, w + 1)
                    v.wait_ge(rsum_ready, w + 1)
                    v.tensor_scalar(sh.cat[:, i, D_GROUP + h * C:D_GROUP + (h + 1) * C], bank[6 + w % 2][:, 0:C],
                                    stat[:, 3, w:w + 1], None, ALU.mult).then_inc(o_ready, 1)


def prepare(nc, io, sh):
    with ExitStack() as ctx:
        e = ctx.enter_context
        w2a2 = e(nc.sbuf_tensor("w2_a2_sb", [P, D_GROUP], F32))
        tanh = e(nc.sbuf_tensor("tanh_w", [C, S], F32))
        sig = e(nc.sbuf_tensor("sig_w", [P, NPAIR, S], F32))
        cum = e(nc.sbuf_tensor("cum", [P, NPAIR, S], F32))
        sqk = e(nc.sbuf_tensor("kk_squares", [P, 2, S], F32))
        root = e(nc.sbuf_tensor("kk_root", [P, NPAIR, S], F32))
        rate = e(nc.sbuf_tensor("rate", [P, 2, S], F32))
        prod = e(nc.sbuf_tensor("rk_prod", [P, 2, S], F32))
        grow = e(nc.sbuf_tensor("decays", [P, 3, 2, S], F32))
        bank = psum_banks(nc, e, "prepare")
        b_hat = sh.b_hat
        KK0 = SHIFT_TILES

        sem = sh.sem
        pw_in, tanh_ready, lora_done, sig_ready, gate_ready = sem("prep_w_in"), sem("tanh_ready"), sem("lora_done"), sem("sigw_ready"), sem("gate_sig_ready")
        kk_raw, kk_squared, kk_summed, kk_rooted = sem("kk_raw"), sem("kk_squared"), sem("kk_summed"), sem("kk_rooted")
        root_step, kk_ready, rate_ready, k_ready, b_ready = sem("root_step"), sem("kk_ready"), sem("rate_ready"), sem("k_ready"), sem("b_ready")
        prod_ready, bonus_done, cum_ready, dif_ready, grown, scaled = sem("prod_ready"), sem("bonus_done"), sem("cum_ready"), sem("dif_ready"), sem("grown"), sem("scaled")
        v_turned, v_copied, bonus_copied, end_ready = sem("v_turned"), sem("v_copied"), sem("bonus_copied"), sem("end_ready")
        R0, K0, V0, WA, G0 = 0, NPAIR, 2 * NPAIR, 3 * NPAIR, 3 * NPAIR + 1
        block = e(nc.Block())

        @block.sync
        def _(sp):
            sp.dma_start(w2a2[0:C, :], io["rwkv_w2"][0]).then_inc(pw_in, 16)
            sp.dma_start(w2a2[C:P, :], io["rwkv_a2"][0]).then_inc(pw_in, 16)

        @block.tensor
        def _(pe):
            ident = sh.const("ident")
            pe.wait_ge(pw_in, 32)
            pe.wait_ge(tanh_ready, 1)
            for g in range(NPAIR):
                cs = slice(g * P, (g + 1) * P)
                if g >= 2:
                    pe.wait_ge(sig_ready, 2 * (g - 1))
                pe.matmul(bank[g % 2][:, :], w2a2[0:C, cs], tanh[:, :], start=True, stop=True).then_inc(lora_done, 1)
                pe.matmul(bank[2 + g % 2][:, :], w2a2[C:P, cs], sh.pT[C:P, WA, :], start=True, stop=True).then_inc(lora_done, 1)
            for g in range(NPAIR):
                pe.wait_ge(kk_squared, g + 1)
                if g >= 2:
                    pe.wait_ge(kk_rooted, g - 1)
                pe.matmul(bank[4 + g % 2][:, :], sh.const("half"), sqk[:, g % 2, :], start=True, stop=True).then_inc(kk_summed, 1)
                if g >= 1:
                    pe.wait_ge(v_copied, g)
                for i in range(NT):
                    last = pe.transpose(bank[6][:, i * P:(i + 1) * P], sh.pT[:, V0 + g, i * P:(i + 1) * P], ident)
                last.then_inc(v_turned, 1)
            for g in range(NPAIR):
                pe.wait_ge(prod_ready, g + 1)
                for i in range(NT):
                    last = pe.matmul(bank[7][:, i * HEADS + 2 * g:i * HEADS + 2 * g + 2], prod[:, g % 2, i * P:(i + 1) * P],
                                     sh.const("heads"), start=True, stop=True)
                last.then_inc(bonus_done, 1)

        @block.scalar
        def _(act):
            act.activation(tanh[:, :], sh.pT[0:C, WA, :], ACT.Tanh).then_inc(tanh_ready, 1)
            act.activation(sh.gate_sig[:, :], sh.pT[:, G0, :], ACT.Sigmoid).then_inc(gate_ready, 1)
            for g in range(NPAIR):
                act.wait_ge(lora_done, 2 * g + 2)
                act.activation(sig[:, g, :], bank[g % 2][:, :], ACT.Sigmoid, bias=sh.col("rwkv_w0", g)).then_inc(sig_ready, 1)
                act.activation(b_hat[:, g, :], bank[2 + g % 2][:, :], ACT.Sigmoid, bias=sh.col("rwkv_a0", g)).then_inc(sig_ready, 1)
            for g in range(NPAIR):
                act.wait_ge(kk_raw, g + 1)
                if g >= 2:
                    act.wait_ge(kk_summed, g - 1)
                act.activation(sqk[:, g % 2, :], sh.pT[:, KK0 + g, :], ACT.Square).then_inc(kk_squared, 1)
                act.wait_ge(kk_summed, g + 1)
                act.activation(root[:, g, :], bank[4 + g % 2][:, :], ACT.Sqrt).then_inc(kk_rooted, 1)
                act.wait_ge(v_turned, g + 1)
                act.copy(sh.v_tm[:, :, g * P:(g + 1) * P], bank[6][:, :].rearrange("p (a b) -> p a b", b=P)).then_inc(v_copied, 1)
            for g in range(NPAIR):
                act.wait_ge(cum_ready, g + 1)
                if g >= 2:
                    act.wait_ge(scaled, 4 * (g - 1))
                    act.wait_ge(end_ready, g - 1)
                act.activation(grow[:, 0, g % 2, :], cum[:, g, :], ACT.Exp, scale=-DECAY).then_inc(grown, 1)
                act.activation(grow[:, 1, g % 2, :], cum[:, g, :], ACT.Exp, scale=DECAY).then_inc(grown, 1)
                act.wait_ge(dif_ready, g + 1)
                act.activation(grow[:, 2, g % 2, :], sig[:, g, :], ACT.Exp, scale=-DECAY).then_inc(grown, 1)

        @block.vector
        def _(v):
            keep = sh.const("keep")
            for g in range(NPAIR):
                v.tensor_scalar(sh.pT[:, KK0 + g, :], sh.pT[:, K0 + g, :], sh.col("rwkv_k_k", g), None, ALU.mult).then_inc(kk_raw, 1)
            for g in range(NPAIR):
                v.wait_ge(sig_ready, 2 * g + 2)
                v.tensor_tensor_scan(cum[:, g, :], keep, sig[:, g, :], 0.0, ALU.mult, ALU.add).then_inc(cum_ready, 1)
                v.tensor_scalar(rate[:, g % 2, :], b_hat[:, g, :], -1.0, sh.col("rwkv_k_a", g), ALU.add, ALU.mult).then_inc(rate_ready, 1)
                v.wait_ge(cum_ready, g + 1)
                v.tensor_tensor(sig[:, g, :], cum[:, g, :], sig[:, g, :], ALU.subtract).then_inc(dif_ready, 1)
                v.wait_ge(rate_ready, g + 1)
                v.scalar_tensor_tensor(sh.pT[:, K0 + g, :], rate[:, g % 2, :], 1.0, sh.pT[:, K0 + g, :], ALU.add, ALU.mult).then_inc(k_ready, 1)
                v.wait_ge(k_ready, g + 1)
                if g >= 2:
                    v.wait_ge(bonus_done, g - 1)
                v.scalar_tensor_tensor(prod[:, g % 2, :], sh.pT[:, R0 + g, :], sh.col("rwkv_r_k", g), sh.pT[:, K0 + g, :], ALU.mult, ALU.mult).then_inc(prod_ready, 1)
            for g in range(NPAIR):
                v.wait_ge(kk_rooted, g + 1)
                v.tensor_scalar(root[:, g, :], root[:, g, :], 1e-12, None, ALU.max).then_inc(root_step, 1)
                v.wait_ge(root_step, 2 * g + 1)
                v.reciprocal(root[:, g, :], root[:, g, :]).then_inc(root_step, 1)
                v.wait_ge(root_step, 2 * g + 2)
                v.tensor_tensor(sh.pT[:, KK0 + g, :], sh.pT[:, KK0 + g, :], root[:, g, :], ALU.mult).then_inc(kk_ready, 1)
                v.wait_ge(kk_ready, g + 1)
                v.tensor_tensor(b_hat[:, g, :], b_hat[:, g, :], sh.pT[:, KK0 + g, :], ALU.mult).then_inc(b_ready, 1)
            v.wait_ge(b_ready, NPAIR)
            v.wait_ge(prod_ready, NPAIR)
            for g in range(NPAIR):
                b = g % 2
                v.wait_ge(grown, 3 * g + 1)
                v.tensor_tensor(sh.pT[:, R0 + g, :], sh.pT[:, R0 + g, :], grow[:, 0, b, :], ALU.mult).then_inc(scaled, 1)
                v.tensor_copy(sh.w_end[:, g, :], grow[:, 0, b, C - 1::C]).then_inc(end_ready, 1)
                v.wait_ge(grown, 3 * g + 2)
                v.tensor_tensor(b_hat[:, g, :], b_hat[:, g, :], grow[:, 1, b, :], ALU.mult).then_inc(scaled, 1)
                v.tensor_tensor(sh.pT[:, K0 + g, :], sh.pT[:, K0 + g, :], grow[:, 1, b, :], ALU.mult).then_inc(scaled, 1)
                v.wait_ge(grown, 3 * g + 3)
                v.scalar_tensor_tensor(sh.pT[:, KK0 + g, :], sh.pT[:, KK0 + g, :], -1.0, grow[:, 2, b, :], ALU.mult, ALU.mult).then_inc(scaled, 1)
            v.wait_ge(bonus_done, NPAIR)
            v.tensor_copy(sh.bonus[:, :, :], bank[7][:, 0:NT * HEADS].rearrange("p (a b) -> p a b", b=HEADS)).then_inc(bonus_copied, 1)


PE_STEPS = ["ba", "ab"] + [f"{s}{n}" for n in LEVELS for s in ("z", "t", "tt") if (s, n) != ("t", LEVELS[-1])] + \
           ["ka", "akv", "x", "oo", "rr", "m0", "n0"]
ACT_STEPS = ["abt"] + [f"{s}{n}" for n in LEVELS for s in ("t", "tt") if (s, n) != ("t", LEVELS[-1])] + ["akv", "x", "oo"]
DVE_STEPS = ["arb", "t", "tt"] + [f"z{n}" for n in LEVELS] + ["ka", "rr", "m0", "n0"]
POOL_STEPS = [f"lv{n}" for n in LEVELS]


def scan(nc, io, sh):
    with ExitStack() as ctx:
        e = ctx.enter_context
        two = range(2)
        g2 = e(nc.sbuf_tensor("g2_sb", [P, D_GROUP], F32))
        lnb = e(nc.sbuf_tensor("rwkv_ln_sb", [P, 2, D_GROUP], F32))
        tm = e(nc.sbuf_tensor("bk_tm", [P, 2, NT, P], F32))
        TA = e(nc.sbuf_tensor("a_akv_tm", [P, 2, NT, 2, C], F32))
        Tm = [e(nc.sbuf_tensor(f"T{h}", [P, NT, P], F32)) for h in two]
        TT = [e(nc.sbuf_tensor(f"TT{h}", [P, NT, P], F32)) for h in two]
        Z1 = [e(nc.sbuf_tensor(f"Z1{h}", [P, NT, P], F32)) for h in two]
        LV = [e(nc.sbuf_tensor(f"LV{h}", [P, NT, P], F32)) for h in two]
        ABT = [e(nc.sbuf_tensor(f"ABT{h}", [P, NT, P], F32)) for h in two]
        ARB = [e(nc.sbuf_tensor(f"ARB{h}", [P, NT, P], F32)) for h in two]
        KA = [e(nc.sbuf_tensor(f"KA{h}", [P, NT, 2, P], F32)) for h in two]
        X = [e(nc.sbuf_tensor(f"X{h}", [P, NT, P], F32)) for h in two]
        RR = e(nc.sbuf_tensor("RR", [P, S], F32))
        M0 = e(nc.sbuf_tensor("M0", [P, NCH, C], F32))
        N0 = e(nc.sbuf_tensor("N0", [P, NCH, C], F32))
        ST = e(nc.sbuf_tensor("state", [P, NCH + 1, C], F32))
        gn = e(nc.sbuf_tensor("gn_stats", [P, NT, 4, HEADS], F32))
        bank = psum_banks(nc, e, "scan")
        own = [bank[0:4], bank[4:8]]
        turned = (bank[0], bank[1], bank[4])

        sem = sh.sem
        sw_in, tm_turned, tm_copied = sem("scan_w_in"), sem("tm_turned"), sem("tm_copied")
        pe_step = [sem(f"pe_step{h}") for h in two]
        act_step = [sem(f"act_step{h}") for h in two]
        dve_step = [sem(f"dve_step{h}") for h in two]
        pool_step = [sem(f"pool_step{h}") for h in two]
        dve_half = sem("dve_half")
        state_done, state_ready, carry_done, carry_added = sem("state_done"), sem("state_ready"), sem("carry_done"), sem("carry_added")
        gn_bonus, gn_normed, gn_weighted, gn_whole = sem("gn_bonus"), sem("gn_normed"), sem("gn_weighted"), sem("gn_whole")
        gn_sum, gn_dev, gn_sq, gn_var, gn_root, gn_step, gate_done, gate_free = (sem("gn_sum"), sem("gn_dev"), sem("gn_sq"), sem("gn_var"),
                                                                    sem("gn_root"), sem("gn_step"), sem("gate_done"), sem("gate_free"))
        R0, K0, A0 = 0, NPAIR, SHIFT_TILES
        half = lambda h: slice(C * h, C * h + C)

        def pe_after(eng, h, r, name):
            eng.wait_ge(pe_step[h], r * len(PE_STEPS) + PE_STEPS.index(name) + 1)

        def act_after(eng, h, r, name):
            eng.wait_ge(act_step[h], r * len(ACT_STEPS) + ACT_STEPS.index(name) + 1)

        def dve_after(eng, h, r, name):
            eng.wait_ge(dve_step[h], r * len(DVE_STEPS) + DVE_STEPS.index(name) + 1)

        def pool_after(eng, h, r, name):
            eng.wait_ge(pool_step[h], r * len(POOL_STEPS) + POOL_STEPS.index(name) + 1)

        flat = lambda t: t[:, :, :].rearrange("p a b -> p (a b)")
        dev = lambda i: flat(Tm[i % 2])
        sqd = lambda i: flat(TT[i % 2])

        def tiles(ap):
            return ap.rearrange("p (a b) -> p a b", b=P)

        def bc(ap, n):
            return ap.rearrange("p (a m) -> p a m", a=1).broadcast_to([ap.shape[0], n, ap.shape[1]])

        block = e(nc.Block())

        @block.sync
        def _(sp):
            sp.dma_start(g2[:, :], io["rwkv_g2"][0]).then_inc(sw_in, 16)
            sp.dma_start(lnb[:, 0, :], io["rwkv_ln_w"].broadcast_to([P, D_GROUP])).then_inc(sw_in, 16)
            sp.dma_start(lnb[:, 1, :], io["rwkv_ln_b"].broadcast_to([P, D_GROUP])).then_inc(sw_in, 16)
            sp.wait_ge(sh.w_out_in, 16)

        @block.tensor
        def _(pe):
            ident = sh.const("ident")

            def turn(r, n):
                src = (sh.pT[:, A0 + r, :], sh.b_hat[:, r, :], sh.pT[:, K0 + r, :])[n]
                if r:
                    dve_after(pe, 0, r - 1, "n0")
                    dve_after(pe, 1, r - 1, "n0")
                for i in range(NT):
                    last = pe.transpose(turned[n][:, i * P:(i + 1) * P], src[:, i * P:(i + 1) * P], ident)
                last.then_inc(tm_turned, 1)

            def b_a(r, h):
                pe.wait_ge(tm_copied, 3 * (r + 1))
                for i in range(NT):
                    ts = slice(i * P, (i + 1) * P)
                    last = pe.matmul(own[h][i // 2][:, (i % 2) * 256:(i % 2) * 256 + 256].rearrange("p (a b) -> p a b", b=P), sh.b_hat[half(h), r, ts],
                                     sh.pT[half(h), R0 + r:A0 + r + 1:A0 - R0, ts],
                                     start=True, stop=True)
                last.then_inc(pe_step[h], 1)

            for n in range(3):
                turn(0, n)
            for h in two:
                b_a(0, h)
            for r in range(NPAIR):
                if r:
                    pe.wait_ge(carry_added, r)
                for h in two:
                    if r:
                        act_after(pe, h, r - 1, "oo")
                    for i in range(NT):
                        ts = slice(i * P, (i + 1) * P)
                        last = pe.matmul(own[h][2][:, ts], sh.pT[half(h), A0 + r, ts], sh.b_hat[half(h), r, ts], start=True, stop=True)
                    last.then_inc(pe_step[h], 1)
                for n in LEVELS:
                    for h in two:
                        pool_after(pe, h, r, f"lv{n}")
                        if n == LEVELS[0]:
                            dve_after(pe, h, r, "tt")
                        else:
                            act_after(pe, h, r, f"t{n // 2}")
                            act_after(pe, h, r, f"tt{n // 2}")
                        for i in range(NT):
                            last = pe.matmul(own[h][3][:, i * P:(i + 1) * P], LV[h][:, i, :], Tm[h][:, i, :], start=True, stop=True)
                        last.then_inc(pe_step[h], 1)
                    for h in two:
                        dve_after(pe, h, r, f"z{n}")
                        if n != LEVELS[-1]:
                            for i in range(NT):
                                last = pe.matmul(own[h][0][:, i * P:(i + 1) * P], TT[h][:, i, :], Z1[h][:, i, :], start=True, stop=True)
                            last.then_inc(pe_step[h], 1)
                        for i in range(NT):
                            last = pe.matmul(own[h][1][:, i * P:(i + 1) * P], Z1[h][:, i, :], TT[h][:, i, :], start=True, stop=True)
                        last.then_inc(pe_step[h], 1)
                for h in two:
                    for i in range(NT):
                        ts = slice(i * P, (i + 1) * P)
                        last = pe.matmul(own[h][2 + i // 2][:, (i % 2) * 256:(i % 2) * 256 + 256].rearrange("p (a b) -> p a b", b=P), sh.pT[half(h), K0 + r, ts],
                                         sh.pT[half(h), R0 + r:A0 + r + 1:A0 - R0, ts], start=True, stop=True)
                    last.then_inc(pe_step[h], 1)
                vs = lambda h: slice(r * P + h * C, r * P + h * C + C)
                for h in two:
                    dve_after(pe, h, r, "ka")
                    for i in range(NT):
                        last = pe.matmul(own[h][0][:, i * C:(i + 1) * C], KA[h][:, i, 1, :], sh.v_tm[:, i, vs(h)], start=True, stop=True)
                    last.then_inc(pe_step[h], 1)
                for h in two:
                    act_after(pe, h, r, "akv")
                    act_after(pe, h, r, f"tt{LEVELS[-1]}")
                    for i in range(NT):
                        last = pe.matmul(own[h][1][:, i * P:(i + 1) * P], TT[h][:, i, :], TA[:, h, i, :, :].rearrange("p a c -> p (a c)"), start=True, stop=True)
                    last.then_inc(pe_step[h], 1)
                for h in two:
                    act_after(pe, h, r, "x")
                    for i in range(NT):
                        pe.matmul(own[h][2][:, i * C:(i + 1) * C], KA[h][:, i, 0, :], sh.v_tm[:, i, vs(h)], start=True, stop=False)
                        last = pe.matmul(own[h][2][:, i * C:(i + 1) * C], ARB[h][:, i, :], X[h][:, i, C:P], start=False, stop=True)
                    last.then_inc(pe_step[h], 1)
                for h in two:
                    for i in range(NT):
                        last = pe.matmul(own[h][3][half(h), i * P:(i + 1) * P], X[h][:, i, 0:C], ARB[h][:, i, :], start=True, stop=True)
                    last.then_inc(pe_step[h], 1)
                for h in two:
                    act_after(pe, h, r, "oo")
                    for n in range(NCH):
                        tok = half(n % 2)
                        last = pe.matmul(own[h][2 * (n % 2)][half(h), n // 2 * C:(n // 2 + 1) * C], X[h][tok, n // 2, 0:C], tm[tok, 0, n // 2, half(h)], start=True, stop=True)
                    last.then_inc(pe_step[h], 1)
                for h in two:
                    dve_after(pe, h, r, "rr")
                    for n in range(NCH):
                        tok = half(n % 2)
                        out = own[h][1 + 2 * (n % 2)][half(h), n // 2 * C:(n // 2 + 1) * C]
                        pe.matmul(out, tm[tok, 1, n // 2, half(h)], sh.v_tm[tok, n // 2, vs(h)], start=True, stop=False)
                        last = pe.matmul(out, tm[tok, 0, n // 2, half(h)], X[h][tok, n // 2, C:P], start=False, stop=True)
                    last.then_inc(pe_step[h], 1)
                for n in range(NCH):
                    if r < NPAIR - 1:
                        if 1 <= n <= 3:
                            turn(r + 1, n - 1)
                        if n in (5, 6):
                            b_a(r + 1, n - 5)
                    pe.wait_ge(state_ready, r * NCH + n + 1)
                    if n < NCH - 1 and n > 0:
                        for h in two:
                            last = pe.matmul(bank[2][half(h), (n % 2) * C:(n % 2) * C + C], M0[half(h), n, :], ST[half(h), n, :], start=True, stop=True)
                        last.then_inc(state_done, 1)
                    for h in two:
                        last = pe.matmul(own[h][3][half(n % 2), (n // 2) * C:(n // 2 + 1) * C], RR[half(h), n * C:(n + 1) * C], ST[half(h), n, :],
                                         start=True, stop=True)
                last.then_inc(carry_done, 1)
            pe.wait_ge(sw_in, 48)
            for i in range(NT):
                pe.wait_ge(carry_added, NPAIR)
                if i >= 2:
                    pe.wait_ge(gate_free, i - 1)
                pe.matmul(bank[i % 2][:, :], sh.gate_sig[:, i * P:(i + 1) * P], g2[:, :], start=True, stop=True).then_inc(gate_done, 1)

        @block.scalar
        def _(act):
            for r in range(NPAIR):
                for n in range(3):
                    act.wait_ge(tm_turned, 3 * r + n + 1)
                    src = tiles(turned[n][:, :])
                    if n == 0:
                        act.copy(TA[:, :, :, 0, :], src.rearrange("p i (h c) -> p h i c", h=2)).then_inc(tm_copied, 1)
                    else:
                        act.copy(tm[:, n - 1, :, :], src).then_inc(tm_copied, 1)
                for h in two:
                    pe_after(act, h, r, "ba")
                    for b in two:
                        last = act.copy(ABT[h][:, 2 * b:2 * b + 2, :], own[h][b][:, :].rearrange("p (a b c) -> p a b c", a=2, b=2)[:, :, 1, :])
                    last.then_inc(act_step[h], 1)
                for n in LEVELS:
                    for h in two:
                        if n != LEVELS[-1]:
                            pe_after(act, h, r, f"t{n}")
                            act.copy(Tm[h][:, :, :], tiles(own[h][0][:, :])).then_inc(act_step[h], 1)
                        pe_after(act, h, r, f"tt{n}")
                        act.copy(TT[h][:, :, :], tiles(own[h][1][:, :])).then_inc(act_step[h], 1)
                for h in two:
                    pe_after(act, h, r, "akv")
                    act.copy(TA[:, h, :, 1, :], own[h][0][:, 0:NT * C].rearrange("p (a b) -> p a b", b=C)).then_inc(act_step[h], 1)
                for h in two:
                    pe_after(act, h, r, "x")
                    act.copy(X[h][:, :, :], tiles(own[h][1][:, :])).then_inc(act_step[h], 1)
                for h in two:
                    pe_after(act, h, r, "oo")
                    act.copy(sh.cat[:, :, r * P + h * C:r * P + (h + 1) * C], own[h][2][:, 0:NT * C].rearrange("p (a b) -> p a b", b=C)).then_inc(act_step[h], 1)
            for i in range(NT):
                act.wait_ge(gn_dev, i + 1)
                act.activation(sqd(i), dev(i), ACT.Square).then_inc(gn_sq, 1)
                act.wait_ge(gn_var, i + 1)
                act.activation(gn[:, i, 2, :], gn[:, i, 1, :], ACT.Sqrt, bias=sh.const("eps")[:, 2:3], scale=1.0 / C).then_inc(gn_root, 1)

        @block.gpsimd
        def _(pool):
            for r in range(NPAIR):
                for n in LEVELS:
                    for h in two:
                        if n == LEVELS[0]:
                            act_after(pool, h, r, "abt")
                        else:
                            pe_after(pool, h, r, f"z{n // 2}")
                        pool.tensor_tensor(LV[h][:, :, :], ABT[h][:, :, :], bc(sh.const(f"lev{n}"), NT), ALU.mult).then_inc(pool_step[h], 1)
            pool.wait_ge(sw_in, 48)
            for i in range(NT):
                pool.wait_ge(gn_normed, i + 1)
                pool.tensor_tensor(dev(i), dev(i), lnb[:, 0, :], ALU.mult).then_inc(gn_weighted, 1)
                pool.wait_ge(gn_weighted, 2 * i + 1)
                pool.tensor_tensor(dev(i), dev(i), lnb[:, 1, :], ALU.add).then_inc(gn_weighted, 1)
                pool.wait_ge(gn_weighted, 2 * i + 2)
                pool.wait_ge(gn_bonus, i + 1)
                pool.tensor_tensor(dev(i), dev(i), sqd(i), ALU.add).then_inc(gn_whole, 1)

        @block.vector
        def _(v):
            halves = 0
            for r in range(NPAIR):
                for h in two:
                    act_after(v, h, r, "abt")
                    if r:
                        pe_after(v, h, r - 1, "n0")
                    for b in two:
                        last = v.tensor_tensor(ARB[h][:, 2 * b:2 * b + 2, :], own[h][b][:, :].rearrange("p (a b c) -> p a b c", a=2, b=2)[:, :, 0, :],
                                               bc(sh.const("incl"), 2), ALU.mult)
                    last.then_inc(dve_step[h], 1)
                    pe_after(v, h, r, "ab")
                    v.tensor_tensor(Tm[h][:, :, :], tiles(own[h][2][:, :]), bc(sh.const("low2"), NT), ALU.mult).then_inc(dve_half, 1)
                    v.tensor_tensor(TT[h][:, :, :], ABT[h][:, :, :], bc(sh.const("up2"), NT), ALU.mult).then_inc(dve_half, 1)
                    halves += 2
                    v.wait_ge(dve_half, halves)
                    v.tensor_tensor(Tm[h][:, :, :], Tm[h][:, :, :], bc(sh.const("ident"), NT), ALU.add).then_inc(dve_step[h], 1)
                    v.tensor_tensor(TT[h][:, :, :], TT[h][:, :, :], bc(sh.const("ident"), NT), ALU.add).then_inc(dve_step[h], 1)
                for n in LEVELS:
                    for h in two:
                        pe_after(v, h, r, f"z{n}")
                        v.tensor_tensor(Z1[h][:, :, :], tiles(own[h][3][:, :]), bc(sh.const("ident"), NT), ALU.add).then_inc(dve_step[h], 1)
                for h in two:
                    pe_after(v, h, r, "ka")
                    for b in two:
                        for q, m in ((0, "incl"), (1, "strict")):
                            last = v.tensor_tensor(KA[h][:, 2 * b:2 * b + 2, q, :], own[h][2 + b][:, :].rearrange("p (a b c) -> p a b c", a=2, b=2)[:, :, q, :],
                                                   bc(sh.const(m), 2), ALU.mult)
                    last.then_inc(dve_step[h], 1)
                for h in two:
                    pe_after(v, h, r, "rr")
                    if r:
                        v.wait_ge(carry_done, r)
                    v.tensor_tensor(RR[half(h), :], own[h][3][half(h), :], sh.pT[half(h), R0 + r, :], ALU.add).then_inc(dve_step[h], 1)
                for h in two:
                    pe_after(v, h, r, "m0")
                    for b in two:
                        last = v.tensor_tensor(M0[half(h), b::2, :], own[h][2 * b][half(h), 0:NCH // 2 * C].rearrange("p (a b) -> p a b", b=C),
                                               bc(sh.const("ident")[half(h), half(h)], NCH // 2), ALU.add)
                    last.then_inc(dve_step[h], 1)
                for h in two:
                    pe_after(v, h, r, "n0")
                    for b in two:
                        last = v.tensor_tensor(N0[half(h), b::2, :], own[h][1 + 2 * b][half(h), 0:NCH // 2 * C].rearrange("p (a b) -> p a b", b=C),
                                               sh.w_end[half(h), r, b::2].rearrange("p (a b) -> p a b", b=1).broadcast_to([C, NCH // 2, C]), ALU.mult)
                    last.then_inc(dve_step[h], 1)
                dve_after(v, 0, r, "n0")
                dve_after(v, 1, r, "n0")
                v.memset(ST[:, 0, :], 0.0).then_inc(state_ready, 1)
                v.tensor_copy(ST[:, 1, :], N0[:, 0, :]).then_inc(state_ready, 1)
                for n in range(1, NCH - 1):
                    v.wait_ge(state_done, r * (NCH - 2) + n)
                    v.scalar_tensor_tensor(ST[:, n + 1, :], bank[2][:, (n % 2) * C:(n % 2) * C + C], sh.w_end[:, r, n:n + 1], N0[:, n, :],
                                           ALU.mult, ALU.add).then_inc(state_ready, 1)
                v.wait_ge(carry_done, r + 1)
                act_after(v, 0, r, "oo")
                act_after(v, 1, r, "oo")
                for h in two:
                    cat = sh.cat[:, :, r * P + h * C:r * P + (h + 1) * C]
                    last = v.tensor_tensor(cat, cat, own[h][3][:, 0:NT * C].rearrange("p (a b) -> p a b", b=C), ALU.add)
                last.then_inc(carry_added, 1)
            v.wait_ge(carry_added, NPAIR)
            v.wait_ge(sw_in, 48)
            wide = lambda ap: ap.rearrange("p (a b) -> p a b", b=1).broadcast_to([P, HEADS, C])
            heads = lambda ap: ap.rearrange("p (a b) -> p a b", b=C)
            steps = 0

            def gated(i):
                v.wait_ge(gn_whole, i + 1)
                v.wait_ge(gate_done, i + 1)
                v.tensor_tensor(sh.cat[:, i, 0:D_GROUP], dev(i), bank[i % 2][:, :], ALU.mult).then_inc(gate_free, 1)

            for i in range(NT):
                o = sh.cat[:, i, 0:D_GROUP]
                v.tensor_reduce(gn[:, i, 0, :], heads(o), AX.X, ALU.add).then_inc(gn_step, 1)
                steps += 1
                v.wait_ge(gn_step, steps)
                v.tensor_scalar(gn[:, i, 3, :], gn[:, i, 0, :], 1.0 / C, None, ALU.mult).then_inc(gn_step, 1)
                steps += 1
                v.wait_ge(gn_step, steps)
                if i >= 2:
                    v.wait_ge(gate_free, i - 1)
                v.tensor_tensor(heads(dev(i)), heads(o), wide(gn[:, i, 3, :]), ALU.subtract).then_inc(gn_dev, 1)
                v.wait_ge(gn_sq, i + 1)
                v.tensor_reduce(gn[:, i, 1, :], heads(sqd(i)), AX.X, ALU.add).then_inc(gn_var, 1)
                v.wait_ge(gn_root, i + 1)
                v.reciprocal(gn[:, i, 3, :], gn[:, i, 2, :]).then_inc(gn_step, 1)
                steps += 1
                v.wait_ge(gn_step, steps)
                v.tensor_tensor(heads(sqd(i)), heads(sh.v_tm[:, i, :]), wide(sh.bonus[:, i, :]), ALU.mult).then_inc(gn_bonus, 1)
                v.tensor_tensor(heads(dev(i)), heads(dev(i)), wide(gn[:, i, 3, :]), ALU.mult).then_inc(gn_normed, 1)
                if i:
                    gated(i - 1)
            gated(NT - 1)


def route(nc, io, sh):
    NR = NT * TOP_E
    with ExitStack() as ctx:
        e = ctx.enter_context
        catT = e(nc.sbuf_tensor("catT", [P, KC, S], F32))
        u2T = catT
        ln = e(nc.sbuf_tensor("ln1_rows", [P, 2, D], F32))
        wr = e(nc.sbuf_tensor("w_router_sb", [P, KC, N_EXP], F32))
        br = e(nc.sbuf_tensor("b_router_sb", [P, N_EXP], F32))
        mixg = e(nc.sbuf_tensor("mix_gated", [P, D], F32))
        u2 = e(nc.sbuf_tensor("u2", [P, 2, D], F32))
        st = e(nc.sbuf_tensor("ln1_stats", [P, NT, 16], F32))
        lg = e(nc.sbuf_tensor("router_logits", [P, NT, N_EXP], F32))
        m8 = e(nc.sbuf_tensor("top8", [P, NT, 8], F32))
        i8 = e(nc.sbuf_tensor("top8_at", [P, NT, 8], mybir.dt.uint32))
        idx = e(nc.sbuf_tensor("top_expert", [P, NT, 8], F32))
        sm = e(nc.sbuf_tensor("gate_stats", [P, NT, 4], F32))
        hot = e(nc.sbuf_tensor("one_hot", [P, TOP_E, NT, N_EXP], F32))
        chosen = e(nc.sbuf_tensor("chosen", [P, NT, N_EXP], F32))
        tmp = e(nc.sbuf_tensor("place_tmp", [P, 8, NT, N_EXP], F32))
        row = e(nc.sbuf_tensor("expert_rows", [P, 8, N_EXP], F32))
        ohx = mixg[:, 0:2 * EXTRA * N_EXP].rearrange("p (a j n) -> p a j n", a=2, n=N_EXP)
        xf = e(nc.sbuf_tensor("extra_f", [P, EXTRA + 2], F32))
        slotk = e(nc.sbuf_tensor("slot_of", [P, NT, TOP_E], F32))
        blkk = e(nc.sbuf_tensor("block_of", [P, NT, TOP_E], F32))
        rowf = e(nc.sbuf_tensor("row_of", [P, NT, TOP_E], F32))
        Qh = e(nc.sbuf_tensor("slot_hot", [P, 4, P], F32))
        Rh = e(nc.sbuf_tensor("block_hot", [P, 4, BLOCKS], F32))
        bank = psum_banks(nc, e, "route")

        sem = sh.sem
        rw_in, cat_turned, catT_ready, mix_done = sem("route_w_in"), sem("cat_turned"), sem("catT_ready"), sem("mix_done")
        ln_step, gated, x1_ready, u2_ready, u2_turned, u2T_ready, u2_stored = (sem("ln1_step"), sem("gated"), sem("x1_ready"), sem("u2_ready"),
                                                                              sem("u2_turned"), sem("u2T_ready"), [sem("u2_stored0"), sem("u2_stored1")])
        var_ready, root_ready, logits_done, rt_step, chosen_ready, rank_done = (sem("ln1_var"), sem("ln1_root"), sem("logits_done"), sem("rt_step"),
                                                                              sem("chosen_ready"), sem("rank_done"))
        sh.x_in, ids_ready = sem("xg_in"), sem("ids_ready")
        sh.expert_bias_in = sem("expert_bias_in")
        sh.bias_raw = sh.w_out[0:2 * N_EXP, :, :].rearrange("p c n -> p (c n)")[:, 0:2 * FF + D]
        sh.w_gu_in = [sem(f"w_gu_in{n}") for n in range(KC)]
        nmax_ready, exp_ready, hot_ready, ids_done = sem("gate_nmax"), sem("gate_exp"), sem("hot_ready"), sem("ids_done")
        block = e(nc.Block())

        @block.sync
        def _(sp):
            sp.dma_start(ln[:, 0, :], io["ln1_g"].broadcast_to([P, D])).then_inc(rw_in, 16)
            sp.dma_start(ln[:, 1, :], io["ln1_b"].broadcast_to([P, D])).then_inc(rw_in, 16)
            sp.dma_start(wr[:, :, :], io["w_router"][0].rearrange("(c p) n -> p c n", p=P)).then_inc(rw_in, 16)
            sp.dma_start(br[:, :], io["b_router"].broadcast_to([P, N_EXP])).then_inc(rw_in, 16)
            for n in range(EARLY):
                sp.dma_start(sh.w_gu_raw[:, n, :, :].rearrange("p a n -> p (a n)"),
                             io["w_gu"][0, 0, n * P:(n + 1) * P, :]).then_inc(sh.w_gu_in[n], 16)
            for i in range(NT):
                sp.wait_ge(u2_ready, i + 1)
                sp.dma_start(sh.u2_dram[i * P:(i + 1) * P, :], u2[:, i % 2, :]).then_inc(u2_stored[i % 2], 16)
            for at in (0, N_EXP):
                sp.dma_start(sh.bias_raw[at:at + N_EXP, 0:2 * FF], io["b_gu"][0]).then_inc(sh.expert_bias_in, 16)
                sp.dma_start(sh.bias_raw[at:at + N_EXP, 2 * FF:2 * FF + D], io["b_dn"][0]).then_inc(sh.expert_bias_in, 16)
            for k in range(2):
                sp.wait_ge(u2_stored[k], 16 * NT // 2)

        @block.tensor
        def _(pe):
            ident = sh.const("ident")
            for j in range(KC):
                if j >= 2:
                    pe.wait_ge(catT_ready, j - 1)
                for i in range(NT):
                    last = pe.transpose(bank[j % 2][:, i * P:(i + 1) * P], sh.cat[:, i, j * P:(j + 1) * P], ident)
                last.then_inc(cat_turned, 1)
            pe.wait_ge(rw_in, 64)
            pe.wait_ge(catT_ready, KC)

            def turn(i):
                pe.wait_ge(u2_ready, i + 1)
                if i:
                    pe.wait_ge(u2T_ready, 2 * i)
                for j in range(KC):
                    last = pe.transpose(bank[6 + j // 4][:, (j % 4) * P:(j % 4 + 1) * P], u2[:, i % 2, j * P:(j + 1) * P], ident)
                last.then_inc(u2_turned, 1)

            def logits(i):
                pe.wait_ge(u2T_ready, 2 * (i + 1))
                for j in range(KC):
                    last = pe.matmul(bank[0][:, i * N_EXP:(i + 1) * N_EXP], u2T[:, j, i * P:(i + 1) * P], wr[:, j, :], start=(j == 0), stop=(j == KC - 1))
                return last

            for i in range(NT):
                if i >= 2:
                    pe.wait_ge(gated, 2 * (i - 1))
                for q in range(2):
                    for j in range(KC):
                        last = pe.matmul(bank[2 + 2 * (i % 2) + q][:, :], catT[:, j, i * P:(i + 1) * P], sh.w_out[:, j, q * 512:(q + 1) * 512],
                                         start=(j == 0), stop=(j == KC - 1))
                    last.then_inc(mix_done, 1)
                if i >= 2:
                    logits(i - 2)
                if i:
                    turn(i - 1)
            logits(NT - 2)
            turn(NT - 1)
            logits(NT - 1).then_inc(logits_done, 1)
            pe.wait_ge(chosen_ready, 1)
            for i in range(NT):
                for k in range(i):
                    pe.matmul(bank[1][:, i * N_EXP:(i + 1) * N_EXP], sh.const("ones"), chosen[:, k, :], start=(k == 0), stop=False)
                pe.matmul(bank[1][:, i * N_EXP:(i + 1) * N_EXP], sh.const("before"), chosen[:, i, :], start=(i == 0), stop=True)
            for k in range(NT):
                last = pe.matmul(bank[1][:, NT * N_EXP:(NT + 1) * N_EXP], sh.const("ones"), chosen[:, k, :], start=(k == 0), stop=(k == NT - 1))
            last.then_inc(rank_done, 1)
            for n in range(NR):
                pe.wait_ge(hot_ready, n + 1)
                pe.matmul(bank[2][:, 0:BLOCKS], Qh[:, n % 4, :], Rh[:, n % 4, :], start=(n == 0), stop=(n == NR - 1)).then_inc(ids_done, 1)

        @block.gpsimd
        def _(pool):
            pool.wait_ge(ids_ready, 1)
            for k in range(2):
                pool.wait_ge(u2_stored[k], 16 * NT // 2)
            pool.indirect_dma_start(sh.modb[:, 0:D], None, sh.u2_dram, bass.IndirectOffsetOnAxis(ap=sh.ids[:, 0:1], axis=0)).then_inc(sh.x_in, 16)

        @block.scalar
        def _(act):
            for j in range(KC):
                act.wait_ge(cat_turned, j + 1)
                act.copy(catT[:, j, :], bank[j % 2][:, :]).then_inc(catT_ready, 1)
            for i in range(NT):
                act.wait_ge(var_ready, i + 1)
                act.activation(st[:, i, 14:15], st[:, i, 13:14], ACT.Sqrt, bias=sh.const("eps")[:, 1:2]).then_inc(root_ready, 1)
                act.wait_ge(u2_turned, i + 1)
                for q in range(2):
                    act.copy(u2T[:, 4 * q:4 * q + 4, i * P:(i + 1) * P], bank[6 + q][:, :].rearrange("p (a b) -> p a b", b=P)).then_inc(u2T_ready, 1)
            act.wait_ge(nmax_ready, 1)
            for i in range(NT):
                last = act.activation(sh.gate[:, i, :], m8[:, i, 0:TOP_E], ACT.Exp, bias=sm[:, i, 0:1], accum_out=sm[:, i, 1:2])
            last.then_inc(exp_ready, 1)

        @block.vector
        def _(v):
            count = {"ln": 0, "rt": 0}

            def ln1(ins):
                ins.then_inc(ln_step, 1)
                count["ln"] += 1
                v.wait_ge(ln_step, count["ln"])

            gate1, shift2, scale2, gate2 = (sh.modb[:, k * D:(k + 1) * D] for k in range(4))
            for m in (gate1, scale2, gate2):
                last = v.tensor_scalar(m, m, 1.0, None, ALU.add)
            ln1(last)
            v.wait_ge(rw_in, 64)
            for i in range(NT):
                x = sh.x_tm[:, i, :]
                for q in range(2):
                    v.wait_ge(mix_done, 2 * i + q + 1)
                    v.tensor_tensor(mixg[:, q * 512:(q + 1) * 512], bank[2 + 2 * (i % 2) + q][:, :], gate1[:, q * 512:(q + 1) * 512], ALU.mult).then_inc(gated, 1)
                v.wait_ge(gated, 2 * i + 2)
                ln1(v.scalar_tensor_tensor(x, x, ALPHA, mixg[:, :], ALU.mult, ALU.add))
                v.bn_stats(st[:, i, 0:6], x[:, 0:512])
                ln1(v.bn_stats(st[:, i, 6:12], x[:, 512:D]))
                v.bn_aggr(st[:, i, 12:14], st[:, i, 0:12].rearrange("p (a b) -> p a b", b=6)).then_inc(var_ready, 1)
                v.wait_ge(root_ready, i + 1)
                ln1(v.reciprocal(st[:, i, 15:16], st[:, i, 14:15]))
                ln1(v.tensor_scalar(x, x, st[:, i, 12:13], st[:, i, 15:16], ALU.subtract, ALU.mult))
                ln1(v.tensor_tensor(x, x, ln[:, 0, :], ALU.mult))
                ln1(v.tensor_tensor(x, x, ln[:, 1, :], ALU.add))
                if i >= 2:
                    v.wait_ge(u2_stored[i % 2], 16 * (i // 2))
                    v.wait_ge(u2_turned, i - 1)
                ln1(v.tensor_tensor(u2[:, i % 2, :], x, scale2, ALU.mult))
                v.tensor_tensor(u2[:, i % 2, :], u2[:, i % 2, :], shift2, ALU.add).then_inc(u2_ready, 1)

            def rt(ins):
                ins.then_inc(rt_step, 1)
                count["rt"] += 1
                v.wait_ge(rt_step, count["rt"])

            def along(ap, n, at):
                if at == 1:
                    return ap.rearrange("p (a m) -> p a m", a=1).broadcast_to([P, n, ap.shape[1]])
                return ap.rearrange("p (m a) -> p m a", a=1).broadcast_to([P, ap.shape[1], n])

            v.wait_ge(logits_done, 1)
            rt(v.tensor_tensor(lg[:, :, :], bank[0][:, 0:NT * N_EXP].rearrange("p (a b) -> p a b", b=N_EXP), along(br[:, :], NT, 1), ALU.add))
            for i in range(NT):
                rt(v.max(m8[:, i, :], lg[:, i, :]))
                rt(v.max_index(i8[:, i, :], m8[:, i, :], lg[:, i, :]))
            v.tensor_scalar(sm[:, :, 0:1], m8[:, :, 0:1], -1.0, None, ALU.mult).then_inc(nmax_ready, 1)
            rt(v.tensor_copy(idx[:, :, :], i8[:, :, :]))
            for k in range(TOP_E):
                last = v.tensor_tensor(hot[:, k, :, :], along(sh.const("expert"), NT, 1), along(idx[:, :, k], N_EXP, 2), ALU.is_equal)
            rt(last)
            rt(v.tensor_tensor(tmp[:, 0, :, :], hot[:, 0, :, :], hot[:, 1, :, :], ALU.add))
            rt(v.tensor_tensor(tmp[:, 1, :, :], hot[:, 2, :, :], hot[:, 3, :, :], ALU.add))
            v.tensor_tensor(chosen[:, :, :], tmp[:, 0, :, :], tmp[:, 1, :, :], ALU.add).then_inc(chosen_ready, 1)
            v.wait_ge(exp_ready, 1)
            rt(v.reciprocal(sm[:, :, 2:3], sm[:, :, 1:2]))
            rt(v.tensor_tensor(sh.gate[:, :, :], sh.gate[:, :, :], sm[:, :, 2:3].broadcast_to([P, NT, TOP_E]), ALU.mult))
            v.wait_ge(rank_done, 1)
            total, extra, upto, first, shift = (row[:, k, :] for k in range(5))
            rt(v.tensor_copy(total, bank[1][:, NT * N_EXP:(NT + 1) * N_EXP]))
            rt(v.tensor_scalar(extra, total, float(P) + 0.5, None, ALU.is_gt))
            for m in range(2, NT):
                rt(v.scalar_tensor_tensor(extra, total, float(m * P) + 0.5, extra, ALU.is_gt, ALU.add))
            rt(v.tensor_tensor_scan(upto, sh.const("ones")[:, 0:N_EXP], extra, 0.0, ALU.mult, ALU.add))
            rt(v.tensor_tensor(first, upto, extra, ALU.subtract))
            rt(v.scalar_tensor_tensor(shift, first, float(N_EXP), sh.const("expert"), ALU.add, ALU.subtract))
            pos, past, deep, slot, blk = (tmp[:, k, :, :] for k in range(5))
            rt(v.tensor_copy(pos, bank[1][:, 0:NT * N_EXP].rearrange("p (a b) -> p a b", b=N_EXP)))
            rt(v.tensor_scalar(past, pos, float(P) - 0.5, None, ALU.is_gt))
            rt(v.tensor_scalar(deep, pos, float(2 * P) - 0.5, None, ALU.is_gt))
            for m in range(3, NT):
                rt(v.scalar_tensor_tensor(deep, pos, float(m * P) - 0.5, deep, ALU.is_gt, ALU.add))
            rt(v.tensor_tensor(blk, past, along(shift, NT, 1), ALU.mult))
            rt(v.tensor_tensor(blk, blk, along(sh.const("expert"), NT, 1), ALU.add))
            rt(v.tensor_tensor(blk, blk, deep, ALU.add))
            rt(v.tensor_tensor(past, past, deep, ALU.add))
            rt(v.scalar_tensor_tensor(slot, past, -float(P), pos, ALU.mult, ALU.add))
            for k in range(TOP_E):
                rt(v.tensor_tensor(tmp[:, 5, :, :], hot[:, k, :, :], slot, ALU.mult))
                v.tensor_reduce(slotk[:, :, k], tmp[:, 5, :, :], AX.X, ALU.add)
                rt(v.tensor_tensor(tmp[:, 6, :, :], hot[:, k, :, :], blk, ALU.mult))
                rt(v.tensor_reduce(blkk[:, :, k], tmp[:, 6, :, :], AX.X, ALU.add))
            rt(v.scalar_tensor_tensor(rowf[:, :, :], blkk[:, :, :], float(P), slotk[:, :, :], ALU.mult, ALU.add))
            rt(v.tensor_copy(sh.rows[:, :, :], rowf[:, :, :]))
            for n in range(NR):
                i, k = divmod(n, TOP_E)
                if n >= 4:
                    v.wait_ge(ids_done, n - 3)
                v.tensor_scalar(Qh[:, n % 4, :], sh.const("slots"), slotk[:, i, k:k + 1], None, ALU.is_equal)
                v.tensor_scalar(Rh[:, n % 4, :], sh.const("blocks"), blkk[:, i, k:k + 1], sh.const("token")[:, i:i + 1], ALU.is_equal, ALU.mult).then_inc(hot_ready, 1)
            v.wait_ge(ids_done, NR)
            v.tensor_copy(sh.ids[:, :], bank[2][:, 0:BLOCKS]).then_inc(ids_ready, 1)
            j_of = along(sh.const("blocks")[:, 0:EXTRA], N_EXP, 2)
            rt(v.tensor_tensor(ohx[:, 0, :, :], j_of, along(first, EXTRA, 1), ALU.is_ge))
            rt(v.tensor_tensor(ohx[:, 1, :, :], j_of, along(upto, EXTRA, 1), ALU.is_lt))
            rt(v.tensor_tensor(ohx[:, 0, :, :], ohx[:, 0, :, :], ohx[:, 1, :, :], ALU.mult))
            rt(v.tensor_tensor(ohx[:, 0, :, :], ohx[:, 0, :, :], along(sh.const("expert"), EXTRA, 1), ALU.mult))
            rt(v.tensor_reduce(xf[:, 1:EXTRA + 1], ohx[:, 0, :, :], AX.X, ALU.add))
            rt(v.tensor_copy(xf[:, 0:1], sh.const("expert")[:, N_EXP - 1:N_EXP]))
            rt(v.tensor_copy(xf[:, EXTRA + 1:EXTRA + 2], upto[:, N_EXP - 1:N_EXP]))
            rt(v.tensor_copy(sh.extra[:, :], xf[0:1, :]))


def experts(nc, io, sh):
    NG, ND = KC, KC // 2
    GH, DH, STAGE = 2 * NG, 2 * ND, 4
    STEP = GH + DH
    HB = 1024
    with ExitStack() as ctx:
        e = ctx.enter_context
        wg = [sh.w_gu_raw[:, n, :, :].rearrange("p a n -> p (a n)") for n in range(EARLY)]
        wg += [sh.cst[:, 0:2 * HB], sh.cat[:, 2:4, :].rearrange("p a n -> p (a n)")]
        wd = sh.w_out[:, :, :].rearrange("p (r a) n -> p r a n", a=2)
        wh = e(nc.sbuf_tensor("w_high", [P, STAGE, HB], F32R))
        wl = e(nc.sbuf_tensor("w_low", [P, STAGE, HB], F32R))
        bias = e(nc.sbuf_tensor("bias_rows", [2 * N_EXP, 2 * FF + D], F32R))
        pick_g = e(nc.sbuf_tensor("pick_gu", [2 * N_EXP, P], F32R))
        pick_d = e(nc.sbuf_tensor("pick_dn", [2 * N_EXP, P], F32R))
        xh = e(nc.sbuf_tensor("xT_high", [P, KC, P], F32R))
        xl = e(nc.sbuf_tensor("xT_low", [P, KC, P], F32R))
        hh = e(nc.sbuf_tensor("hT_high", [P, KC, P], F32R))
        hl = e(nc.sbuf_tensor("hT_low", [P, KC, P], F32R))
        gt, sg = sh.cat[:, 0, :], sh.cat[:, 1, :]
        idb = e(nc.sbuf_tensor("id_block", [P, 1], I32))
        fence = e(nc.sbuf_tensor("fence", [1, 4], F32))
        xg, y, up = (sh.modb[:, k * D:(k + 1) * D] for k in range(3))
        ps_gu = e(nc.psum_tensor("ps_gu", [P, 4, 512], F32))
        ps_y = e(nc.psum_tensor("ps_y", [P, 2, 512], F32))
        ps_t = e(nc.psum_tensor("ps_t", [P, KC, P], F32))

        sem = sh.sem
        g_in = sh.w_gu_in
        d_in = [sem(f"w_dn_in{n}") for n in range(ND)]
        bias_high, bias_ready = sem("expert_bias_high"), sem("expert_bias_ready")
        pg_ready, pd_ready, pg_used, pd_used = sem("pick_gu_ready"), sem("pick_dn_ready"), sem("pick_gu_used"), sem("pick_dn_used")
        high_ready, low_ready, half_used = sem("high_ready"), sem("low_ready"), sem("half_used")
        id_ready, x_in, x_turned, xh_ready, xl_ready = sem("id_ready"), sh.x_in, sem("xg_turned"), sem("xh_ready"), sem("xl_ready")
        gt_ready, up_ready, up1_ready, sg_ready, gs_ready, h_ready = sem("gt_ready"), sem("up_ready"), sem("up1_ready"), sem("sg_ready"), sem("gs_ready"), sem("h_ready")
        h_turned, hh_ready, hl_ready, y_ready, y_stored = sem("h_turned"), sem("hh_ready"), sem("hl_ready"), sem("y_ready"), sem("y_stored")
        fence_ready, fenced = sem("fence_ready"), sem("fenced")
        bias_raw = sh.bias_raw
        w_gu = io["w_gu"][0].rearrange("e (c p) n -> e p c n", p=P)
        w_dn = io["w_dn"][0].rearrange("e (c a p) n -> e p c a n", p=P, a=2)

        def gate_at(b):
            return b * STEP

        def down_at(b, final=False):
            return (b + 1) * STEP + (0 if final else GH)

        def extra_count(eng):
            return eng.value_load(sh.extra[0:1, EXTRA + 1:EXTRA + 2], min_val=0, max_val=EXTRA)

        def expert_of(eng, j):
            return eng.value_load(sh.extra[0:1, bass.ds(j, 1)], min_val=0, max_val=N_EXP - 1)

        def raw_half(g, k):
            return wg[k // 2][:, k % 2 * HB:(k % 2 + 1) * HB] if g else wd[:, k // 2, k % 2, :]

        def stage(g, k):
            return (k if g else GH + k) % STAGE

        LAST = N_EXP - 1
        block = e(nc.Block())

        @block.sync
        def _(sp):
            def load_gate(b, x):
                first = isinstance(b, int) and b == 0
                for n in range(EARLY if first else 0, NG):
                    if not first:
                        sp.wait_ge(low_ready, gate_at(b - 1) + 2 * n + 2)
                    sp.dma_start(wg[n], w_gu[bass.ds(x, 1), :, n, :].rearrange("e p n -> (e p) n")).then_inc(g_in[n], 16)

            def load_down(b, x):
                first = isinstance(b, int) and b == 0
                if first:
                    sp.wait_ge(bias_ready, 1)
                for n in range(ND):
                    if not first:
                        sp.wait_ge(low_ready, down_at(b - 1) + 2 * n + 2)
                    sp.dma_start(wd[:, n, :, :], w_dn[bass.ds(x, 1), :, n, :, :].rearrange("e p a n -> (e p) a n")).then_inc(d_in[n], 16)

            load_gate(0, 0)
            load_down(0, 0)
            load_gate(1, 1)
            with sp.Fori(2, N_EXP) as b:
                load_gate(b, b)
                load_down(b - 1, b - 1)
            n = extra_count(sp)
            with sp.Fori(0, EXTRA) as j:
                with sp.If(j < n):
                    load_gate(j + N_EXP, expert_of(sp, j + 1))
                    load_down(j + LAST, expert_of(sp, j))
            load_down(n + LAST, expert_of(sp, n))

        @block.gpsimd
        def _(pool):
            def gather(b):
                pool.wait_ge(id_ready, b + 1)
                if not isinstance(b, int) or b > 0:
                    pool.wait_ge(x_turned, b)
                pool.tensor_tensor(fence[0:1, 0:1], fence[0:1, 1:2], fence[0:1, 2:3], ALU.add).then_inc(fenced, 1)
                if isinstance(b, int) and b == 0:
                    return
                pool.indirect_dma_start(xg, None, sh.u2_dram, bass.IndirectOffsetOnAxis(ap=idb[:, 0:1], axis=0)).then_inc(x_in, 16)

            def hidden(b):
                up8 = up.rearrange("p (c t) -> p c t", t=P)
                pool.wait_ge(up_ready, b + 1)
                pool.tensor_tensor(up8, up8, sh.const("ones").rearrange("p (a t) -> p a t", a=1).broadcast_to([P, KC, P]), ALU.add).then_inc(up1_ready, 1)
                pool.wait_ge(sg_ready, b + 1)
                pool.tensor_tensor(sg, gt, sg, ALU.mult).then_inc(gs_ready, 1)
                pool.wait_ge(gs_ready, b + 1)
                pool.wait_ge(up1_ready, b + 1)
                pool.tensor_tensor(up, up, sg, ALU.mult).then_inc(h_ready, 1)

            pool.memset(fence[:, :], 0.0).then_inc(fence_ready, 1)
            pool.wait_ge(fence_ready, 1)
            gather(0)
            gather(1)
            hidden(0)
            with pool.Fori(1, N_EXP) as b:
                gather(b + 1)
                hidden(b)
            n = extra_count(pool)
            with pool.Fori(0, EXTRA) as j:
                with pool.If(j < n):
                    gather(j + N_EXP + 1)
                    hidden(j + N_EXP)

        @block.tensor
        def _(pe):
            ident = sh.const("ident")

            def turn_x(b):
                pe.wait_ge(x_in, b * 16 + 16)
                if not isinstance(b, int) or b > 1:
                    pe.wait_ge(hl_ready, b - 1)
                for j in range(KC):
                    last = pe.transpose(ps_t[:, j, :], xg[:, j * P:(j + 1) * P], ident)
                last.then_inc(x_turned, 1)

            def turn_h(b):
                pe.wait_ge(h_ready, b + 1)
                pe.wait_ge(xl_ready, b + 2)
                for j in range(KC):
                    last = pe.transpose(ps_t[:, j, :], up[:, j * P:(j + 1) * P], ident)
                last.then_inc(h_turned, 1)

            def three(out, ah, al, n, stage, stop):
                for a, w in ((ah, wh), (ah, wl), (al, wh)):
                    for q in range(2):
                        last = pe.matmul(out[:, q, :], a[:, n, :], w[:, stage, q * 512:(q + 1) * 512], start=False, stop=(stop and a is al))
                return last

            def gate(b, gap=0):
                if not isinstance(b, int) or b > 0:
                    pe.wait_ge(up_ready, b)
                pe.wait_ge(pg_ready, b + 1)
                for q in range(4):
                    last = pe.matmul(ps_gu[:, q, :], pick_g[:, :], bias[:, q * 512:(q + 1) * 512], start=True, stop=False)
                last.then_inc(pg_used, 1)
                pe.wait_ge(xl_ready, b + 1)
                for k in range(GH):
                    pe.wait_ge(low_ready, gate_at(b) + k + 1)
                    last = three(ps_gu[:, 2 * (k % 2):2 * (k % 2) + 2, :], xh, xl, k // 2, stage(True, k), k // 2 == NG - 1)
                    last.then_inc(half_used, 1 + (gap if k == GH - 1 else 0))
                turn_x(b + 1)

            def down(b, final=False):
                pe.wait_ge(y_ready, b + 1)
                pe.wait_ge(pd_ready, b + 1)
                for q in range(2):
                    last = pe.matmul(ps_y[:, q, :], pick_d[:, :], bias[:, 2 * FF + q * 512:2 * FF + (q + 1) * 512], start=True, stop=False)
                last.then_inc(pd_used, 1)
                pe.wait_ge(hl_ready, b + 1)
                for k in range(DH):
                    pe.wait_ge(low_ready, down_at(b, final) + k + 1)
                    last = three(ps_y, hh, hl, k, stage(False, k), k == DH - 1)
                    last.then_inc(half_used, 1)

            turn_x(0)
            gate(0, gap=DH)

            def main(b):
                turn_h(b - 1)
                gate(b)
                down(b - 1)

            with pe.Fori(1, N_EXP) as b:
                main(b)
            n = extra_count(pe)
            with pe.Fori(0, EXTRA) as j:
                with pe.If(j < n):
                    main(j + N_EXP)
            turn_h(n + LAST)
            down(n + LAST, final=True)

        @block.scalar
        def _(act):
            def high(g, b, ks, final=False, gap=0):
                at = gate_at(b) if g else down_at(b, final)
                for k in ks:
                    if k % 2 == 0:
                        act.wait_ge((g_in if g else d_in)[k // 2], b * 16 + 16)
                    if not (isinstance(b, int) and b == 0 and g and k < STAGE):
                        act.wait_ge(half_used, at + (0 if final and k < STAGE else k - STAGE + 1))
                    act.copy(wh[:, stage(g, k), :], raw_half(g, k)).then_inc(high_ready, 1 + (gap if k == ks[-1] else 0))

            def x_high(b):
                act.wait_ge(x_turned, b + 1)
                act.copy(xh[:, :, :], ps_t[:, :, :]).then_inc(xh_ready, 1)

            def h_high(b):
                act.wait_ge(h_turned, b + 1)
                act.copy(hh[:, :, :], ps_t[:, :, :]).then_inc(hh_ready, 1)

            def sigmoid(b):
                act.wait_ge(gt_ready, b + 1)
                act.activation(sg, gt, ACT.Sigmoid, scale=SWIGLU_ALPHA).then_inc(sg_ready, 1)

            def store(b, used):
                act.wait_ge(half_used, used)
                act.wait_ge(y_stored, b * 16 + 16)
                act.copy(y.rearrange("p (q n) -> p q n", q=2), ps_y[:, :, :]).then_inc(y_ready, 1)
                act.wait_ge(y_ready, b + 2)
                act.dma_start(sh.y_dram[bass.ds(b * P, P), :], y).then_inc(y_stored, 16)

            act.wait_ge(fence_ready, 1)
            act.copy(fence[0:1, 3:4], fence[0:1, 2:3]).then_inc(y_ready, 1)
            act.wait_ge(y_ready, 1)
            act.copy(fence[0:1, 3:4], fence[0:1, 2:3]).then_inc(y_stored, 16)
            x_high(0)
            high(True, 0, range(GH), gap=DH)
            x_high(1)
            sigmoid(0)
            high(True, 1, range(STAGE))

            def main(b, next_exists=None):
                h_high(b - 1)
                high(True, b, range(STAGE, GH))
                high(False, b - 1, range(STAGE))
                x_high(b + 1)
                sigmoid(b)
                high(False, b - 1, range(STAGE, DH))
                with act.If(next_exists) if next_exists is not None else nullcontext():
                    high(True, b + 1, range(STAGE))
                store(b - 1, (b + 1) * STEP)

            with act.Fori(1, LAST) as b:
                main(b)
            n = extra_count(act)
            main(LAST, n > 0)
            with act.Fori(0, EXTRA) as j:
                with act.If(j < n):
                    main(j + N_EXP, j + 1 < n)
            b = n + LAST
            h_high(b)
            high(False, b, range(DH), final=True)
            store(b, down_at(b, True) + DH)
            act.wait_ge(y_stored, (n + N_EXP + 1) * 16)
            act.copy(fence[0:1, 3:4], fence[0:1, 2:3])

        @block.vector
        def _(v):
            def ids(b):
                if not isinstance(b, int) or b > 0:
                    v.wait_ge(x_in, b * 16)
                    v.wait_ge(fenced, b)
                v.tensor_copy(idb[:, :], sh.ids[:, bass.ds(b, 1)]).then_inc(id_ready, 1)

            def low(g, b, ks, final=False, gap=0):
                at = gate_at(b) if g else down_at(b, final)
                for k in ks:
                    v.wait_ge(high_ready, at + k + 1)
                    v.tensor_tensor(wl[:, stage(g, k), :], raw_half(g, k), wh[:, stage(g, k), :].bitcast(F32), ALU.subtract).then_inc(
                        low_ready, 1 + (gap if k == ks[-1] else 0))

            def x_low(b):
                v.wait_ge(xh_ready, b + 1)
                v.tensor_tensor(xl[:, :, :], ps_t[:, :, :], xh[:, :, :].bitcast(F32), ALU.subtract).then_inc(xl_ready, 1)

            def h_low(b):
                v.wait_ge(hh_ready, b + 1)
                v.tensor_tensor(hl[:, :, :], ps_t[:, :, :], hh[:, :, :].bitcast(F32), ALU.subtract).then_inc(hl_ready, 1)

            def clamp(b, used):
                v.wait_ge(half_used, used)
                if not isinstance(b, int) or b > 0:
                    v.wait_ge(h_turned, b)
                halves = ps_gu[:, :, :].rearrange("p q (n two) -> p q n two", two=2)
                v.tensor_scalar(gt.rearrange("p (q n) -> p q n", q=4), halves[:, :, :, 0], LIMIT, None, ALU.min).then_inc(gt_ready, 1)
                v.tensor_scalar(up.rearrange("p (q n) -> p q n", q=4), halves[:, :, :, 1], LIMIT, -LIMIT, ALU.min, ALU.max).then_inc(up_ready, 1)

            def pick(g, b, x):
                if not isinstance(b, int) or b > 0:
                    v.wait_ge(pg_used if g else pd_used, b)
                p, ready = (pick_g, pg_ready) if g else (pick_d, pd_ready)
                v.tensor_scalar(p[:, :], sh.const("ones")[0:2 * N_EXP, :], sh.const("picks")[0:2 * N_EXP, bass.ds(x, 1)],
                                None, ALU.mult).then_inc(ready, 1)

            ids(0)
            v.wait_ge(sh.expert_bias_in, 64)
            v.tensor_copy(bias[:, :], bias_raw).then_inc(bias_high, 1)
            v.wait_ge(bias_high, 1)
            v.tensor_tensor(bias[N_EXP:2 * N_EXP, :], bias_raw[N_EXP:2 * N_EXP, :], bias[N_EXP:2 * N_EXP, :].bitcast(F32), ALU.subtract).then_inc(bias_ready, 1)
            v.wait_ge(bias_ready, 1)
            pick(True, 0, 0)
            pick(False, 0, 0)
            x_low(0)
            ids(1)
            low(True, 0, range(GH), gap=DH)
            clamp(0, STEP)
            x_low(1)
            low(True, 1, range(STAGE))

            def main(b, x, next_exists=None):
                ids(b + 1)
                pick(True, b, x)
                h_low(b - 1)
                low(True, b, range(STAGE, GH))
                low(False, b - 1, range(STAGE))
                clamp(b, gate_at(b) + GH)
                x_low(b + 1)
                pick(False, b, x)
                low(False, b - 1, range(STAGE, DH))
                with v.If(next_exists) if next_exists is not None else nullcontext():
                    low(True, b + 1, range(STAGE))

            with v.Fori(1, LAST) as b:
                main(b, b)
            n = extra_count(v)
            main(LAST, LAST, n > 0)
            with v.Fori(0, EXTRA) as j:
                with v.If(j < n):
                    main(j + N_EXP, expert_of(v, j + 1), j + 1 < n)
            h_low(n + LAST)
            low(False, n + LAST, range(DH), final=True)


def finish(nc, io, sh):
    NY = 8
    with ExitStack() as ctx:
        e = ctx.enter_context
        ln = e(nc.sbuf_tensor("ln2_rows", [P, 2, D], F32))
        yk = e(nc.sbuf_tensor("y_gathered", [P, NY, D], F32))
        acc = e(nc.sbuf_tensor("ffn", [P, NT, D], F32))
        st = e(nc.sbuf_tensor("ln2_stats", [P, NT, 16], F32))
        sem = sh.sem
        nb = e(nc.sbuf_tensor("ln2_shift", [P, NT], F32))
        shift_ready, last_ready, normed, weighted = sem("ln2_shift_ready"), sem("last_out_ready"), sem("ln2_normed"), sem("ln2_weighted")
        l_in, y_in, y_used, step, var_ready, root_ready, o_ready, o_stored = (sem("ln2_in"), [sem(f"yk_in{n}") for n in range(NY)], sem("yk_used"), sem("ln2_step"),
                                                                             sem("ln2_var"), sem("ln2_root"), sem("out_ready"), sem("out_stored"))
        block = e(nc.Block())

        @block.sync
        def _(sp):
            sp.dma_start(ln[:, 0, :], io["ln2_g"].broadcast_to([P, D])).then_inc(l_in, 16)
            sp.dma_start(ln[:, 1, :], io["ln2_b"].broadcast_to([P, D])).then_inc(l_in, 16)
            for i in range(NT):
                if i < NT - 1:
                    sp.wait_ge(o_ready, i + 1)
                else:
                    sp.wait_ge(last_ready, 1)
                sp.dma_start(io["out"][0, i * P:(i + 1) * P, :], acc[:, i, :]).then_inc(o_stored, 16)
            sp.wait_ge(o_stored, 16 * NT)

        @block.gpsimd
        def _(pool):
            for n in range(NT * TOP_E):
                i, k = divmod(n, TOP_E)
                if n >= NY:
                    pool.wait_ge(y_used, n - NY + 1)
                pool.indirect_dma_start(yk[:, n % NY, :], None, sh.y_dram, bass.IndirectOffsetOnAxis(ap=sh.rows[:, i, k:k + 1], axis=0)).then_inc(y_in[n % NY], 16)
            pool.wait_ge(l_in, 32)
            for i in range(NT - 1):
                pool.wait_ge(normed, i + 1)
                pool.tensor_tensor(acc[:, i, :], acc[:, i, :], ln[:, 0, :], ALU.mult).then_inc(weighted, 1)
                pool.wait_ge(weighted, i + 1)
                pool.tensor_tensor(acc[:, i, :], acc[:, i, :], ln[:, 1, :], ALU.add).then_inc(o_ready, 1)

        @block.scalar
        def _(act):
            for i in range(NT):
                act.wait_ge(var_ready, i + 1)
                act.activation(st[:, i, 14:15], st[:, i, 13:14], ACT.Sqrt, bias=sh.const("eps")[:, 1:2]).then_inc(root_ready, 1)
                act.wait_ge(shift_ready, i + 1)
                act.activation(acc[:, i, :], acc[:, i, :], ACT.Identity, bias=nb[:, i:i + 1], scale=st[:, i, 15:16]).then_inc(normed, 1)

        @block.vector
        def _(v):
            count = [0]

            def link(ins):
                ins.then_inc(step, 1)
                count[0] += 1
                v.wait_ge(step, count[0])

            v.wait_ge(l_in, 32)
            for i in range(NT):
                a = acc[:, i, :]
                for k in range(TOP_E):
                    n = i * TOP_E + k
                    v.wait_ge(y_in[n % NY], 16 * (n // NY + 1))
                    g = sh.gate[:, i, k:k + 1]
                    if k == 0:
                        v.tensor_scalar(a, yk[:, n % NY, :], g, None, ALU.mult).then_inc(y_used, 1)
                    else:
                        v.scalar_tensor_tensor(a, yk[:, n % NY, :], g, a, ALU.mult, ALU.add).then_inc(y_used, 1)
                    v.wait_ge(y_used, n + 1)
                link(v.tensor_tensor(a, a, sh.modb[:, 3 * D:4 * D], ALU.mult))
                link(v.scalar_tensor_tensor(a, sh.x_tm[:, i, :], ALPHA, a, ALU.mult, ALU.add))
                v.bn_stats(st[:, i, 0:6], a[:, 0:512])
                link(v.bn_stats(st[:, i, 6:12], a[:, 512:D]))
                v.bn_aggr(st[:, i, 12:14], st[:, i, 0:12].rearrange("p (a b) -> p a b", b=6)).then_inc(var_ready, 1)
                v.wait_ge(root_ready, i + 1)
                link(v.reciprocal(st[:, i, 15:16], st[:, i, 14:15]))
                v.tensor_scalar(nb[:, i:i + 1], st[:, i, 12:13], st[:, i, 15:16], -1.0, ALU.mult, ALU.mult).then_inc(shift_ready, 1)
            v.wait_ge(normed, NT)
            link(v.tensor_tensor(a, a, ln[:, 0, :], ALU.mult))
            v.tensor_tensor(a, a, ln[:, 1, :], ALU.add).then_inc(last_ready, 1)


INPUTS = ["x", "c", "w_ada", "b_ada", "w_in", "shift_mu", "rwkv_w0", "rwkv_w2", "rwkv_a0", "rwkv_a2", "rwkv_g2",
          "rwkv_k_k", "rwkv_k_a", "rwkv_r_k", "rwkv_ln_w", "rwkv_ln_b", "mla_q_norm", "mla_w_q_up",
          "mla_kv_norm", "mla_w_uk", "mla_w_uv", "idx_w_q", "idx_ln_g", "idx_ln_b", "w_out", "ln1_g", "ln1_b",
          "w_router", "b_router", "w_gu", "b_gu", "w_dn", "b_dn", "ln2_g", "ln2_b"]


def build(nc, io, stages=5):
    with ExitStack() as ctx:
        e = ctx.enter_context
        sh = Shared()
        live = []

        def new_semaphore(name):
            live.append(nc.alloc_semaphore(name=name))
            return live[-1]

        def clear_semaphores():
            nc.clear_and_free_semaphores(live)
            live.clear()
            nc.all_engine_barrier()

        sh.sem = new_semaphore
        sh.cst = e(nc.sbuf_tensor("consts_sb", [P, N_CONST], F32))
        sh.cols = e(nc.sbuf_tensor("cols", [P, N_VEC], F32))
        sh.x_tm = e(nc.sbuf_tensor("x_tm", [P, NT, D], F32))
        sh.modb = e(nc.sbuf_tensor("modb", [P, 4 * D], F32))
        sh.const = lambda n: sh.cst[:, CONST[n][0]:CONST[n][0] + CONST[n][1]]
        sh.col = lambda n, i: sh.cols[:, VEC[n][0] + i:VEC[n][0] + i + 1]
        sh.gate = e(nc.sbuf_tensor("gate", [P, NT, TOP_E], F32))
        sh.rows = e(nc.sbuf_tensor("rows", [P, NT, TOP_E], I32))
        sh.ids = e(nc.sbuf_tensor("ids", [P, BLOCKS], I32))
        sh.extra = e(nc.sbuf_tensor("extra", [1, EXTRA + 2], I32))
        sh.u2_dram = nc.dram_tensor("u2_dram", (S, D), F32, kind="Internal").ap()
        sh.y_dram = nc.dram_tensor("y_dram", ((BLOCKS - 1) * P, D), F32, kind="Internal").ap()
        middle = ctx.enter_context(ExitStack())
        sh.cat = middle.enter_context(nc.sbuf_tensor("cat_tm", [P, NT, D], F32))
        sh.w_out = middle.enter_context(nc.sbuf_tensor("w_out_sb", [P, KC, D], F32))
        with ExitStack() as front:
            sh.pT = front.enter_context(nc.sbuf_tensor("pT", [P, COL_TILES, S], F32))
            project(nc, io, sh)
            if stages >= 2:
                attend(nc, io, sh)
            if stages >= 3:
                sh.b_hat = front.enter_context(nc.sbuf_tensor("b_hat", [P, NPAIR, S], F32))
                sh.v_tm = front.enter_context(nc.sbuf_tensor("v_tm", [P, NT, D_GROUP], F32))
                sh.gate_sig = front.enter_context(nc.sbuf_tensor("gate_sig", [P, S], F32))
                sh.w_end = front.enter_context(nc.sbuf_tensor("w_end", [P, NPAIR, NCH], F32))
                sh.bonus = front.enter_context(nc.sbuf_tensor("bonus", [P, NT, HEADS], F32))
                prepare(nc, io, sh)
                scan(nc, io, sh)
                clear_semaphores()
        if stages >= 4:
            sh.w_gu_raw = middle.enter_context(nc.sbuf_tensor("w_gu_raw", [P, EARLY, 2, FF], F32))
            route(nc, io, sh)
        if stages >= 5:
            experts(nc, io, sh)
        middle.close()
        if stages >= 5:
            finish(nc, io, sh)


def kernel(**inputs):
    import concourse.bacc as bacc
    from concourse.bass_utils import run_bass_kernel_spmd

    nc = bacc.Bacc("TRN2", target_bir_lowering=False, num_devices=1)
    arrays, io = {}, {}
    for name in INPUTS:
        a = np.ascontiguousarray(inputs[name])
        arrays[f"{name}_dram"] = a
        io[name] = nc.dram_tensor(f"{name}_dram", a.shape, mybir.dt.from_np(a.dtype), kind="ExternalInput").ap()
    arrays["consts_dram"] = CONST_ARRAY
    io["consts"] = nc.dram_tensor("consts_dram", CONST_ARRAY.shape, F32, kind="ExternalInput").ap()
    io["out"] = nc.dram_tensor("out_dram", (1, S, D), F32, kind="ExternalOutput").ap()
    build(nc, io)
    r = run_bass_kernel_spmd(nc, [arrays], core_ids=[0])
    return r.results[0]["out_dram"]
```
